# Optimizing a Trainium2 kernel written in Bass

```python
import jax, jax.numpy as jnp
from jax import lax
import numpy as np

D_MODEL = 1024
BATCH = 1
SEQ = 1024
DEPTH = 1

F32 = jnp.float32
N_META = 16
EPS = 1e-5
ROPE_THETA = 500000.0
ATT_HEADS = 8
ATT_KV_HEADS = 2
ATT_HEAD_DIM = 64
ATT_WIDTH = ATT_HEADS * ATT_HEAD_DIM
IDX_HEADS = 8
IDX_DIM = 32
IDX_SCALE = (IDX_DIM ** -0.5) * (IDX_HEADS ** -0.5)
TOPK_MAX = 256
Q_BLOCK = 128
HG_HEADS = 4
HG_DK = 128
HG_DV = 128
HG_KWIDTH = HG_HEADS * HG_DK
HG_WIDTH = HG_HEADS * HG_DV
HG_CHUNK = 64
N_EXPERTS = 32
TOP_K = 4
D_FF = 1024
SWIGLU_LIMIT = 7.0
SWIGLU_ALPHA = 1.702
MOE_BLOCK = 128
IN_SPLITS = (ATT_WIDTH, ATT_KV_HEADS * ATT_HEAD_DIM, ATT_KV_HEADS * ATT_HEAD_DIM,
             IDX_HEADS * IDX_DIM, IDX_DIM, IDX_HEADS,
             HG_KWIDTH, HG_KWIDTH, HG_WIDTH, HG_WIDTH, D_MODEL, D_MODEL)
IN_COLS = sum(IN_SPLITS)

kernel_name = "hybrid_dsa_hgrn2_moe_meta"

def rmsnorm(x, g):
    xf = x.astype(F32)
    y = xf * lax.rsqrt(jnp.mean(xf * xf, axis=-1, keepdims=True) + EPS)
    return (y * g.astype(F32)).astype(x.dtype)

def partial_rope(x, pos):
    d = x.shape[-1]
    rot = d // 4
    half = rot // 2
    inv = ROPE_THETA ** (-jnp.arange(half, dtype=F32) * 2.0 / rot)
    ang = pos.astype(F32)[:, None] * inv[None, :]
    c = jnp.cos(ang)[:, None, :]
    s = jnp.sin(ang)[:, None, :]
    xf = x.astype(F32)
    x1 = xf[..., :half]
    x2 = xf[..., half:rot]
    out = jnp.concatenate([x1 * c - x2 * s, x2 * c + x1 * s, xf[..., rot:]], axis=-1)
    return out.astype(x.dtype)

def dsa_attention(q, k, v, iq, ik, iw, n_valid):
    B, Lp = q.shape[0], q.shape[1]
    nqb = Lp // Q_BLOCK
    k_sel = min(TOPK_MAX, n_valid // 4)
    groups = ATT_HEADS // ATT_KV_HEADS
    scale = ATT_HEAD_DIM ** -0.5
    key_pos = jnp.arange(Lp)
    ikf = ik.astype(F32)
    bidx = jnp.arange(B)[:, None, None]

    def to_blocks(a):
        return jnp.moveaxis(a.reshape((B, nqb, Q_BLOCK) + a.shape[2:]), 1, 0)

    def block(args):
        qb, iqb, iwb, qpos = args
        rel = jax.nn.relu(jnp.einsum('bqhd,bkd->bqhk', iqb.astype(F32), ikf))
        score = jnp.einsum('bqhk,bqh->bqk', rel, iwb.astype(F32)) * IDX_SCALE
        causal = key_pos[None, :] <= qpos[:, None]
        score = jnp.where(causal[None], score, -jnp.inf)
        _, sel = lax.top_k(score, k_sel)
        valid = sel <= qpos[None, :, None]
        kg = k[bidx, sel].astype(F32)
        vg = v[bidx, sel].astype(F32)
        qg = qb.reshape(B, Q_BLOCK, ATT_KV_HEADS, groups, ATT_HEAD_DIM).astype(F32)
        logits = jnp.einsum('bqgrd,bqkgd->bqgrk', qg, kg) * scale
        logits = jnp.where(valid[:, :, None, None, :], logits, -jnp.inf)
        p = jax.nn.softmax(logits, axis=-1)
        o = jnp.einsum('bqgrk,bqkgd->bqgrd', p, vg)
        return o.reshape(B, Q_BLOCK, ATT_WIDTH).astype(q.dtype)

    out = lax.map(block, (to_blocks(q), to_blocks(iq), to_blocks(iw), key_pos.reshape(nqb, Q_BLOCK)))
    return jnp.moveaxis(out, 0, 1).reshape(B, Lp, ATT_WIDTH)

def hgrn2_chunk(state, inp):
    q, kk, v, logf = inp
    C = q.shape[2]
    b = jnp.cumsum(logf, axis=2)
    mask = jnp.tril(jnp.ones((C, C), dtype=bool))
    diff = b[:, :, :, None, :] - b[:, :, None, :, :]
    decay = jnp.exp(jnp.where(mask[None, None, :, :, None], diff, -jnp.inf))
    scores = jnp.einsum('bhtd,bhtsd,bhsd->bhts', q, decay, kk)
    o = jnp.einsum('bhts,bhse->bhte', scores, v) + jnp.einsum('bhtd,bhde->bhte', q * jnp.exp(b), state)
    b_last = b[:, :, -1:, :]
    new_state = (jnp.exp(b_last[:, :, 0, :])[..., None] * state
                 + jnp.einsum('bhsd,bhse->bhde', kk * jnp.exp(b_last - b), v))
    return new_state, o

def hgrn2(q, f_pre, i, lb):
    B, L = q.shape[0], q.shape[1]

    def heads(a, d):
        return a.reshape(B, L, HG_HEADS, d).transpose(0, 2, 1, 3).astype(F32)

    lbh = lb.reshape(HG_HEADS, 1, HG_DK).astype(F32)
    f = lbh + (1.0 - lbh) * jax.nn.sigmoid(heads(f_pre, HG_DK))
    logf = jnp.log(f)
    kk = 1.0 - f
    qh = heads(q, HG_DK) * (HG_DK ** -0.5)
    vh = heads(i, HG_DV)
    state0 = jnp.zeros((B, HG_HEADS, HG_DK, HG_DV), F32)
    state, o_meta = hgrn2_chunk(state0, (qh[:, :, :N_META], kk[:, :, :N_META],
                                         vh[:, :, :N_META], logf[:, :, :N_META]))
    n_chunks = (L - N_META) // HG_CHUNK

    def chunks(a):
        return jnp.moveaxis(a[:, :, N_META:].reshape(B, HG_HEADS, n_chunks, HG_CHUNK, a.shape[-1]), 2, 0)

    _, o_real = lax.scan(hgrn2_chunk, state, (chunks(qh), chunks(kk), chunks(vh), chunks(logf)))
    o_real = jnp.moveaxis(o_real, 0, 2).reshape(B, HG_HEADS, L - N_META, HG_DV)
    o = jnp.concatenate([o_meta, o_real], axis=2)
    return o.transpose(0, 2, 1, 3)

def moe(x, router_w, router_b, w_gate, b_gate, w_up, b_up, w_down, b_down):
    B, L, D = x.shape
    T = B * L
    xt = x.reshape(T, D)
    logits = (xt @ router_w + router_b).astype(F32)
    top_vals, top_idx = lax.top_k(logits, TOP_K)
    gates = jax.nn.softmax(top_vals, axis=-1)
    n_assign = T * TOP_K
    expert = top_idx.reshape(-1)
    token = jnp.repeat(jnp.arange(T, dtype=jnp.int32), TOP_K)
    weight = gates.reshape(-1)
    order = jnp.argsort(expert)
    e_sorted = expert[order]
    t_sorted = token[order]
    w_sorted = weight[order]
    counts = jnp.bincount(expert, length=N_EXPERTS)
    starts = jnp.cumsum(counts) - counts
    padded = (counts + MOE_BLOCK - 1) // MOE_BLOCK * MOE_BLOCK
    pad_ends = jnp.cumsum(padded)
    pad_starts = pad_ends - padded
    dest = pad_starts[e_sorted] + (jnp.arange(n_assign) - starts[e_sorted])
    n_blocks = -(-n_assign // MOE_BLOCK) + N_EXPERTS
    cap = n_blocks * MOE_BLOCK
    slot_token = jnp.full((cap,), T, jnp.int32).at[dest].set(t_sorted)
    slot_weight = jnp.zeros((cap,), F32).at[dest].set(w_sorted)
    block_expert = jnp.minimum(
        jnp.searchsorted(pad_ends, jnp.arange(n_blocks) * MOE_BLOCK, side='right'), N_EXPERTS - 1)
    x_pad = jnp.concatenate([xt, jnp.zeros((1, D), xt.dtype)], axis=0)

    def expert_block(args):
        tok, e = args
        xb = x_pad[tok]
        g = xb @ w_gate[e] + b_gate[e]
        u = xb @ w_up[e] + b_up[e]
        g = jnp.minimum(g, SWIGLU_LIMIT)
        u = jnp.clip(u, -SWIGLU_LIMIT, SWIGLU_LIMIT)
        act = (u + 1.0) * (g * jax.nn.sigmoid(SWIGLU_ALPHA * g))
        return act @ w_down[e] + b_down[e]

    out = lax.map(expert_block, (slot_token.reshape(n_blocks, MOE_BLOCK), block_expert))
    out = out.reshape(cap, D) * slot_weight[:, None].astype(out.dtype)
    y = jnp.zeros((T + 1, D), out.dtype).at[slot_token].add(out)[:T]
    return y.reshape(B, L, D).astype(x.dtype)

def hybrid_layer(h, attn_norm_g, w_in, hgrn_norm_g, w_up_attn, w_up_hgrn, w_out, lb,
                 ffn_norm_g, router_w, router_b, w_gate, b_gate, w_up, b_up, w_down, b_down):
    B, L, _ = h.shape
    Lp = -(-L // Q_BLOCK) * Q_BLOCK
    pos = jnp.arange(Lp)
    xn = rmsnorm(h, attn_norm_g)
    proj = xn @ w_in
    (q, k, v, iq, ik, iw, hq, hf, hi, hg, ga, gh) = jnp.split(
        proj, [int(c) for c in np.cumsum(IN_SPLITS)[:-1]], axis=-1)

    def pad(a):
        return jnp.pad(a, ((0, 0), (0, Lp - L)) + ((0, 0),) * (a.ndim - 2))

    qa = partial_rope(pad(q).reshape(B, Lp, ATT_HEADS, ATT_HEAD_DIM), pos)
    ka = partial_rope(pad(k).reshape(B, Lp, ATT_KV_HEADS, ATT_HEAD_DIM), pos)
    va = pad(v).reshape(B, Lp, ATT_KV_HEADS, ATT_HEAD_DIM)
    iqa = partial_rope(pad(iq).reshape(B, Lp, IDX_HEADS, IDX_DIM), pos)
    ika = partial_rope(pad(ik)[:, :, None, :], pos)[:, :, 0, :]
    att = dsa_attention(qa, ka, va, iqa, ika, pad(iw), L)[:, :L]

    o = hgrn2(hq, hf, hi, lb)
    o = o * lax.rsqrt(jnp.mean(o * o, axis=-1, keepdims=True) + EPS)
    o = o * hgrn_norm_g.reshape(HG_HEADS, HG_DV).astype(F32)
    o = o.reshape(B, L, HG_WIDTH) * jax.nn.silu(hg.astype(F32))
    hgr = o.astype(h.dtype)

    mix = jax.nn.sigmoid(ga) * (att @ w_up_attn) + jax.nn.sigmoid(gh) * (hgr @ w_up_hgrn)
    h = h + mix @ w_out

    h = h + moe(rmsnorm(h, ffn_norm_g), router_w, router_b, w_gate, b_gate, w_up, b_up, w_down, b_down)
    return h

def setup_inputs(seed: int = 0) -> dict:
    key = jax.random.key(seed)
    ks = jax.random.split(key, 20)
    D = D_MODEL

    def nrm(k, shape, scale):
        return jax.random.normal(k, shape, F32) * scale

    return {
        "x": nrm(ks[0], (BATCH, SEQ, D), 1.0),
        "meta_tokens": nrm(ks[1], (N_META, D), 1.0),
        "attn_norm_g": 1.0 + nrm(ks[2], (DEPTH, D), 0.01),
        "w_in": nrm(ks[3], (DEPTH, D, IN_COLS), D ** -0.5),
        "hgrn_norm_g": 1.0 + nrm(ks[4], (DEPTH, HG_WIDTH), 0.01),
        "w_up_attn": nrm(ks[5], (DEPTH, ATT_WIDTH, D), ATT_WIDTH ** -0.5),
        "w_up_hgrn": nrm(ks[6], (DEPTH, HG_WIDTH, D), HG_WIDTH ** -0.5),
        "w_out": nrm(ks[7], (DEPTH, D, D), D ** -0.5),
        "hgrn_lb_logits": nrm(ks[8], (DEPTH + 1, HG_KWIDTH), 0.5),
        "ffn_norm_g": 1.0 + nrm(ks[9], (DEPTH, D), 0.01),
        "router_w": nrm(ks[10], (DEPTH, D, N_EXPERTS), D ** -0.5),
        "router_b": nrm(ks[11], (DEPTH, N_EXPERTS), 0.01),
        "w_gate": nrm(ks[12], (DEPTH, N_EXPERTS, D, D_FF), D ** -0.5),
        "b_gate": nrm(ks[13], (DEPTH, N_EXPERTS, D_FF), 0.01),
        "w_up": nrm(ks[14], (DEPTH, N_EXPERTS, D, D_FF), D ** -0.5),
        "b_up": nrm(ks[15], (DEPTH, N_EXPERTS, D_FF), 0.01),
        "w_down": nrm(ks[16], (DEPTH, N_EXPERTS, D_FF, D), D_FF ** -0.5),
        "b_down": nrm(ks[17], (DEPTH, N_EXPERTS, D), 0.01),
        "final_norm_g": 1.0 + nrm(ks[18], (D,), 0.01),
    }

def reference(x, meta_tokens, attn_norm_g, w_in, hgrn_norm_g, w_up_attn, w_up_hgrn, w_out,
              hgrn_lb_logits, ffn_norm_g, router_w, router_b, w_gate, b_gate, w_up, b_up,
              w_down, b_down, final_norm_g):
    B = x.shape[0]
    meta = jnp.broadcast_to(meta_tokens[None].astype(x.dtype), (B, N_META, D_MODEL))
    h = jnp.concatenate([meta, x], axis=1)
    lb_all = jnp.cumsum(jax.nn.softmax(hgrn_lb_logits.astype(F32), axis=0), axis=0)
    for l in range(DEPTH):
        h = hybrid_layer(h, attn_norm_g[l], w_in[l], hgrn_norm_g[l], w_up_attn[l], w_up_hgrn[l],
                         w_out[l], lb_all[l], ffn_norm_g[l], router_w[l], router_b[l],
                         w_gate[l], b_gate[l], w_up[l], b_up[l], w_down[l], b_down[l])
    return rmsnorm(h[:, N_META:], final_norm_g)


_drawn_inputs = setup_inputs


def setup_inputs(seed=0):
    import zlib

    import numpy as np

    out = dict(_drawn_inputs(seed))
    spreads = {}
    factors = {'hgrn_norm_g': 2.882, 'b_gate': 8.0, 'b_up': 8.0, 'b_down': 8.0, 'final_norm_g': 5.808}
    for name, (base, spread) in spreads.items():
        noise = np.random.default_rng([zlib.crc32(name.encode()), seed]).standard_normal(out[name].shape)
        drawn = base * np.exp(spread * noise) if base else spread * noise
        out[name] = __import__('jax').numpy.asarray(drawn.astype(out[name].dtype))
    for name, factor in factors.items():
        out[name] = (out[name] * factor).astype(out[name].dtype)
    return out
```

```python
from contextlib import ExitStack

import numpy as np

import concourse.bass as bass
from concourse import mybir

F32 = mybir.dt.float32
I32 = mybir.dt.int32
U32 = mybir.dt.uint32
ALU = mybir.AluOpType
ACT = mybir.ActivationFunctionType
AX = mybir.AxisListType

P = 128
D = 1024
KT = D // P
SEQ, N_META = 1024, 16
L = SEQ + N_META
NT = -(-L // P)
LP = NT * P
TAIL = L - (NT - 1) * P
EPS = 1e-5

ATT_HEADS, KV_HEADS, HD = 8, 2, 64
IDX_HEADS, IDX_DIM = 8, 32
QK_HEADS = ATT_HEADS + KV_HEADS
C_Q = 0
C_K = C_Q + ATT_HEADS * HD
C_V = C_K + KV_HEADS * HD
C_IQ = C_V + KV_HEADS * HD
C_IK = C_IQ + IDX_HEADS * IDX_DIM
C_IW = C_IK + IDX_DIM
C_HQ = C_IW + IDX_HEADS
HG_HEADS, HG_D = 4, 128
HGW = HG_HEADS * HG_D
C_HF, C_HI, C_HG = C_HQ + HGW, C_HQ + 2 * HGW, C_HQ + 3 * HGW
C_GA = C_HG + HGW
C_GH = C_GA + D
IN_COLS = C_GH + D
CHUNKS = 12
CW = IN_COLS // CHUNKS

IDX_SCALE = float(IDX_DIM ** -0.5) * float(IDX_HEADS ** -0.5)
ATT_SCALE = float(HD) ** -0.5
K_SEL = min(256, L // 4)
ROUNDS = K_SEL // 8
MASKED = -3.0e38
TAKEN = -3.3e38
SPLIT = -3.15e38
DROP = -1.0e30

ROT, IROT = HD // 4, IDX_DIM // 4
N_EXP = 32
TOP = 4
HALF = 80
ITEM = 2 * HALF
MORE = TOP * L // ITEM
ITEMS = N_EXP + MORE
SLOTS = ITEMS * ITEM
PAD = SLOTS + ITEM
TABLE = PAD + TOP * P
ZERO_P, ZERO_DMAS = 104, NT - 1
ZERO_N = MORE * ITEM // ZERO_P // ZERO_DMAS
assert ZERO_N * ZERO_P * ZERO_DMAS == MORE * ITEM
TAB = 2 * QK_HEADS * (ROT // 2) + 2 * (IDX_HEADS + 1) * (IROT // 2)


def rope_tables():
    pos = np.arange(LP, dtype=np.float32)
    parts = []
    for rot, heads in ((ROT, QK_HEADS), (IROT, IDX_HEADS + 1)):
        half = rot // 2
        inv = np.float32(500000.0) ** (-np.arange(half, dtype=np.float32) * np.float32(2.0) / np.float32(rot))
        ang = (pos[:, None] * inv[None, :].astype(np.float32)).astype(np.float32)
        for f in (np.cos, np.sin):
            parts.append(np.tile(f(ang).astype(np.float32), (1, heads)))
    return np.concatenate(parts, axis=1)


class Chain:

    def __init__(self, eng, sem, base=0):
        self.eng, self.sem, self.base, self.n = eng, sem, base, 0

    def link(self, ins):
        self.n += 1
        ins.then_inc(self.sem, 1)
        self.eng.wait_ge(self.sem, self.base + self.n)


def stage_project(nc, io, scr, ident):
    with ExitStack() as ctx:
        def sb(name, shape, dt=F32):
            return ctx.enter_context(nc.sbuf_tensor(name, shape, dt))

        def sem(name):
            return ctx.enter_context(nc.semaphore(name))

        h_rows = sb("p_h_rows", [P, NT, D])
        g_bc = sb("p_g_bc", [P, D])
        ssq = sb("p_ssq", [P, NT])
        ms = sb("p_ms", [P, NT])
        rms = sb("p_rms", [P, NT])
        rstd = sb("p_rstd", [P, NT])
        xn = sb("p_xn", [P, 2, D])
        xnT = sb("p_xnT", [P, KT, LP])
        w = sb("p_w", [P, 2, KT, CW])
        NB = 6
        stage = sb("p_stage", [P, NB, CW])
        tp = ctx.enter_context(nc.psum_tensor("p_tp", [P, 2, 512], F32))
        acc = ctx.enter_context(nc.psum_tensor("p_acc", [P, NB, 512], F32))

        s_zero = sem("p_zeroed")
        s_h = sem("p_h_landed")
        s_g = sem("p_g_landed")
        s_hout = sem("p_h_stored")
        s_ssq = sem("p_ssq_ready")
        s_stat = sem("p_stat_chain")
        s_ms = sem("p_ms_ready")
        s_rms = sem("p_rms_ready")
        s_xn = sem("p_xn_ready")
        s_tp = sem("p_tp_ready")
        s_tpa = sem("p_tp_taken_act")
        s_tpv = sem("p_tp_taken_dve")
        s_w = [sem(f"p_w_landed{b}") for b in range(2)]
        s_mm = sem("p_product_ready")
        s_eva = sem("p_evacuated_act")
        s_evv = sem("p_evacuated_dve")
        s_st = [sem(f"p_stored{b}") for b in range(NB)]

        w_in = io["w_in"][0].rearrange("(kt p) n -> p kt n", p=P)
        x = io["x"][0]
        block = ctx.enter_context(nc.Block())

        @block.sync
        def _(sp):
            sp.dma_start(g_bc[:, :], io["attn_norm_g"].partition_broadcast(P)).then_inc(s_g, 16)
            sp.dma_start(h_rows[0:N_META, 0, :], io["meta_tokens"]).then_inc(s_h, 16)
            sp.dma_start(h_rows[N_META:P, 0, :], x[0:P - N_META, :]).then_inc(s_h, 16)
            sp.dma_start(h_rows[:, 1:NT - 1, :],
                         x[P - N_META:SEQ - TAIL, :].rearrange("(t p) d -> p t d", p=P)).then_inc(s_h, 16)
            sp.wait_ge(s_zero, 1)
            sp.dma_start(h_rows[0:TAIL, NT - 1, :], x[SEQ - TAIL:SEQ, :]).then_inc(s_h, 16)
            sp.wait_ge(s_h, 64)
            sp.dma_start(scr["h"].rearrange("(t p) d -> p t d", p=P), h_rows[:, :, :]).then_inc(s_hout, 16)
            with sp.Fori(0, CHUNKS // 2) as c2:
                for u in range(2):
                    for t in range(NT):
                        n = u * NT + t
                        b = n % NB
                        if n % 2 == 0:
                            sp.wait_ge(s_eva, c2 * NT + (n // 2 + 1))
                        else:
                            sp.wait_ge(s_evv, c2 * NT + (n // 2 + 1))
                        sp.dma_start(scr["proj"][t * P:(t + 1) * P, bass.ds(c2 * (2 * CW) + u * CW, CW)],
                                     stage[:, b, :]).then_inc(s_st[b], 16)
            for b in range(NB):
                sp.wait_ge(s_st[b], 16 * (CHUNKS * NT // NB))
            sp.wait_ge(s_hout, 16)

        @block.gpsimd
        def _(pool):
            pool.dma_start(w[:, 0, :, :], w_in[:, :, 0:CW]).then_inc(s_w[0], 16)
            pool.dma_start(w[:, 1, :, :], w_in[:, :, CW:2 * CW]).then_inc(s_w[1], 16)
            with pool.Fori(1, CHUNKS // 2) as c2:
                for u in range(2):
                    pool.wait_ge(s_mm, (c2 - 1) * (2 * NT) + (u + 1) * NT)
                    pool.dma_start(w[:, u, :, :], w_in[:, :, bass.ds(c2 * (2 * CW) + u * CW, CW)]).then_inc(s_w[u], 16)

        @block.scalar
        def _(act):
            act.wait_ge(s_h, 64)
            for t in range(NT):
                if t >= 2:
                    act.wait_ge(s_ssq, t - 1)
                act.activation(xn[:, t % 2, :], h_rows[:, t, :], ACT.Square,
                               accum_out=ssq[:, t:t + 1]).then_inc(s_ssq, 1)
            act.wait_ge(s_ms, 1)
            act.activation(rms[:, :], ms[:, :], ACT.Sqrt).then_inc(s_rms, 1)
            for t in range(NT):
                act.wait_ge(s_tp, 2 * t + 1)
                act.copy(xnT[:, 0:4, t * P:(t + 1) * P],
                         tp[:, 0, :].rearrange("p (k t) -> p k t", k=4)).then_inc(s_tpa, 1)
            with act.Fori(0, CHUNKS // 2) as c2:
                for n in range(0, 2 * NT, 2):
                    b = n % NB
                    act.wait_ge(s_mm, c2 * (2 * NT) + (n + 1))
                    if n >= NB:
                        act.wait_ge(s_st[b], c2 * (16 * 2 * NT // NB) + 16 * (n // NB))
                    else:
                        act.wait_ge(s_st[b], c2 * (16 * 2 * NT // NB))
                    act.copy(stage[:, b, :], acc[:, b, 0:CW]).then_inc(s_eva, 1)

        @block.vector
        def _(dve):
            dve.memset(h_rows[:, NT - 1, :], 0.0).then_inc(s_zero, 1)
            dve.wait_ge(s_ssq, NT)
            dve.tensor_scalar(ms[:, :], ssq[:, :], 1.0 / D, EPS, ALU.mult, ALU.add).then_inc(s_ms, 1)
            dve.wait_ge(s_rms, 1)
            dve.reciprocal(rstd[:, :], rms[:, :]).then_inc(s_stat, 1)
            dve.wait_ge(s_stat, 1)
            dve.wait_ge(s_g, 16)

            def evacuate(t):
                dve.wait_ge(s_tp, 2 * t + 2)
                dve.tensor_copy(xnT[:, 4:8, t * P:(t + 1) * P],
                                tp[:, 1, :].rearrange("p (k t) -> p k t", k=4)).then_inc(s_tpv, 1)

            for t in range(NT):
                if t >= 2:
                    evacuate(t - 2)
                dve.scalar_tensor_tensor(out=xn[:, t % 2, :], in0=h_rows[:, t, :], scalar=rstd[:, t:t + 1],
                                         in1=g_bc[:, :], op0=ALU.mult, op1=ALU.mult).then_inc(s_xn, 1)
            evacuate(NT - 2)
            evacuate(NT - 1)
            with dve.Fori(0, CHUNKS // 2) as c2:
                for n in range(1, 2 * NT, 2):
                    b = n % NB
                    dve.wait_ge(s_mm, c2 * (2 * NT) + (n + 1))
                    if n >= NB:
                        dve.wait_ge(s_st[b], c2 * (16 * 2 * NT // NB) + 16 * (n // NB))
                    else:
                        dve.wait_ge(s_st[b], c2 * (16 * 2 * NT // NB))
                    dve.tensor_copy(stage[:, b, :], acc[:, b, 0:CW]).then_inc(s_evv, 1)

        @block.tensor
        def _(pe):
            for t in range(NT):
                pe.wait_ge(s_xn, t + 1)
                for half, taken in ((0, s_tpa), (1, s_tpv)):
                    if t >= 1:
                        pe.wait_ge(taken, t)
                    for j in range(4):
                        k = half * 4 + j
                        last = pe.transpose(tp[:, half, j * P:(j + 1) * P], xn[:, t % 2, k * P:(k + 1) * P],
                                            ident[:, :])
                    last.then_inc(s_tp, 1)
            pe.wait_ge(s_tpa, NT)
            pe.wait_ge(s_tpv, NT)
            with pe.Fori(0, CHUNKS // 2) as c2:
                for u in range(2):
                    pe.wait_ge(s_w[u], c2 * 16 + 16)
                    for t in range(NT):
                        n = u * NT + t
                        b = n % NB
                        if n % 2 == 0:
                            pe.wait_ge(s_eva, c2 * NT + max(0, n // 2 + 1 - NB // 2)) if n >= NB else \
                                pe.wait_ge(s_eva, c2 * NT)
                        else:
                            pe.wait_ge(s_evv, c2 * NT + max(0, n // 2 + 1 - NB // 2)) if n >= NB else \
                                pe.wait_ge(s_evv, c2 * NT)
                        for k in range(KT):
                            last = pe.matmul(acc[:, b, 0:CW], xnT[:, k, t * P:(t + 1) * P], w[:, u, k, :],
                                             start=(k == 0), stop=(k == KT - 1))
                        last.then_inc(s_mm, 1)


def stage_attention(nc, io, scr, ident):
    W = [min(P * (i + 1), L) for i in range(NT)]
    ZW = P * (NT - 1)
    with ExitStack() as ctx:
        def sb(name, shape, dt=F32):
            return ctx.enter_context(nc.sbuf_tensor(name, shape, dt))

        def sem(name):
            return ctx.enter_context(nc.semaphore(name))

        tab = sb("a_tab", [P, NT, TAB])
        rows = sb("a_rows", [P, 2, C_HQ])
        t1 = sb("a_t1", [P, 4, QK_HEADS * ROT // 2])
        t2 = sb("a_t2", [P, 4, (IDX_HEADS + 1) * IROT // 2])
        ik4 = sb("a_ik4", [P, 2, 4 * IDX_DIM])
        qpair = sb("a_qpair", [P, 2, 4, 2, HD])
        iws = sb("a_iws", [P, NT, IDX_HEADS])
        keyT = sb("a_keyT", [P, LP])
        ikT = sb("a_ikT", [P, LP])
        val = sb("a_val", [P, NT, KV_HEADS * HD])
        qT = sb("a_qT", [P, 2, 4, P])
        iqT = sb("a_iqT", [P, 2, 2, P])
        start = sb("a_start", [P, ZW + P])
        rel = sb("a_rel", [P, 2, L])
        score = sb("a_score", [P, 2, L])
        top8 = sb("a_top8", [P, 8])
        drop = sb("a_drop", [P, L])
        lg = sb("a_lg", [P, 2, L])
        mx = sb("a_mx", [P, 2, ATT_HEADS])
        nmx = sb("a_nmx", [P, 2, ATT_HEADS])
        rsum = sb("a_rsum", [P, 2, ATT_HEADS])
        rinv = sb("a_rinv", [P, ATT_HEADS])
        pT = sb("a_pT", [P, 2, NT, P])
        att = sb("a_att", [P, 2, ATT_HEADS * HD])
        ps_x = ctx.enter_context(nc.psum_tensor("a_ps_x", [P, 3, 512], F32))
        ps_l = ctx.enter_context(nc.psum_tensor("a_ps_l", [P, 3, 512], F32))
        ps_t = ctx.enter_context(nc.psum_tensor("a_ps_t", [P, 512], F32))
        ps_o = ctx.enter_context(nc.psum_tensor("a_ps_o", [P, 512], F32))

        s_tab = sem("a_tab_landed")
        s_row = [sem(f"a_rows_landed{b}") for b in range(2)]
        s_mask = sem("a_mask_ready")
        s_rope = sem("a_rope_done")
        s_copy = sem("a_value_and_ik_copied")
        s_t = sem("a_transposes_ready")
        s_te = sem("a_transposes_taken")
        s_x = sem("a_index_product_ready")
        s_relu = sem("a_relu_ready")
        s_acc = sem("a_score_added")
        s_dv = sem("a_dve_chain")
        s_l = sem("a_logit_product_ready")
        s_lm = sem("a_logit_masked")
        s_nm = sem("a_negmax_ready")
        s_exp = sem("a_exp_ready")
        s_pv = sem("a_pv_done")
        s_att = sem("a_att_ready")
        s_out = [sem(f"a_att_stored{b}") for b in range(2)]
        s_zs = sem("a_zeros_stored")

        number = {}
        for i in range(-1, NT):
            if i + 1 < NT:
                number["q", i + 1] = len(number)
                number["k", i + 1] = len(number)
            if i >= 0:
                for h in range(ATT_HEADS):
                    for g in range(-(-(i + 1) // 4)):
                        number["p", i, h, g] = len(number)

        block = ctx.enter_context(nc.Block())

        def store(sp, i):
            sp.wait_ge(s_att, i + 1)
            sp.dma_start(scr["att"][i * P:(i + 1) * P, :], att[:, i % 2, :]).then_inc(s_out[i % 2], 16)

        @block.sync
        def _(sp):
            sp.dma_start(tab[:, :, :], io["rope"].rearrange("(t p) c -> p t c", p=P)).then_inc(s_tab, 16)
            for i in range(NT):
                if i >= 2:
                    sp.wait_ge(s_t, number["k", i - 2] + 1)
                    sp.wait_ge(s_copy, 4 * (i - 1))
                sp.dma_start(rows[:, i % 2, :], scr["proj"][i * P:(i + 1) * P, 0:C_HQ]).then_inc(s_row[i % 2], 16)
                if i >= 3:
                    store(sp, i - 3)
                if i < ZERO_DMAS:
                    if i == 0:
                        sp.wait_ge(s_mask, 1)
                    r0 = N_EXP * ITEM + i * ZERO_P * ZERO_N
                    sp.dma_start(scr["y"][r0:r0 + ZERO_P * ZERO_N, :].rearrange("(p n) d -> p n d", p=ZERO_P),
                                 start[0:ZERO_P, 0:D].unsqueeze(1).to_broadcast([ZERO_P, ZERO_N, D])).then_inc(s_zs, 16)
            for i in range(NT - 3, NT):
                store(sp, i)
            sp.wait_ge(s_zs, 16 * ZERO_DMAS)
            for b in range(2):
                sp.wait_ge(s_out[b], 16 * len(range(b, NT, 2)))

        @block.gpsimd
        def _(pool):
            pool.memset(start[:, :], 0.0).then_inc(s_mask, 1)
            pool.wait_ge(s_mask, 1)
            pool.affine_select(out=start[:, ZW:], in_=start[:, ZW:], compare_op=ALU.is_ge, fill=MASKED,
                               base=0, pattern=[[-1, P]], channel_multiplier=1).then_inc(s_mask, 1)
            for i in range(NT):
                pool.wait_ge(s_rope, i + 1)
                pool.tensor_copy(val[:, i, :], rows[:, i % 2, C_V:C_IQ]).then_inc(s_copy, 1)
                if i >= 2:
                    pool.wait_ge(s_t, number["k", i - 2] + 1)
                ik = rows[:, i % 2, C_IK:C_IW].unsqueeze(1).to_broadcast([P, 4, IDX_DIM])
                pool.tensor_copy(ik4[:, i % 2, :].rearrange("p (r d) -> p r d", r=4), ik).then_inc(s_copy, 1)
                for g in range(KV_HEADS):
                    pool.tensor_copy(qpair[:, i % 2, :, g, :],
                                     rows[:, i % 2, g * 4 * HD:(g + 1) * 4 * HD].rearrange("p (m d) -> p m d", d=HD)
                                     ).then_inc(s_copy, 1)

        @block.vector
        def _(dve):
            ch = Chain(dve, s_dv)

            def rope(i):
                dve.wait_ge(s_row[i % 2], 16 * (i // 2 + 1))
                parts = []
                c0 = 0
                for heads, d, half, base, t in ((QK_HEADS, HD, ROT // 2, C_Q, t1),
                                                (IDX_HEADS + 1, IDX_DIM, IROT // 2, C_IQ, t2)):
                    n = heads * half
                    v = rows[:, i % 2, base:base + heads * d].rearrange("p (h d) -> p h d", d=d) \
                        if base == C_IQ else rows[:, i % 2, 0:heads * d].rearrange("p (h d) -> p h d", d=d)
                    co = tab[:, i, c0:c0 + n].rearrange("p (h d) -> p h d", d=half)
                    si = tab[:, i, c0 + n:c0 + 2 * n].rearrange("p (h d) -> p h d", d=half)
                    c0 += 2 * n
                    tv = [t[:, j, :].rearrange("p (h d) -> p h d", d=half) for j in range(4)]
                    parts.append((v[:, :, 0:half], v[:, :, half:2 * half], co, si, tv))
                for x1, x2, co, si, tv in parts:
                    dve.tensor_tensor(tv[0], x1, co, ALU.mult)
                    dve.tensor_tensor(tv[1], x2, si, ALU.mult)
                    dve.tensor_tensor(tv[2], x2, co, ALU.mult)
                    last = dve.tensor_tensor(tv[3], x1, si, ALU.mult)
                ch.link(last)
                for x1, x2, co, si, tv in parts:
                    dve.tensor_tensor(x1, tv[0], tv[1], ALU.subtract)
                    dve.tensor_tensor(x2, tv[2], tv[3], ALU.add)
                dve.tensor_scalar(iws[:, i, :], rows[:, i % 2, C_IW:C_HQ], IDX_SCALE, None,
                                  ALU.mult).then_inc(s_rope, 1)

            def add_head(i, h):
                n = IDX_HEADS * i + h
                w = W[i]
                dve.wait_ge(s_relu, n + 1)
                before = start[:, ZW - P * i:ZW - P * i + w] if h == 0 else score[:, i % 2, 0:w]
                if h:
                    dve.wait_ge(s_acc, n)
                dve.scalar_tensor_tensor(out=score[:, i % 2, 0:w], in0=rel[:, n % 2, 0:w], scalar=iws[:, i, h:h + 1],
                                         in1=before, op0=ALU.mult, op1=ALU.add).then_inc(s_acc, 1)

            def select(i):
                s = score[:, i % 2, 0:W[i]]
                dve.wait_ge(s_acc, IDX_HEADS * (i + 1))
                if P * (i + 1) > K_SEL:
                    for r in range(ROUNDS):
                        ch.link(dve.max(top8[:, :], s))
                        ch.link(dve.match_replace(s, top8[:, :], s, TAKEN))
                    ch.link(dve.tensor_scalar(drop[:, 0:W[i]], s, SPLIT, DROP, ALU.is_gt, ALU.mult))
                else:
                    ch.link(dve.tensor_scalar(drop[:, 0:W[i]], s, MASKED / 2, DROP, ALU.is_le, ALU.mult))

            def mask_logits(i, h):
                n = ATT_HEADS * i + h
                w = W[i]
                dve.wait_ge(s_l, n + 1)
                if n >= 2:
                    dve.wait_ge(s_pv, n - 1)
                dve.tensor_tensor_reduce(lg[:, n % 2, 0:w], ps_l[:, :, :].rearrange("p b c -> p (b c)")[:, 0:w],
                                         drop[:, 0:w], 1.0, -3.4e38, ALU.add, ALU.max,
                                         mx[:, i % 2, h:h + 1]).then_inc(s_lm, 1)
                dve.wait_ge(s_lm, n + 1)
                dve.tensor_scalar(nmx[:, i % 2, h:h + 1], mx[:, i % 2, h:h + 1], -ATT_SCALE, None,
                                  ALU.mult).then_inc(s_nm, 1)

            def normalize(i):
                dve.wait_ge(s_pv, ATT_HEADS * (i + 1))
                ch.link(dve.reciprocal(rinv[:, :], rsum[:, i % 2, :]))
                if i >= 2:
                    dve.wait_ge(s_out[i % 2], 16 * (i // 2))
                dve.tensor_tensor(att[:, i % 2, :].rearrange("p (h d) -> p h d", d=HD),
                                  ps_o[:, :].rearrange("p (h d) -> p h d", d=HD),
                                  rinv[:, :].unsqueeze(2).to_broadcast([P, ATT_HEADS, HD]),
                                  ALU.mult).then_inc(s_att, 1)

            dve.wait_ge(s_tab, 16)
            rope(0)
            dve.wait_ge(s_mask, 2)
            for h in range(IDX_HEADS):
                add_head(0, h)
            for i in range(NT):
                if i + 1 < NT:
                    rope(i + 1)
                select(i)
                for h in range(ATT_HEADS):
                    mask_logits(i, h)
                    if i + 1 < NT:
                        add_head(i + 1, h)
                normalize(i)

        @block.scalar
        def _(act):
            def take_rows(i):
                act.wait_ge(s_t, number["q", i] + 1)
                act.copy(qT[:, i % 2, :, :], ps_t[:, :].rearrange("p (m t) -> p m t", m=4)).then_inc(s_te, 1)
                act.wait_ge(s_t, number["k", i] + 1)
                act.copy(keyT[:, i * P:(i + 1) * P], ps_t[:, 0:P])
                act.copy(iqT[:, i % 2, :, :], ps_t[:, P:3 * P].rearrange("p (m t) -> p m t", m=2))
                act.copy(ikT[:, i * P:(i + 1) * P], ps_t[:, 3 * P:4 * P]).then_inc(s_te, 1)

            def relu(i, h):
                n = IDX_HEADS * i + h
                act.wait_ge(s_x, n + 1)
                if n >= 2:
                    act.wait_ge(s_acc, n - 1)
                act.activation(rel[:, n % 2, 0:W[i]], ps_x[:, :, :].rearrange("p b c -> p (b c)")[:, 0:W[i]],
                               ACT.Relu).then_inc(s_relu, 1)

            def exponent(i, h):
                n = ATT_HEADS * i + h
                act.wait_ge(s_nm, n + 1)
                act.activation(lg[:, n % 2, 0:W[i]], lg[:, n % 2, 0:W[i]], ACT.Exp, bias=nmx[:, i % 2, h:h + 1],
                               scale=ATT_SCALE, accum_out=rsum[:, i % 2, h:h + 1]).then_inc(s_exp, 1)

            def take_probs(i, h):
                n = ATT_HEADS * i + h
                if n >= 2:
                    act.wait_ge(s_pv, n - 1)
                for g in range(-(-(i + 1) // 4)):
                    act.wait_ge(s_t, number["p", i, h, g] + 1)
                    k = min(4, i + 1 - 4 * g)
                    rows_ = min(P, W[i] - 4 * g * P)
                    act.copy(pT[0:rows_, n % 2, 4 * g:4 * g + k, :],
                             ps_t[0:rows_, 0:k * P].rearrange("p (m t) -> p m t", m=k)).then_inc(s_te, 1)

            take_rows(0)
            for h in range(IDX_HEADS):
                relu(0, h)
            for i in range(NT):
                if i + 1 < NT:
                    take_rows(i + 1)
                for h in range(ATT_HEADS):
                    if i + 1 < NT:
                        relu(i + 1, h)
                    exponent(i, h)
                    if h:
                        take_probs(i, h - 1)
                take_probs(i, ATT_HEADS - 1)

        @block.tensor
        def _(pe):
            def bank_free(key):
                if number[key]:
                    pe.wait_ge(s_te, number[key])

            def turn_rows(i):
                pe.wait_ge(s_rope, i + 1)
                pe.wait_ge(s_copy, 4 * (i + 1))
                bank_free(("q", i))
                for m in range(4):
                    last = pe.transpose(ps_t[:, m * P:(m + 1) * P],
                                        qpair[:, i % 2, m, :, :].rearrange("p g d -> p (g d)"), ident[:, :])
                last.then_inc(s_t, 1)
                bank_free(("k", i))
                pe.transpose(ps_t[:, 0:P], rows[:, i % 2, C_K:C_V], ident[:, :])
                pe.transpose(ps_t[:, P:2 * P], rows[:, i % 2, C_IQ:C_IQ + P], ident[:, :])
                pe.transpose(ps_t[:, 2 * P:3 * P], rows[:, i % 2, C_IQ + P:C_IK], ident[:, :])
                pe.transpose(ps_t[:, 3 * P:4 * P], ik4[:, i % 2, :], ident[:, :]).then_inc(s_t, 1)

            def index_product(i, h):
                n = IDX_HEADS * i + h
                if h == 0:
                    pe.wait_ge(s_te, number["k", i] + 1)
                if n:
                    pe.wait_ge(s_relu, n)
                r = IDX_DIM * (h % 4)
                for c in range(0, W[i], 512):
                    e = min(c + 512, W[i])
                    last = pe.matmul(ps_x[:, c // 512, 0:e - c], iqT[r:r + IDX_DIM, i % 2, h // 4, :],
                                     ikT[r:r + IDX_DIM, c:e], start=True, stop=True)
                last.then_inc(s_x, 1)

            def logits(i, h):
                n = ATT_HEADS * i + h
                if n:
                    pe.wait_ge(s_lm, n)
                r = HD * (h // 4)
                for c in range(0, W[i], 512):
                    e = min(c + 512, W[i])
                    last = pe.matmul(ps_l[:, c // 512, 0:e - c], qT[r:r + HD, i % 2, h % 4, :],
                                     keyT[r:r + HD, c:e], start=True, stop=True)
                last.then_inc(s_l, 1)

            def turn_probs(i, h):
                n = ATT_HEADS * i + h
                pe.wait_ge(s_exp, n + 1)
                for g in range(-(-(i + 1) // 4)):
                    bank_free(("p", i, h, g))
                    for t in range(4 * g, min(4 * g + 4, i + 1)):
                        k = min(P, W[i] - t * P)
                        last = pe.transpose(ps_t[0:k, (t - 4 * g) * P:(t - 4 * g + 1) * P],
                                            lg[:, n % 2, t * P:t * P + k], ident[:, :])
                    last.then_inc(s_t, 1)

            def attend(i, h):
                n = ATT_HEADS * i + h
                groups = -(-(i + 1) // 4)
                pe.wait_ge(s_te, number["p", i, h, groups - 1] + 1)
                if h == 0 and i:
                    pe.wait_ge(s_att, i)
                v = HD * (h // 4)
                for t in range(i + 1):
                    k = min(P, W[i] - t * P)
                    last = pe.matmul(ps_o[:, h * HD:(h + 1) * HD], pT[0:k, n % 2, t, :], val[0:k, t, v:v + HD],
                                     start=(t == 0), stop=(t == i))
                last.then_inc(s_pv, 1)

            turn_rows(0)
            for h in range(IDX_HEADS):
                index_product(0, h)
            for i in range(NT):
                if i + 1 < NT:
                    turn_rows(i + 1)
                for h in range(ATT_HEADS):
                    if i + 1 < NT:
                        index_product(i + 1, h)
                    logits(i, h)
                    if h:
                        turn_probs(i, h - 1)
                        attend(i, h - 1)
                turn_probs(i, ATT_HEADS - 1)
                attend(i, ATT_HEADS - 1)


BL = 32
NB4 = P // BL
BIG = 1.0e37


def stage_hgrn(nc, io, scr, ident):
    with ExitStack() as ctx:
        def sb(name, shape, dt=F32):
            return ctx.enter_context(nc.sbuf_tensor(name, shape, dt))

        def bank(name):
            return ctx.enter_context(nc.psum_tensor(name, [P, 512], F32))

        def sem(name):
            return ctx.enter_context(nc.semaphore(name))

        lb_rows = sb("g_lb_rows", [2 * HG_HEADS, P])
        lbt = sb("g_lbt", [P, 8, HG_HEADS])
        g_bc = sb("g_g_bc", [P, HGW])
        ones = sb("g_run", [P, HGW])
        cmask = sb("g_cmask", [P, HG_HEADS, BL])
        qf = sb("g_qf", [P, 2 * HGW])
        v = sb("g_v", [P, HGW])
        hg = sb("g_hg", [P, HGW])
        sg = sb("g_sg", [P, HGW])
        f = sb("g_f", [P, HGW])
        kk = sb("g_kk", [P, HGW])
        lf = sb("g_lf", [P, HGW])
        b = sb("g_b", [P, HGW])
        bm = sb("g_bm", [P, HGW])
        bl = sb("g_bl", [P, HGW])
        e = sb("g_e", [P, 4, HGW])
        dec = sb("g_dec", [P, HG_HEADS, NB4])
        qe = sb("g_qe", [P, HGW])
        ke = sb("g_ke", [P, HGW])
        qs = sb("g_qs", [P, HGW])
        ks = sb("g_ks", [P, HGW])
        kst = sb("g_kst", [P, HGW])
        at = sb("g_at", [P, HG_HEADS, BL])
        state = sb("g_state", [P, NB4, HGW])
        sq = sb("g_sq", [P, HG_HEADS, P])
        st4 = sb("g_st4", [P, 4, HG_HEADS])
        sl = sb("g_sl", [P, 2, HGW])
        on = sb("g_on", [P, HGW])
        res = sb("g_res", [P, HGW])
        ps_q, ps_f, ps_k, ps_o = bank("g_ps_q"), bank("g_ps_f"), bank("g_ps_k"), bank("g_ps_o")
        ps_s = [bank(f"g_ps_s{j}") for j in range(NB4)]

        s_lb = sem("g_lb_landed")
        s_gb = sem("g_g_landed")
        s_qf = sem("g_qf_landed")
        s_v = sem("g_v_landed")
        s_hg = sem("g_hg_landed")
        s_cst = sem("g_constants")
        s_lbt = sem("g_lb_turned")
        s_dv = sem("g_dve_chain")
        s_ac = sem("g_act_chain")
        s_lbe = sem("g_lb_exp_ready")
        s_lbm = sem("g_lb_shifted")
        s_st0 = sem("g_state_zeroed")
        s_turn = sem("g_q_and_f_turned")
        s_eg = sem("g_exp_gate_ready")
        s_f = sem("g_f_ready")
        s_lf = sem("g_log_ready")
        s_b = sem("g_b_ready")
        s_e = sem("g_exps_ready")
        s_qk = sem("g_scaled_ready")
        s_kt = sem("g_ks_turned")
        s_kst = sem("g_kst_ready")
        s_a = sem("g_pairs_ready")
        s_at = sem("g_masked_ready")
        s_ps = sem("g_outer_ready")
        s_s = sem("g_state_ready")
        s_o = sem("g_o_ready")
        s_sq = sem("g_squares_ready")
        s_var = sem("g_variance_ready")
        s_rs = sem("g_rstd_ready")
        s_sl = sem("g_gate_exp_ready")
        s_res = sem("g_result_ready")
        s_out = sem("g_result_stored")

        def blocks(ap):
            return ap.rearrange("p (c t) -> p c t", t=BL)

        block = ctx.enter_context(nc.Block())

        @block.sync
        def _(sp):
            sp.dma_start(lb_rows[:, :], io["hgrn_lb_logits"].rearrange("r (h d) -> (r h) d", d=P)).then_inc(s_lb, 16)
            sp.dma_start(g_bc[:, :], io["hgrn_norm_g"].partition_broadcast(P)).then_inc(s_gb, 16)
            with sp.Fori(0, NT) as i:
                rows = bass.ds(i * P, P)
                sp.wait_ge(s_turn, i)
                sp.dma_start(qf[:, :], scr["proj"][rows, C_HQ:C_HI]).then_inc(s_qf, 16)
                sp.wait_ge(s_o, i * NB4)
                sp.dma_start(v[:, :], scr["proj"][rows, C_HI:C_HG]).then_inc(s_v, 16)
                sp.wait_ge(s_res, i)
                sp.dma_start(hg[:, :], scr["proj"][rows, C_HG:C_GA]).then_inc(s_hg, 16)
                sp.wait_ge(s_res, i + 1)
                sp.dma_start(scr["hgr"][rows, :], res[:, :]).then_inc(s_out, 16)
            sp.wait_ge(s_out, 16 * NT)

        @block.gpsimd
        def _(pool):
            pool.memset(ones[:, :], 1.0).then_inc(s_cst, 1)
            pool.memset(cmask[:, :, :], 0.0).then_inc(s_cst, 1)
            pool.memset(state[:, 0, :], 0.0).then_inc(s_st0, 1)
            pool.wait_ge(s_cst, 2)
            pool.memset(blocks(ones[:, :])[:, :, 0:1], 0.0).then_inc(s_cst, 1)
            for j in range(NB4):
                pool.wait_ge(s_cst, 3 + j)
                pool.affine_select(out=cmask[BL * j:BL * (j + 1), :, :], in_=cmask[BL * j:BL * (j + 1), :, :],
                                   compare_op=ALU.is_gt, fill=1.0, base=0, pattern=[[0, HG_HEADS], [-1, BL]],
                                   channel_multiplier=1).then_inc(s_cst, 1)

        @block.vector
        def _(dve):
            ch = Chain(dve, s_dv)
            a0, a1 = lbt[:, 0, :], lbt[:, 1, :]
            dve.wait_ge(s_lbt, 1)
            ch.link(dve.tensor_copy(lbt[:, 0:2, :], ps_q[:, 0:2 * HG_HEADS].rearrange("p (r h) -> p r h", r=2)))
            ch.link(dve.tensor_tensor(lbt[:, 2, :], a0, a1, ALU.max))
            dve.tensor_tensor(lbt[:, 3, :], a0, lbt[:, 2, :], ALU.subtract)
            dve.tensor_tensor(lbt[:, 4, :], a1, lbt[:, 2, :], ALU.subtract).then_inc(s_lbm, 1)
            dve.wait_ge(s_lbe, 1)
            ch.link(dve.tensor_tensor(lbt[:, 6, :], lbt[:, 3, :], lbt[:, 4, :], ALU.add))
            ch.link(dve.reciprocal(lbt[:, 7, :], lbt[:, 6, :]))
            ch.link(dve.tensor_tensor(lbt[:, 0, :], lbt[:, 3, :], lbt[:, 7, :], ALU.mult))
            ch.link(dve.tensor_scalar(lbt[:, 1, :], lbt[:, 0, :], -1.0, 1.0, ALU.mult, ALU.add))
            before = ch.n
            PER = 15
            dve.wait_ge(s_gb, 16)
            dve.wait_ge(s_cst, 3 + NB4)
            with dve.Fori(0, NT) as i:
                ch = Chain(dve, s_dv, base=i * PER + before)
                dve.wait_ge(s_eg, i + 1)
                ch.link(dve.tensor_scalar(sg[:, :], sg[:, :], 1.0, None, ALU.add))
                ch.link(dve.reciprocal(sg[:, :], sg[:, :]))
                for h in range(HG_HEADS):
                    c = slice(h * P, (h + 1) * P)
                    last = dve.tensor_scalar(f[:, c], sg[:, c], lbt[:, 1, h:h + 1], lbt[:, 0, h:h + 1],
                                             ALU.mult, ALU.add)
                last.then_inc(s_f, 1)
                dve.wait_ge(s_f, i + 1)
                dve.tensor_scalar(kk[:, :], f[:, :], -1.0, 1.0, ALU.mult, ALU.add)
                dve.wait_ge(s_lf, i + 1)
                ch.link(dve.tensor_tensor_scan(b[:, :], ones[:, :], lf[:, :], 0.0, ALU.mult, ALU.add))
                bb = blocks(b[:, :])
                wide = [P, HG_HEADS * NB4, BL]
                dve.tensor_tensor(blocks(bm[:, :]), bb, bb[:, :, BL // 2 - 1:BL // 2].to_broadcast(wide), ALU.subtract)
                dve.tensor_tensor(blocks(bl[:, :]), bb[:, :, BL - 1:BL].to_broadcast(wide), bb,
                                  ALU.subtract).then_inc(s_b, 1)
                dve.wait_ge(s_e, i + 1)
                dve.scalar_tensor_tensor(out=qe[:, :], in0=ps_q[:, :], scalar=float(HG_D) ** -0.5, in1=e[:, 0, :],
                                         op0=ALU.mult, op1=ALU.mult)
                dve.scalar_tensor_tensor(out=qs[:, :], in0=ps_q[:, :], scalar=float(HG_D) ** -0.5, in1=e[:, 2, :],
                                         op0=ALU.mult, op1=ALU.mult)
                dve.tensor_tensor(ke[:, :], kk[:, :], e[:, 1, :], ALU.mult)
                dve.tensor_tensor(ks[:, :], kk[:, :], e[:, 3, :], ALU.mult).then_inc(s_qk, 1)
                dve.wait_ge(s_a, i + 1)
                ch.link(dve.tensor_scalar(at[:, :, :], ps_f[:, 0:HG_HEADS * BL].rearrange("p (h t) -> p h t", t=BL),
                                          -BIG, BIG, ALU.max, ALU.min))
                dve.tensor_tensor(at[:, :, :], at[:, :, :], cmask[:, :, :], ALU.mult).then_inc(s_at, 1)
                for j in range(NB4):
                    dve.wait_ge(s_ps, i * NB4 + (j + 1))
                    if j == 0:
                        dve.wait_ge(s_st0, 1)
                    if j == NB4 - 1:
                        dve.wait_ge(s_o, i * NB4 + 1)
                    for h in range(HG_HEADS):
                        c = slice(h * P, (h + 1) * P)
                        last = dve.scalar_tensor_tensor(out=state[:, (j + 1) % NB4, c], in0=state[:, j, c],
                                                        scalar=dec[:, h, j:j + 1], in1=ps_s[j][:, c],
                                                        op0=ALU.mult, op1=ALU.add)
                    last.then_inc(s_s, 1)
                    dve.wait_ge(s_s, i * NB4 + (j + 1))
                dve.wait_ge(s_sl, i + 1)
                ch.link(dve.tensor_scalar(sl[:, 0, :], sl[:, 0, :], 1.0, None, ALU.add))
                ch.link(dve.reciprocal(sl[:, 0, :], sl[:, 0, :]))
                ch.link(dve.tensor_tensor(sl[:, 1, :], hg[:, :], sl[:, 0, :], ALU.mult))
                ch.link(dve.tensor_tensor(sl[:, 1, :], sl[:, 1, :], g_bc[:, :], ALU.mult))
                dve.wait_ge(s_sq, i + 1)
                dve.tensor_scalar(st4[:, 1, :], st4[:, 0, :], 1.0 / HG_D, EPS, ALU.mult, ALU.add).then_inc(s_var, 1)
                dve.wait_ge(s_rs, i + 1)
                ch.link(dve.tensor_tensor(on[:, :].rearrange("p (h d) -> p h d", h=HG_HEADS),
                                          ps_o[:, :].rearrange("p (h d) -> p h d", h=HG_HEADS),
                                          st4[:, 3, :].unsqueeze(2).to_broadcast([P, HG_HEADS, P]), ALU.mult))
                dve.wait_ge(s_out, i * 16)
                dve.tensor_tensor(res[:, :], on[:, :], sl[:, 1, :], ALU.mult).then_inc(s_res, 1)
                for _ in range(PER - ch.n):
                    ch.link(dve.tensor_copy(lbt[:, 5, 0:1], lbt[:, 1, 0:1]))

        @block.scalar
        def _(act):
            act.wait_ge(s_lbm, 1)
            act.activation(lbt[:, 3:5, :], lbt[:, 3:5, :], ACT.Exp).then_inc(s_lbe, 1)
            with act.Fori(0, NT) as i:
                act.wait_ge(s_turn, i + 1)
                act.activation(sg[:, :], ps_f[:, :], ACT.Exp, scale=-1.0).then_inc(s_eg, 1)
                act.wait_ge(s_f, i + 1)
                act.activation(lf[:, :], f[:, :], ACT.Ln).then_inc(s_lf, 1)
                act.wait_ge(s_b, i + 1)
                act.activation(e[:, 0, :], bm[:, :], ACT.Exp)
                act.activation(e[:, 1, :], bm[:, :], ACT.Exp, scale=-1.0)
                act.activation(e[:, 2, :], b[:, :], ACT.Exp)
                act.activation(e[:, 3, :], bl[:, :], ACT.Exp)
                act.wait_ge(s_s, i * NB4)
                act.activation(dec[:, :, :], b[:, :].rearrange("p (h j t) -> p h j t", h=HG_HEADS, t=BL)[:, :, :, BL - 1],
                               ACT.Exp).then_inc(s_e, 1)
                act.wait_ge(s_kt, i + 1)
                act.copy(kst[:, :], ps_k[:, :]).then_inc(s_kst, 1)
                act.wait_ge(s_hg, 16 * i + 16)
                act.wait_ge(s_res, i)
                act.activation(sl[:, 0, :], hg[:, :], ACT.Exp, scale=-1.0).then_inc(s_sl, 1)
                act.wait_ge(s_o, i * NB4 + NB4)
                for h in range(HG_HEADS):
                    last = act.activation(sq[:, h, :], ps_o[:, h * P:(h + 1) * P], ACT.Square,
                                          accum_out=st4[:, 0, h:h + 1])
                last.then_inc(s_sq, 1)
                act.wait_ge(s_var, i + 1)
                act.activation(st4[:, 2, :], st4[:, 1, :], ACT.Ln).then_inc(s_ac, 1)
                act.wait_ge(s_ac, i + 1)
                act.activation(st4[:, 3, :], st4[:, 2, :], ACT.Exp, scale=-0.5).then_inc(s_rs, 1)

        @block.tensor
        def _(pe):
            pe.wait_ge(s_lb, 16)
            pe.transpose(ps_q[:, 0:2 * HG_HEADS], lb_rows[:, :], ident[0:2 * HG_HEADS, 0:2 * HG_HEADS]).then_inc(s_lbt, 1)
            pe.wait_ge(s_lbe, 1)
            with pe.Fori(0, NT) as i:
                pe.wait_ge(s_qf, 16 * i + 16)
                pe.wait_ge(s_qk, i)
                pe.wait_ge(s_at, i)
                for h in range(HG_HEADS):
                    c = slice(h * P, (h + 1) * P)
                    pe.transpose(ps_q[:, c], qf[:, c], ident[:, :])
                    last = pe.transpose(ps_f[:, c], qf[:, HGW + h * P:HGW + (h + 1) * P], ident[:, :])
                last.then_inc(s_turn, 1)
                pe.wait_ge(s_qk, i + 1)
                for h in range(HG_HEADS):
                    c = slice(h * P, (h + 1) * P)
                    last = pe.transpose(ps_k[:, c], ks[:, c], ident[:, :])
                last.then_inc(s_kt, 1)
                for j in range(NB4):
                    for h in range(HG_HEADS):
                        c = slice(h * P + j * BL, h * P + (j + 1) * BL)
                        last = pe.matmul(ps_f[BL * j:BL * (j + 1), h * BL:(h + 1) * BL], ke[:, c], qe[:, c],
                                         start=True, stop=True)
                last.then_inc(s_a, 1)
                pe.wait_ge(s_v, 16 * i + 16)
                pe.wait_ge(s_kst, i + 1)
                for j in range(NB4):
                    r = slice(BL * j, BL * (j + 1))
                    for h in range(HG_HEADS):
                        c = slice(h * P, (h + 1) * P)
                        last = pe.matmul(ps_s[j][:, c], kst[r, c], v[r, c], start=True, stop=True)
                    last.then_inc(s_ps, 1)
                pe.wait_ge(s_at, i + 1)
                pe.wait_ge(s_res, i)
                for j in range(NB4):
                    r = slice(BL * j, BL * (j + 1))
                    pe.wait_ge(s_s, i * NB4 + j) if j else pe.wait_ge(s_st0, 1)
                    for h in range(HG_HEADS):
                        c = slice(h * P, (h + 1) * P)
                        pe.matmul(ps_o[r, c], qs[:, h * P + j * BL:h * P + (j + 1) * BL], state[:, j, c],
                                  start=True, stop=False)
                        last = pe.matmul(ps_o[r, c], at[r, h, :], v[r, c], start=False, stop=True)
                    last.then_inc(s_o, 1)




def stage_merge(nc, io, scr, ident):
    with ExitStack() as ctx:
        def sb(name, shape, dt=F32):
            return ctx.enter_context(nc.sbuf_tensor(name, shape, dt))

        def banks(name, n):
            return ctx.enter_context(nc.psum_tensor(name, [P, n, 512], F32))

        def sem(name):
            return ctx.enter_context(nc.semaphore(name))

        KH = HGW // P
        wa = sb("m_wa", [P, KH, D])
        wh = sb("m_wh", [P, KH, D])
        wo = sb("m_wo", [P, KT, D])
        wr = sb("m_wr", [P, KT, N_EXP])
        rb = sb("m_rb", [P, N_EXP])
        g_bc = sb("m_g_bc", [P, D])
        br = sb("m_br", [P, 2, HGW])
        brT = sb("m_brT", [P, 2, KH, P])
        gate = sb("m_gate", [P, 2, D])
        eg = sb("m_eg", [P, 2, D])
        mixa = sb("m_mixa", [P, D])
        mix = sb("m_mix", [P, D])
        mixT = sb("m_mixT", [P, KT, P])
        hin = sb("m_hin", [P, D])
        h2 = sb("m_h2", [P, D])
        sq = sb("m_sq", [P, D])
        st = sb("m_st", [P, 4])
        xn = sb("m_xn", [P, D])
        xT = sb("m_xT", [P, KT, P])
        lgt = sb("m_lgt", [P, 2, N_EXP])
        ps_b = banks("m_ps_b", 1)
        ps_u = banks("m_ps_u", 4)
        ps_t = banks("m_ps_t", 1)
        ps_o = banks("m_ps_o", 2)

        s_w = sem("m_weights_landed")
        s_br = sem("m_branches_landed")
        s_gate = sem("m_gates_landed")
        s_h = sem("m_h_landed")
        s_bt = sem("m_branches_turned")
        s_bte = sem("m_branches_taken")
        s_u = sem("m_branch_products_ready")
        s_eg = sem("m_exp_gates_ready")
        s_dv = sem("m_dve_chain")
        s_mix = sem("m_mix_ready")
        s_mt = sem("m_mix_turned")
        s_mte = sem("m_mix_taken")
        s_o = sem("m_out_product_ready")
        s_h2 = sem("m_h2_ready")
        s_h2s = sem("m_h2_stored")
        s_ssq = sem("m_squares_ready")
        s_var = sem("m_variance_ready")
        s_ac = sem("m_act_chain")
        s_rs = sem("m_rstd_ready")
        s_xn = sem("m_xn_ready")
        s_xns = sem("m_xn_stored")
        s_xt = sem("m_xn_turned")
        s_xte = sem("m_xn_taken")
        s_lg = sem("m_logits_ready")
        s_lgb = sem("m_logits_biased")
        s_lgs = sem("m_logits_stored")

        def skewed(eng, stages):
            for i in (0, 1):
                for d, f in enumerate(stages):
                    if 0 <= i - d:
                        f(i - d)
            with eng.Fori(2, NT) as i:
                for d, f in enumerate(stages):
                    f(i - d)
            for i in (NT, NT + 1):
                for d, f in enumerate(stages):
                    if i - d < NT:
                        f(i - d)

        def rows(i):
            return bass.ds(i * P, P)

        block = ctx.enter_context(nc.Block())

        @block.sync
        def _(sp):
            sp.dma_start(g_bc[:, :], io["ffn_norm_g"].partition_broadcast(P)).then_inc(s_w, 16)
            sp.dma_start(rb[:, :], io["router_b"].partition_broadcast(P)).then_inc(s_w, 16)
            sp.dma_start(wa[:, :, :], io["w_up_attn"][0].rearrange("(k p) n -> p k n", p=P)).then_inc(s_w, 16)
            sp.dma_start(wh[:, :, :], io["w_up_hgrn"][0].rearrange("(k p) n -> p k n", p=P)).then_inc(s_w, 16)
            sp.dma_start(wo[:, :, :], io["w_out"][0].rearrange("(k p) n -> p k n", p=P)).then_inc(s_w, 16)
            sp.dma_start(wr[:, :, :], io["router_w"][0].rearrange("(k p) n -> p k n", p=P)).then_inc(s_w, 16)

            def load(i):
                sp.wait_ge(s_bt, 2 * i)
                sp.dma_start(br[:, 0, :], scr["att"][rows(i), :]).then_inc(s_br, 16)
                sp.dma_start(br[:, 1, :], scr["hgr"][rows(i), :]).then_inc(s_br, 16)
                sp.wait_ge(s_eg, i)
                sp.dma_start(gate[:, :, :], scr["proj"][rows(i), C_GA:IN_COLS].rearrange("p (g c) -> p g c", g=2)
                             ).then_inc(s_gate, 16)

            def residual(i):
                sp.wait_ge(s_h2, i)
                sp.dma_start(hin[:, :], scr["h"][rows(i), :]).then_inc(s_h, 16)
                sp.wait_ge(s_h2, i + 1)
                sp.dma_start(scr["h2"][rows(i), :], h2[:, :]).then_inc(s_h2s, 16)

            def store(i):
                sp.wait_ge(s_xn, i + 1)
                sp.dma_start(scr["xn"][rows(i), :], xn[:, :]).then_inc(s_xns, 16)
                sp.wait_ge(s_lgb, i + 1)
                sp.dma_start(scr["logits"][rows(i), :], lgt[:, 0, :]).then_inc(s_lgs, 16)

            skewed(sp, (load, residual, store))
            sp.wait_ge(s_h2s, 16 * NT)
            sp.wait_ge(s_xns, 16 * NT)
            sp.wait_ge(s_lgs, 16 * NT)

        @block.tensor
        def _(pe):
            def branches(i):
                for j in range(2):
                    pe.wait_ge(s_br, 32 * i + 32)
                    pe.wait_ge(s_bte, 2 * i + j)
                    for k in range(KH):
                        last = pe.transpose(ps_b[:, 0, k * P:(k + 1) * P], br[:, j, k * P:(k + 1) * P], ident[:, :])
                    last.then_inc(s_bt, 1)
                pe.wait_ge(s_mix, i)
                for j, w in ((0, wa), (1, wh)):
                    pe.wait_ge(s_bte, 2 * i + (j + 1))
                    for n in range(2):
                        for k in range(KH):
                            last = pe.matmul(ps_u[:, 2 * j + n, :], brT[:, j, k, :], w[:, k, n * 512:(n + 1) * 512],
                                             start=(k == 0), stop=(k == KH - 1))
                last.then_inc(s_u, 1)

            def project(i):
                pe.wait_ge(s_mix, i + 1)
                for n in range(2):
                    pe.wait_ge(s_mte, 2 * i + n)
                    for k in range(4):
                        c = (4 * n + k) * P
                        last = pe.transpose(ps_t[:, 0, k * P:(k + 1) * P], mix[:, c:c + P], ident[:, :])
                    last.then_inc(s_mt, 1)
                pe.wait_ge(s_h2, i)
                pe.wait_ge(s_mte, 2 * i + 2)
                for n in range(2):
                    for k in range(KT):
                        last = pe.matmul(ps_o[:, n, :], mixT[:, k, :], wo[:, k, n * 512:(n + 1) * 512],
                                         start=(k == 0), stop=(k == KT - 1))
                last.then_inc(s_o, 1)

            def route(i):
                pe.wait_ge(s_xn, i + 1)
                for n in range(2):
                    pe.wait_ge(s_xte, 2 * i + n)
                    for k in range(4):
                        c = (4 * n + k) * P
                        last = pe.transpose(ps_t[:, 0, k * P:(k + 1) * P], xn[:, c:c + P], ident[:, :])
                    last.then_inc(s_xt, 1)
                pe.wait_ge(s_xte, 2 * i + 2)
                for k in range(KT):
                    last = pe.matmul(ps_t[:, 0, 0:N_EXP], xT[:, k, :], wr[:, k, :], start=(k == 0), stop=(k == KT - 1))
                last.then_inc(s_lg, 1)
                pe.wait_ge(s_lgb, i + 1)

            pe.wait_ge(s_w, 16 * 6)
            skewed(pe, (branches, project, route))

        @block.scalar
        def _(act):
            def branches(i):
                act.wait_ge(s_gate, 16 * i + 16)
                act.wait_ge(s_mix, i)
                act.activation(eg[:, :, :], gate[:, :, :], ACT.Exp, scale=-1.0).then_inc(s_eg, 1)
                for j in range(2):
                    act.wait_ge(s_bt, 2 * i + (j + 1))
                    act.wait_ge(s_u, i)
                    act.copy(brT[:, j, :, :], ps_b[:, 0, :].rearrange("p (k t) -> p k t", t=P)).then_inc(s_bte, 1)

            def project(i):
                for n in range(2):
                    act.wait_ge(s_mt, 2 * i + (n + 1))
                    act.wait_ge(s_o, i)
                    act.copy(mixT[:, 4 * n:4 * n + 4, :],
                             ps_t[:, 0, :].rearrange("p (k t) -> p k t", t=P)).then_inc(s_mte, 1)
                act.wait_ge(s_h2, i + 1)
                act.wait_ge(s_ssq, i)
                act.activation(sq[:, :], h2[:, :], ACT.Square, accum_out=st[:, 0:1]).then_inc(s_ssq, 1)
                act.wait_ge(s_var, i + 1)
                act.activation(st[:, 2:3], st[:, 1:2], ACT.Ln).then_inc(s_ac, 1)
                act.wait_ge(s_ac, i + 1)
                act.activation(st[:, 3:4], st[:, 2:3], ACT.Exp, scale=-0.5).then_inc(s_rs, 1)

            def route(i):
                for n in range(2):
                    act.wait_ge(s_xt, 2 * i + (n + 1))
                    act.wait_ge(s_lg, i)
                    act.copy(xT[:, 4 * n:4 * n + 4, :],
                             ps_t[:, 0, :].rearrange("p (k t) -> p k t", t=P)).then_inc(s_xte, 1)

            skewed(act, (branches, project, route))

        @block.vector
        def _(dve):
            def merge(i):
                ch = Chain(dve, s_dv, base=4 * i)
                dve.wait_ge(s_eg, i + 1)
                ch.link(dve.tensor_scalar(eg[:, :, :], eg[:, :, :], 1.0, None, ALU.add))
                ch.link(dve.reciprocal(eg[:, :, :], eg[:, :, :]))
                dve.wait_ge(s_u, i + 1)
                dve.tensor_tensor(mixa[:, :], ps_u[:, 0:2, :].rearrange("p n c -> p (n c)"), eg[:, 0, :], ALU.mult)
                ch.link(dve.tensor_tensor(eg[:, 1, :], ps_u[:, 2:4, :].rearrange("p n c -> p (n c)"), eg[:, 1, :],
                                          ALU.mult))
                dve.wait_ge(s_mt, 2 * i)
                ch.link(dve.tensor_tensor(mix[:, :], mixa[:, :], eg[:, 1, :], ALU.add))
                dve.sem_inc(s_mix, 1)

            def residual(i):
                dve.wait_ge(s_o, i + 1)
                dve.wait_ge(s_h, 16 * i + 16)
                dve.wait_ge(s_h2s, 16 * i)
                dve.wait_ge(s_ssq, i)
                dve.tensor_tensor(h2[:, :], hin[:, :], ps_o[:, :, :].rearrange("p n c -> p (n c)"),
                                  ALU.add).then_inc(s_h2, 1)
                dve.wait_ge(s_ssq, i + 1)
                dve.tensor_scalar(st[:, 1:2], st[:, 0:1], 1.0 / D, EPS, ALU.mult, ALU.add).then_inc(s_var, 1)
                dve.wait_ge(s_rs, i + 1)
                dve.wait_ge(s_xns, 16 * i)
                dve.wait_ge(s_xt, 2 * i)
                dve.scalar_tensor_tensor(out=xn[:, :], in0=h2[:, :], scalar=st[:, 3:4], in1=g_bc[:, :],
                                         op0=ALU.mult, op1=ALU.mult).then_inc(s_xn, 1)

            def bias(i):
                dve.wait_ge(s_lg, i + 1)
                dve.wait_ge(s_lgs, 16 * i)
                dve.tensor_tensor(lgt[:, 0, :], ps_t[:, 0, 0:N_EXP], rb[:, :], ALU.add).then_inc(s_lgb, 1)

            dve.wait_ge(s_w, 16 * 6)
            skewed(dve, (merge, residual, bias))




def stage_route(nc, io, scr, items, n_items):
    with ExitStack() as ctx:
        def sb(name, shape, dt=F32):
            return ctx.enter_context(nc.sbuf_tensor(name, shape, dt))

        def sem(name):
            return ctx.enter_context(nc.semaphore(name))

        lg = sb("r_lg", [P, NT, N_EXP])
        top = sb("r_top", [P, NT, 8])
        topi = sb("r_topi", [P, NT, 8], U32)
        topf = sb("r_topf", [P, NT, 8])
        gate = sb("r_gate", [P, NT, TOP])
        gsum = sb("r_gsum", [P, 2, NT])
        expert = sb("r_expert", [P, N_EXP])
        first = sb("r_first", [P, N_EXP])
        work = sb("r_work", [P, MORE])
        item_id = sb("r_item_id", [1, ITEMS])
        valid = sb("r_valid", [P, NT])
        pad = sb("r_pad", [P, TOP])
        before = sb("r_before", [P, P])
        ones = sb("r_ones", [P, P])
        pick = sb("r_pick", [P, TOP, NT, N_EXP])
        chosen = sb("r_chosen", [P, NT, N_EXP])
        prior = sb("r_prior", [P, NT + 1, N_EXP])
        slot = sb("r_slot", [P, NT, N_EXP])
        over = sb("r_over", [P, NT, N_EXP])
        more = sb("r_more", [P, 4, N_EXP])
        prod = sb("r_prod", [P, NT, N_EXP])
        slots = sb("r_slots", [P, NT, TOP])
        slots_i = sb("r_slots_i", [P, NT, TOP], U32)
        token = sb("r_token", [P, NT], I32)
        zero = sb("r_zero", [P, TABLE // P + 1], I32)
        cmp = sb("r_cmp", [1, MORE, N_EXP])
        rank = ctx.enter_context(nc.psum_tensor("r_rank", [P, 512], F32))
        count = ctx.enter_context(nc.psum_tensor("r_count", [P, 512], F32))

        s_lg = sem("r_logits_landed")
        s_pc = sem("r_pool_chain")
        s_dv = sem("r_dve_chain")
        s_sh = sem("r_gates_shifted")
        s_ge = sem("r_gates_exp")
        s_gate = sem("r_gates_ready")
        s_m = sem("r_chosen_ready")
        s_rank = sem("r_rank_ready")
        s_slot = sem("r_slots_ready")
        s_z = sem("r_table_zeroed")
        s_sc = sem("r_scattered")
        s_st = sem("r_stored")
        block = ctx.enter_context(nc.Block())

        @block.sync
        def _(sp):
            sp.dma_start(lg[:, :, :], scr["logits"].rearrange("(t p) e -> p t e", p=P)).then_inc(s_lg, 16)
            sp.wait_ge(s_gate, 1)
            sp.dma_start(scr["gate"].rearrange("(t p) c -> p t c", p=P), gate[:, :, :]).then_inc(s_st, 16)
            sp.wait_ge(s_slot, 1)
            sp.dma_start(scr["slot"].rearrange("(t p) c -> p t c", p=P), slots_i[:, :, :]).then_inc(s_st, 16)
            sp.wait_ge(s_st, 32)

        @block.gpsimd
        def _(pool):
            ch = Chain(pool, s_pc)
            n = TABLE // P
            ch.link(pool.memset(zero[:, :], 0))
            pool.dma_start(scr["token"][0:n * P, :].rearrange("(p n) o -> p (n o)", p=P), zero[:, 0:n]).then_inc(s_z, 16)
            ch.link(pool.iota(token[:, :], [[P, NT]], base=0, channel_multiplier=1))
            pool.iota(expert[:, :], [[1, N_EXP]], base=0, channel_multiplier=0, allow_small_or_imprecise_dtypes=True)
            pool.iota(first[:, :], [[ITEM, N_EXP]], base=0, channel_multiplier=0, allow_small_or_imprecise_dtypes=True)
            pool.iota(work[:, :], [[1, MORE]], base=0, channel_multiplier=0, allow_small_or_imprecise_dtypes=True)
            pool.iota(item_id[:, :], [[1, ITEMS]], base=0, channel_multiplier=0, allow_small_or_imprecise_dtypes=True)
            pool.iota(pad[:, :], [[P, TOP]], base=PAD, channel_multiplier=1, allow_small_or_imprecise_dtypes=True)
            pool.memset(ones[:, :], 1.0)
            pool.memset(valid[:, :], 1.0)
            ch.link(pool.memset(before[:, :], 1.0))
            pool.affine_select(out=before[:, :], in_=before[:, :], compare_op=ALU.is_gt, fill=0.0, base=0,
                               pattern=[[1, P]], channel_multiplier=-1)
            ch.link(pool.affine_select(out=valid[:, :], in_=valid[:, :], compare_op=ALU.is_ge, fill=0.0, base=L - 1,
                                       pattern=[[-P, NT]], channel_multiplier=-1))
            assert ch.n == POOL_SET
            pool.wait_ge(s_z, 16)
            pool.wait_ge(s_slot, 1)
            for t in range(NT):
                for c in range(TOP):
                    pool.indirect_dma_start(out=scr["token"],
                                            out_offset=bass.IndirectOffsetOnAxis(ap=slots_i[:, t, c:c + 1], axis=0),
                                            in_=token[:, t:t + 1], in_offset=None).then_inc(s_sc, 16)
            pool.wait_ge(s_sc, 16 * NT * TOP)

        @block.vector
        def _(dve):
            ch = Chain(dve, s_dv)
            all_t = [P, NT, N_EXP]
            dve.wait_ge(s_lg, 16)
            for t in range(NT):
                last = dve.max(top[:, t, :], lg[:, t, :])
            ch.link(last)
            for t in range(NT):
                last = dve.max_index(topi[:, t, :], top[:, t, :], lg[:, t, :])
            ch.link(last)
            ch.link(dve.tensor_copy(topf[:, :, :], topi[:, :, :]))
            dve.tensor_tensor(gate[:, :, :], top[:, :, 0:TOP], top[:, :, 0:1].to_broadcast([P, NT, TOP]),
                              ALU.subtract).then_inc(s_sh, 1)
            dve.wait_ge(s_ge, 1)
            ch.link(dve.tensor_reduce(gsum[:, 0, :], gate[:, :, :], AX.X, ALU.add))
            ch.link(dve.reciprocal(gsum[:, 1, :], gsum[:, 0, :]))
            dve.tensor_tensor(gate[:, :, :], gate[:, :, :], gsum[:, 1, :].unsqueeze(2).to_broadcast([P, NT, TOP]),
                              ALU.mult).then_inc(s_gate, 1)
            dve.wait_ge(s_pc, POOL_SET)
            for c in range(TOP):
                last = dve.tensor_tensor(pick[:, c, :, :], expert[:, :].unsqueeze(1).to_broadcast(all_t),
                                         topf[:, :, c:c + 1].to_broadcast(all_t), ALU.is_equal)
            ch.link(last)
            dve.tensor_tensor(chosen[:, :, :], pick[:, 0, :, :], pick[:, 1, :, :], ALU.add)
            ch.link(dve.tensor_tensor(prod[:, :, :], pick[:, 2, :, :], pick[:, 3, :, :], ALU.add))
            ch.link(dve.tensor_tensor(chosen[:, :, :], chosen[:, :, :], prod[:, :, :], ALU.add))
            ch.link(dve.tensor_tensor(chosen[:, :, :], chosen[:, :, :], valid[:, :].unsqueeze(2).to_broadcast(all_t),
                                      ALU.mult))
            ch.link(dve.memset(prior[:, 0, :], 0.0))
            for t in range(NT):
                ch.link(dve.tensor_tensor(prior[:, t + 1, :], prior[:, t, :], chosen[:, t, :], ALU.add))
            dve.sem_inc(s_m, 1)
            dve.wait_ge(s_rank, 1)
            cnt = more[:, 0, :]
            ch.link(dve.tensor_copy(cnt, count[:, 0:N_EXP]))
            ch.link(dve.memset(more[:, 1, :], 0.0))
            for c in range(1, -(-L // ITEM)):
                ch.link(dve.scalar_tensor_tensor(out=more[:, 1, :], in0=cnt, scalar=float(c * ITEM),
                                                 in1=more[:, 1, :], op0=ALU.is_gt, op1=ALU.add))
            ch.link(dve.tensor_tensor_scan(more[:, 2, :], ones[:, 0:N_EXP], more[:, 1, :], 0.0, ALU.mult, ALU.add))
            ch.link(dve.tensor_tensor(more[:, 3, :], more[:, 2, :], more[:, 1, :], ALU.subtract))
            ch.link(dve.tensor_scalar(more[:, 3, :], more[:, 3, :], float(ITEM), float(ITEM * (N_EXP - 1)),
                                      ALU.mult, ALU.add))
            ch.link(dve.tensor_tensor(more[:, 3, :], more[:, 3, :], first[:, :], ALU.subtract))
            r3 = rank[:, 0:NT * N_EXP].rearrange("p (t e) -> p t e", e=N_EXP)
            dve.tensor_tensor(slot[:, :, :], r3, first[:, :].unsqueeze(1).to_broadcast(all_t), ALU.add)
            ch.link(dve.tensor_scalar(over[:, :, :], r3, float(ITEM), None, ALU.is_ge))
            ch.link(dve.tensor_tensor(over[:, :, :], over[:, :, :], more[:, 3, :].unsqueeze(1).to_broadcast(all_t),
                                      ALU.mult))
            ch.link(dve.tensor_tensor(slot[:, :, :], slot[:, :, :], over[:, :, :], ALU.add))
            for c in range(TOP):
                ch.link(dve.tensor_tensor(prod[:, :, :], pick[:, c, :, :], slot[:, :, :], ALU.mult))
                ch.link(dve.tensor_reduce(slots[:, :, c], prod[:, :, :], AX.X, ALU.add))
            ch.link(dve.tensor_tensor(slots[:, :, :], slots[:, :, :], valid[:, :].unsqueeze(2).to_broadcast([P, NT, TOP]),
                                      ALU.mult))
            ch.link(dve.tensor_scalar(gsum[:, 0, :], valid[:, :], -1.0, 1.0, ALU.mult, ALU.add))
            ch.link(dve.tensor_tensor(prod[:, :, 0:TOP], pad[:, :].unsqueeze(1).to_broadcast([P, NT, TOP]),
                                      gsum[:, 0, :].unsqueeze(2).to_broadcast([P, NT, TOP]), ALU.mult))
            ch.link(dve.tensor_tensor(slots[:, :, :], slots[:, :, :], prod[:, :, 0:TOP], ALU.add))
            dve.tensor_copy(slots_i[:, :, :], slots[:, :, :]).then_inc(s_slot, 1)
            one = [1, MORE, N_EXP]
            ch.link(dve.tensor_tensor(cmp[:, :, :], more[0:1, 2, :].unsqueeze(1).to_broadcast(one),
                                      work[0:1, :].unsqueeze(2).to_broadcast(one), ALU.is_le))
            ch.link(dve.tensor_reduce(item_id[:, N_EXP:ITEMS], cmp[:, :, :], AX.X, ALU.add))
            ch.link(dve.tensor_scalar(item_id[:, N_EXP:ITEMS], item_id[:, N_EXP:ITEMS], float(N_EXP - 1), None, ALU.min))
            ch.link(dve.tensor_copy(items[:, :], item_id[:, :]))
            ch.link(dve.tensor_scalar(n_items[:, :], more[0:1, 2, N_EXP - 1:N_EXP], float(N_EXP), None, ALU.add))

        @block.scalar
        def _(act):
            act.wait_ge(s_sh, 1)
            act.activation(gate[:, :, :], gate[:, :, :], ACT.Exp).then_inc(s_ge, 1)

        @block.tensor
        def _(pe):
            pe.wait_ge(s_m, 1)
            w = NT * N_EXP
            pe.matmul(rank[:, 0:w], before[:, :], chosen[:, :, :].rearrange("p t e -> p (t e)"), start=True, stop=False)
            pe.matmul(rank[:, 0:w], ones[:, :], prior[:, 0:NT, :].rearrange("p t e -> p (t e)"), start=False, stop=True)
            pe.matmul(count[:, 0:N_EXP], ones[:, :], prior[:, NT, :], start=True, stop=True).then_inc(s_rank, 1)


POOL_SET = 4


D_FF = 1024
FT = D_FF // P
LIMIT, ALPHA = 7.0, 1.702


def stage_experts(nc, io, scr, ident, items, n_items):
    with ExitStack() as ctx:
        def sb(name, shape, dt=F32):
            return ctx.enter_context(nc.sbuf_tensor(name, shape, dt))

        def sem(name):
            return ctx.enter_context(nc.semaphore(name))

        w = {m: sb(f"e_w_{m}", [P, KT, D_FF]) for m in ("gate", "up", "down")}
        bT = sb("e_bT", [P, 3, FT, N_EXP])
        be = sb("e_be", [P, 3, FT])
        idx = sb("e_idx", [HALF, 2], U32)
        xg = sb("e_xg", [HALF, 2, D])
        xT = sb("e_xT", [P, KT, ITEM])
        g = sb("e_g", [P, FT, ITEM])
        sg = sb("e_sg", [P, FT, ITEM])
        u = sb("e_u", [P, 2, ITEM])
        a = sb("e_a", [P, FT, ITEM])
        yT = sb("e_yT", [P, KT, ITEM])
        yr = sb("e_yr", [HALF, 2, D])
        ACC, TR = 4, 4
        acc = [ctx.enter_context(nc.psum_tensor(f"e_acc{b}", [P, 512], F32)) for b in range(ACC)]
        tr = [ctx.enter_context(nc.psum_tensor(f"e_tr{b}", [P, 512], F32)) for b in range(TR)]

        s_w = {m: sem(f"e_{m}_landed") for m in w}
        s_b = sem("e_biases_landed")
        s_bt = sem("e_biases_turned")
        s_bte = sem("e_biases_taken")
        s_be = sem("e_bias_ready")
        s_idx = sem("e_indices_landed")
        s_x = sem("e_rows_gathered")
        s_go = sem("e_gathers_started")
        s_xt = sem("e_rows_turned")
        s_xte = sem("e_rows_taken")
        s_gm = sem("e_gate_products")
        s_ge = sem("e_gate_taken")
        s_um = sem("e_up_products")
        s_ue = sem("e_up_taken")
        s_dm = sem("e_down_products")
        s_de = sem("e_down_taken")
        s_sg = sem("e_sigmoid_ready")
        s_gs = sem("e_gated_ready")
        s_dv = sem("e_dve_chain")
        s_a = sem("e_act_ready")
        s_yt = sem("e_y_turned")
        s_yte = sem("e_y_taken")
        s_y = sem("e_y_stored")

        block = ctx.enter_context(nc.Block())
        bias_rows = xg[0:N_EXP, :, :]

        def count_of(eng):
            return eng.value_load(n_items[0:1, 0:1], min_val=N_EXP, max_val=ITEMS)

        def expert_of(eng, i):
            return eng.value_load(items[0:1, bass.ds(i, 1)], min_val=0, max_val=N_EXP - 1)

        @block.sync
        def _(sp):
            sp.dma_start(bias_rows[:, 0, :], io["b_gate"][0]).then_inc(s_b, 16)
            sp.dma_start(bias_rows[:, 1, :], io["b_up"][0]).then_inc(s_b, 16)
            sp.dma_start(yr[0:N_EXP, 0, :], io["b_down"][0]).then_inc(s_b, 16)
            n = count_of(sp)
            with sp.Fori(0, n) as i:
                e = expert_of(sp, i)
                for m, used in (("gate", s_gm), ("up", s_um), ("down", s_dm)):
                    sp.wait_ge(used, i * FT)
                    src = io[f"w_{m}"][0][bass.ds(e, 1), :, :].rearrange("o (k p) f -> p (o k) f", p=P)
                    sp.dma_start(w[m][:, :, :], src).then_inc(s_w[m], 16)

        @block.gpsimd
        def _(pool):
            n = count_of(pool)

            def gather(i):
                pool.dma_start(idx[:, :].bitcast(I32),
                               scr["token"][bass.ds(i * ITEM, ITEM), :].rearrange("(a p) o -> p (a o)", a=2),
                               allow_slow_non_contiguous=True).then_inc(s_idx, 16)
                pool.wait_ge(s_idx, i * 16 + 16)
                pool.sem_inc(s_go, 1)
                for a_ in range(2):
                    pool.indirect_dma_start(out=xg[:, a_, :], out_offset=None, in_=scr["xn"],
                                            in_offset=bass.IndirectOffsetOnAxis(ap=idx[:, a_:a_ + 1], axis=0)
                                            ).then_inc(s_x, 16)

            pool.wait_ge(s_bt, 3)
            gather(0)
            with pool.Fori(0, n) as i:
                pool.wait_ge(s_xt, i * 4 + 4)
                gather(i + 1)
                pool.wait_ge(s_yte, i * 4 + 4)
                pool.dma_start(scr["y"][bass.ds(i * ITEM, ITEM), :].rearrange("(a p) d -> p a d", a=2),
                               yr[:, :, :]).then_inc(s_y, 16)
            pool.wait_ge(s_y, n * 16)
            pool.wait_ge(s_x, n * 32 + 32)

        @block.tensor
        def _(pe):
            n = count_of(pe)
            pe.wait_ge(s_b, 48)
            for j, src in enumerate((bias_rows[:, 0, :], bias_rows[:, 1, :], yr[0:N_EXP, 0, :])):
                for f in range(FT):
                    last = pe.transpose(tr[j][:, f * N_EXP:(f + 1) * N_EXP], src[:, f * P:(f + 1) * P],
                                        ident[0:N_EXP, 0:N_EXP])
                last.then_inc(s_bt, 1)
            pe.wait_ge(s_bte, 3)

            def turn(i):
                pe.wait_ge(s_x, i * 32 + 32)
                for q in range(4):
                    for k in range(2):
                        for a_ in range(2):
                            c = k * ITEM + a_ * HALF
                            last = pe.transpose(tr[q][:, c:c + HALF], xg[:, a_, (2 * q + k) * P:(2 * q + k + 1) * P],
                                                ident[0:HALF, 0:HALF])
                    last.then_inc(s_xt, 1)

            turn(0)
            with pe.Fori(0, n) as i:
                pe.wait_ge(s_xte, i * 4 + 4)
                pe.wait_ge(s_w["gate"], i * 16 + 16)
                for f in range(FT):
                    pe.wait_ge(s_ge, i * FT + (f + 1 - ACC)) if f >= ACC else pe.wait_ge(s_de, i * FT)
                    for k in range(KT):
                        last = pe.matmul(acc[f % ACC][:, 0:ITEM], w["gate"][:, k, f * P:(f + 1) * P], xT[:, k, :],
                                         start=(k == 0), stop=(k == KT - 1))
                    last.then_inc(s_gm, 1)
                pe.wait_ge(s_w["up"], i * 16 + 16)
                for f in range(FT):
                    pe.wait_ge(s_ge, i * FT + (f + 1 + FT - ACC)) if f < ACC else pe.wait_ge(s_ue, i * FT + (f + 1 - ACC))
                    for k in range(KT):
                        last = pe.matmul(acc[f % ACC][:, 0:ITEM], w["up"][:, k, f * P:(f + 1) * P], xT[:, k, :],
                                         start=(k == 0), stop=(k == KT - 1))
                    last.then_inc(s_um, 1)
                pe.wait_ge(s_yte, i * 4)
                turn(i + 1)
                pe.wait_ge(s_w["down"], i * 16 + 16)
                pe.wait_ge(s_a, i * FT + FT)
                for f in range(KT):
                    pe.wait_ge(s_ue, i * FT + (f + 1 + FT - ACC)) if f < ACC else pe.wait_ge(s_de, i * FT + (f + 1 - ACC))
                    for k in range(FT):
                        last = pe.matmul(acc[f % ACC][:, 0:ITEM], w["down"][:, k, f * P:(f + 1) * P], a[:, k, :],
                                         start=(k == 0), stop=(k == FT - 1))
                    last.then_inc(s_dm, 1)
                for q in range(4):
                    a_, half = q // 2, q % 2
                    pe.wait_ge(s_de, i * FT + (4 * half + 4) if a_ == 0 else i * FT + FT)
                    pe.wait_ge(s_xte, i * 4 + (4 + q + 1))
                    for k in range(4):
                        last = pe.transpose(tr[q][0:HALF, k * P:(k + 1) * P],
                                            yT[:, 4 * half + k, a_ * HALF:(a_ + 1) * HALF], ident[:, :])
                    last.then_inc(s_yt, 1)

        @block.vector
        def _(dve):
            n = count_of(dve)
            for j in range(3):
                dve.wait_ge(s_bt, j + 1)
                dve.tensor_copy(bT[:, j, :, :], tr[j][:, 0:FT * N_EXP].rearrange("p (f e) -> p f e", e=N_EXP)
                                ).then_inc(s_bte, 1)
            dve.wait_ge(s_bte, 3)

            with dve.Fori(0, n) as i:
                e = expert_of(dve, i)
                dve.wait_ge(s_de, i * FT)
                dve.tensor_copy(be[:, :, :], bT[:, :, :, bass.ds(e, 1)].rearrange("p j f o -> p j (f o)")).then_inc(s_be, 1)
                dve.wait_ge(s_be, i + 1)
                dve.wait_ge(s_a, i * FT)
                for f in range(FT):
                    dve.wait_ge(s_gm, i * FT + (f + 1))
                    dve.tensor_scalar(g[:, f, :], acc[f % ACC][:, 0:ITEM], be[:, 0, f:f + 1], LIMIT,
                                      ALU.add, ALU.min).then_inc(s_ge, 1)
                dve.wait_ge(s_ge, i * FT + FT)
                dve.wait_ge(s_sg, i + 1)
                dve.tensor_tensor(g[:, :, :], g[:, :, :], sg[:, :, :], ALU.mult).then_inc(s_gs, 1)
                dve.wait_ge(s_gs, i + 1)
                for f in range(FT):
                    ch = Chain(dve, s_dv, base=i * FT + f)
                    dve.wait_ge(s_um, i * FT + (f + 1))
                    dve.tensor_scalar(u[:, 0, :], acc[f % ACC][:, 0:ITEM], be[:, 1, f:f + 1], LIMIT,
                                      ALU.add, ALU.min).then_inc(s_ue, 1)
                    dve.wait_ge(s_ue, i * FT + (f + 1))
                    ch.link(dve.tensor_scalar(u[:, 1, :], u[:, 0, :], -LIMIT, 1.0, ALU.max, ALU.add))
                    if f == 0:
                        dve.wait_ge(s_dm, i * FT)
                    dve.tensor_tensor(a[:, f, :], u[:, 1, :], g[:, f, :], ALU.mult).then_inc(s_a, 1)
                dve.wait_ge(s_y, i * 16)
                for q in range(4):
                    a_, half = q // 2, q % 2
                    dve.wait_ge(s_yt, i * 4 + (q + 1))
                    dve.tensor_copy(yr[:, a_, half * 512:(half + 1) * 512], tr[q][0:HALF, :]).then_inc(s_yte, 1)

        @block.scalar
        def _(act):
            n = count_of(act)

            def take_rows(i):
                for q in range(4):
                    act.wait_ge(s_xt, i * 4 + (q + 1))
                    if not isinstance(i, int):
                        act.wait_ge(s_um, i * FT)
                    act.copy(xT[:, 2 * q:2 * q + 2, :], tr[q][:, 0:2 * ITEM].rearrange("p (k t) -> p k t", k=2)
                             ).then_inc(s_xte, 1)

            take_rows(0)
            with act.Fori(0, n) as i:
                act.wait_ge(s_ge, i * FT + FT)
                act.wait_ge(s_gs, i)
                act.activation(sg[:, :, :], g[:, :, :], ACT.Sigmoid, scale=ALPHA).then_inc(s_sg, 1)
                take_rows(i + 1)
                for f in range(KT):
                    act.wait_ge(s_dm, i * FT + (f + 1))
                    act.wait_ge(s_yt, i * 4)
                    act.activation(yT[:, f, :], acc[f % ACC][:, 0:ITEM], ACT.Identity,
                                   bias=be[:, 2, f:f + 1]).then_inc(s_de, 1)


def stage_combine(nc, io, out, scr):
    OT = SEQ // P
    with ExitStack() as ctx:
        def sb(name, shape, dt=F32):
            return ctx.enter_context(nc.sbuf_tensor(name, shape, dt))

        def sem(name):
            return ctx.enter_context(nc.semaphore(name))

        g_bc = sb("c_g_bc", [P, D])
        slot = sb("c_slot", [P, OT, TOP], U32)
        gate = sb("c_gate", [P, OT, TOP])
        yg = sb("c_yg", [P, 2, TOP, D])
        hr = sb("c_hr", [P, 2, D])
        sq = sb("c_sq", [P, D])
        st = sb("c_st", [P, 2, 4])
        res = sb("c_res", [P, 2, D])
        s_in = sem("c_tables_landed")
        s_h = [sem(f"c_h_landed{b}") for b in range(2)]
        s_y = [sem(f"c_rows_gathered{b}") for b in range(2)]
        s_acc = sem("c_sum_chain")
        s_sum = sem("c_sum_ready")
        s_sq = sem("c_squares_ready")
        s_var = sem("c_variance_ready")
        s_ln = sem("c_log_ready")
        s_rs = sem("c_rstd_ready")
        s_res = sem("c_result_ready")
        s_out = [sem(f"c_result_stored{b}") for b in range(2)]
        block = ctx.enter_context(nc.Block())

        @block.sync
        def _(sp):
            sp.dma_start(g_bc[:, :], io["final_norm_g"].partition_broadcast(P)).then_inc(s_in, 16)
            sp.dma_start(slot[:, :, :], scr["slot"][N_META:L, :].rearrange("(t p) c -> p t c", p=P)).then_inc(s_in, 16)
            sp.dma_start(gate[:, :, :], scr["gate"][N_META:L, :].rearrange("(t p) c -> p t c", p=P)).then_inc(s_in, 16)
            sp.dma_start(hr[:, 0, :], scr["h2"][N_META:N_META + P, :]).then_inc(s_h[0], 16)
            for t in range(OT):
                if t + 1 < OT:
                    if t >= 1:
                        sp.wait_ge(s_res, t)
                    sp.dma_start(hr[:, (t + 1) % 2, :],
                                 scr["h2"][N_META + (t + 1) * P:N_META + (t + 2) * P, :]).then_inc(s_h[(t + 1) % 2], 16)
                sp.wait_ge(s_res, t + 1)
                sp.dma_start(out[0, t * P:(t + 1) * P, :], res[:, t % 2, :]).then_inc(s_out[t % 2], 16)
            for b in range(2):
                sp.wait_ge(s_out[b], 16 * OT // 2)

        @block.gpsimd
        def _(pool):
            pool.wait_ge(s_in, 48)
            for t in range(OT):
                if t >= 2:
                    pool.wait_ge(s_sum, t - 1)
                for c in range(TOP):
                    pool.indirect_dma_start(out=yg[:, t % 2, c, :], out_offset=None, in_=scr["y"],
                                            in_offset=bass.IndirectOffsetOnAxis(ap=slot[:, t, c:c + 1], axis=0)
                                            ).then_inc(s_y[t % 2], 16)

        @block.vector
        def _(dve):
            ch = Chain(dve, s_acc)
            dve.wait_ge(s_in, 48)
            for t in range(OT):
                b = t % 2
                dve.wait_ge(s_h[b], 16 * (t // 2 + 1))
                dve.wait_ge(s_y[b], 16 * TOP * (t // 2 + 1))
                for c in range(TOP):
                    ins = dve.scalar_tensor_tensor(out=hr[:, b, :], in0=yg[:, b, c, :], scalar=gate[:, t, c:c + 1],
                                                   in1=hr[:, b, :], op0=ALU.mult, op1=ALU.add)
                    if c < TOP - 1:
                        ch.link(ins)
                    else:
                        ins.then_inc(s_sum, 1)
                dve.wait_ge(s_sq, t + 1)
                dve.tensor_scalar(st[:, b, 1:2], st[:, b, 0:1], 1.0 / D, EPS, ALU.mult, ALU.add).then_inc(s_var, 1)
                dve.wait_ge(s_rs, t + 1)
                if t >= 2:
                    dve.wait_ge(s_out[b], 16 * (t // 2))
                dve.scalar_tensor_tensor(out=res[:, b, :], in0=hr[:, b, :], scalar=st[:, b, 3:4], in1=g_bc[:, :],
                                         op0=ALU.mult, op1=ALU.mult).then_inc(s_res, 1)

        @block.scalar
        def _(act):
            for t in range(OT):
                b = t % 2
                act.wait_ge(s_sum, t + 1)
                if t:
                    act.wait_ge(s_sq, t)
                act.activation(sq[:, :], hr[:, b, :], ACT.Square, accum_out=st[:, b, 0:1]).then_inc(s_sq, 1)
                act.wait_ge(s_var, t + 1)
                act.activation(st[:, b, 2:3], st[:, b, 1:2], ACT.Ln).then_inc(s_ln, 1)
                act.wait_ge(s_ln, t + 1)
                act.activation(st[:, b, 3:4], st[:, b, 2:3], ACT.Exp, scale=-0.5).then_inc(s_rs, 1)


def hybrid_layer(nc, io, out, scr):
    with ExitStack() as ctx:
        ident = ctx.enter_context(nc.sbuf_tensor("ident", [P, P], F32))
        items = ctx.enter_context(nc.sbuf_tensor("items", [1, ITEMS], I32))
        n_items = ctx.enter_context(nc.sbuf_tensor("n_items", [1, 1], I32))
        s_c = ctx.enter_context(nc.semaphore("constants"))
        with nc.Block() as block:
            @block.gpsimd
            def _(pool):
                pool.memset(ident[:, :], 0.0).then_inc(s_c, 1)
                pool.wait_ge(s_c, 1)
                pool.affine_select(out=ident[:, :], in_=ident[:, :], compare_op=ALU.not_equal, fill=1.0,
                                   base=0, pattern=[[-1, P]], channel_multiplier=1).then_inc(s_c, 1)
        stage_project(nc, io, scr, ident)
        stage_attention(nc, io, scr, ident)
        stage_hgrn(nc, io, scr, ident)
        stage_merge(nc, io, scr, ident)
        stage_route(nc, io, scr, items, n_items)
        stage_experts(nc, io, scr, ident, items, n_items)
        stage_combine(nc, io, out, scr)


SCRATCH = {
    "h": ((LP, D), F32), "proj": ((LP, IN_COLS), F32), "att": ((LP, ATT_HEADS * HD), F32), "hgr": ((LP, HGW), F32),
    "h2": ((LP, D), F32), "xn": ((LP, D), F32), "logits": ((LP, N_EXP), F32), "gate": ((LP, TOP), F32),
    "slot": ((LP, TOP), U32), "token": ((TABLE, 1), I32), "y": ((SLOTS, D), F32),
}


def build(nc, shapes):
    io = {n: nc.dram_tensor(f"in_{n}", s, F32, kind="ExternalInput").ap() for n, s in shapes.items()}
    out = nc.dram_tensor("out_0", (1, SEQ, D), F32, kind="ExternalOutput").ap()
    scr = {n: nc.dram_tensor(f"scratch_{n}", s, dt, kind="Internal").ap() for n, (s, dt) in SCRATCH.items()}
    hybrid_layer(nc, io, out, scr)


_INS = ["x", "meta_tokens", "attn_norm_g", "w_in", "hgrn_norm_g", "w_up_attn", "w_up_hgrn", "w_out",
        "hgrn_lb_logits", "ffn_norm_g", "router_w", "router_b", "w_gate", "b_gate", "w_up", "b_up",
        "w_down", "b_down", "final_norm_g"]


def extra_inputs(inputs):
    return {**inputs, "rope": rope_tables()}


def kernel(**inputs):
    import concourse.bacc as _bacc
    from concourse.bass_utils import run_bass_kernel_spmd as _run

    arrays = {n: np.ascontiguousarray(inputs[n]) for n in _INS}
    arrays["rope"] = rope_tables()
    nc = _bacc.Bacc("TRN2", target_bir_lowering=False, num_devices=1)
    build(nc, {n: a.shape for n, a in arrays.items()})
    r = _run(nc, [{f"in_{n}": a for n, a in arrays.items()}], core_ids=[0])
    return r.results[0]["out_0"]
```

```python
from contextlib import ExitStack

import numpy as np

import concourse.bass as bass
from concourse import mybir

F32 = mybir.dt.float32
I32 = mybir.dt.int32
U32 = mybir.dt.uint32
F16 = mybir.dt.float16
ALU = mybir.AluOpType
ACT = mybir.ActivationFunctionType
AX = mybir.AxisListType

P = 128
D = 1024
KT = D // P
SEQ, N_META = 1024, 16
L = SEQ + N_META
NT = -(-L // P)
LP = NT * P
TAIL = L - (NT - 1) * P
EPS = 1e-5

ATT_HEADS, KV_HEADS, HD = 8, 2, 64
IDX_HEADS, IDX_DIM = 8, 32
QK_HEADS = ATT_HEADS + KV_HEADS
C_Q = 0
C_K = C_Q + ATT_HEADS * HD
C_V = C_K + KV_HEADS * HD
C_IQ = C_V + KV_HEADS * HD
C_IK = C_IQ + IDX_HEADS * IDX_DIM
C_IW = C_IK + IDX_DIM
C_HQ = C_IW + IDX_HEADS
HG_HEADS, HG_D = 4, 128
HGW = HG_HEADS * HG_D
C_HF, C_HI, C_HG = C_HQ + HGW, C_HQ + 2 * HGW, C_HQ + 3 * HGW
C_GA = C_HG + HGW
C_GH = C_GA + D
IN_COLS = C_GH + D
CHUNKS = 4
CW = C_HQ // CHUNKS
FW = 512
FCHUNKS = (IN_COLS - C_HQ) // FW
assert CW * CHUNKS == C_HQ and FW * FCHUNKS == IN_COLS - C_HQ

IDX_SCALE = float(IDX_DIM ** -0.5) * float(IDX_HEADS ** -0.5)
ATT_SCALE = float(HD) ** -0.5
K_SEL = min(256, L // 4)
ROUNDS = K_SEL // 8
MASKED = -3.0e38
TAKEN = -3.3e38
SPLIT = -3.15e38
DROP = -1.0e30

ROT, IROT = HD // 4, IDX_DIM // 4
N_EXP = 32
TOP = 4
HALF = 80
ITEM = 2 * HALF
MORE = TOP * L // ITEM
ITEMS = N_EXP + MORE
SLOTS = ITEMS * ITEM
PAD = SLOTS + ITEM
TABLE = PAD + TOP * P
ZERO_P, ZERO_DMAS = 104, NT - 1
ZERO_N = MORE * ITEM // ZERO_P // ZERO_DMAS
assert ZERO_N * ZERO_P * ZERO_DMAS == MORE * ITEM
TAB = 2 * QK_HEADS * (ROT // 2) + 2 * (IDX_HEADS + 1) * (IROT // 2)


def rope_tables():
    pos = np.arange(LP, dtype=np.float32)
    parts = []
    for rot, heads in ((ROT, QK_HEADS), (IROT, IDX_HEADS + 1)):
        half = rot // 2
        inv = np.float32(500000.0) ** (-np.arange(half, dtype=np.float32) * np.float32(2.0) / np.float32(rot))
        ang = (pos[:, None] * inv[None, :].astype(np.float32)).astype(np.float32)
        for f in (np.cos, np.sin):
            parts.append(np.tile(f(ang).astype(np.float32), (1, heads)))
    return np.concatenate(parts, axis=1)


class Chain:

    def __init__(self, eng, sem, base=0):
        self.eng, self.sem, self.base, self.n = eng, sem, base, 0

    def link(self, ins):
        self.n += 1
        ins.then_inc(self.sem, 1)
        self.eng.wait_ge(self.sem, self.base + self.n)


def clear(nc, sems):
    with nc.Block() as block:
        @block.gpsimd
        def _(pool):
            for s in sems:
                pool.sem_clear(s)


def stage_project(nc, io, scr, ident, xnT):
    used = []
    with ExitStack() as ctx:
        def sb(name, shape, dt=F32):
            return ctx.enter_context(nc.sbuf_tensor(name, shape, dt))

        def sem(name):
            used.append(ctx.enter_context(nc.semaphore(name)))
            return used[-1]

        h_rows = sb("p_h_rows", [P, NT, D])
        g_bc = sb("p_g_bc", [P, D])
        ssq = sb("p_ssq", [P, NT])
        ms = sb("p_ms", [P, NT])
        rms = sb("p_rms", [P, NT])
        rstd = sb("p_rstd", [P, NT])
        xn = sb("p_xn", [P, 2, D])
        w = sb("p_w", [P, 2, KT, CW])
        NB = 6
        stage = sb("p_stage", [P, NB, CW])
        tp = ctx.enter_context(nc.psum_tensor("p_tp", [P, 2, 512], F32))
        acc = ctx.enter_context(nc.psum_tensor("p_acc", [P, NB, 512], F32))

        s_zero = sem("p_zeroed")
        s_h = sem("p_h_landed")
        s_g = sem("p_g_landed")
        s_hout = sem("p_h_stored")
        s_ssq = sem("p_ssq_ready")
        s_stat = sem("p_stat_chain")
        s_ms = sem("p_ms_ready")
        s_rms = sem("p_rms_ready")
        s_xn = sem("p_xn_ready")
        s_tp = sem("p_tp_ready")
        s_tpa = sem("p_tp_taken_act")
        s_tpv = sem("p_tp_taken_dve")
        s_w = [nc.alloc_semaphore(f"p_w_landed{b}") for b in range(2)]
        s_mm = sem("p_product_ready")
        s_eva = sem("p_evacuated_act")
        s_evv = sem("p_evacuated_dve")
        s_st = [sem(f"p_stored{b}") for b in range(NB)]

        w_in = io["w_in"][0].rearrange("(kt p) n -> p kt n", p=P)
        x = io["x"][0]
        block = ctx.enter_context(nc.Block())

        @block.sync
        def _(sp):
            sp.dma_start(g_bc[:, :], io["attn_norm_g"].partition_broadcast(P)).then_inc(s_g, 16)
            sp.dma_start(h_rows[0:N_META, 0, :], io["meta_tokens"]).then_inc(s_h, 16)
            sp.dma_start(h_rows[N_META:P, 0, :], x[0:P - N_META, :]).then_inc(s_h, 16)
            sp.dma_start(h_rows[:, 1:NT - 1, :],
                         x[P - N_META:SEQ - TAIL, :].rearrange("(t p) d -> p t d", p=P)).then_inc(s_h, 16)
            sp.wait_ge(s_zero, 1)
            sp.dma_start(h_rows[0:TAIL, NT - 1, :], x[SEQ - TAIL:SEQ, :]).then_inc(s_h, 16)
            sp.wait_ge(s_h, 64)
            sp.dma_start(scr["h"].rearrange("(t p) d -> p t d", p=P), h_rows[:, :, :]).then_inc(s_hout, 16)
            with sp.Fori(0, CHUNKS // 2) as c2:
                for u in range(2):
                    for t in range(NT):
                        n = u * NT + t
                        b = n % NB
                        if n % 2 == 0:
                            sp.wait_ge(s_eva, c2 * NT + (n // 2 + 1))
                        else:
                            sp.wait_ge(s_evv, c2 * NT + (n // 2 + 1))
                        sp.dma_start(scr["proj"][t * P:(t + 1) * P, bass.ds(c2 * (2 * CW) + u * CW, CW)],
                                     stage[:, b, :]).then_inc(s_st[b], 16)
            for b in range(NB):
                sp.wait_ge(s_st[b], 16 * (CHUNKS * NT // NB))
            sp.wait_ge(s_hout, 16)

        @block.gpsimd
        def _(pool):
            pool.dma_start(w[:, 0, :, :], w_in[:, :, 0:CW]).then_inc(s_w[0], 16)
            pool.dma_start(w[:, 1, :, :], w_in[:, :, CW:2 * CW]).then_inc(s_w[1], 16)
            with pool.Fori(1, CHUNKS // 2) as c2:
                for u in range(2):
                    pool.wait_ge(s_mm, (c2 - 1) * (2 * NT) + (u + 1) * NT)
                    pool.dma_start(w[:, u, :, :], w_in[:, :, bass.ds(c2 * (2 * CW) + u * CW, CW)]).then_inc(s_w[u], 16)

        @block.scalar
        def _(act):
            act.wait_ge(s_h, 64)
            for t in range(NT):
                if t >= 2:
                    act.wait_ge(s_ssq, t - 1)
                act.activation(xn[:, t % 2, :], h_rows[:, t, :], ACT.Square,
                               accum_out=ssq[:, t:t + 1]).then_inc(s_ssq, 1)
            act.wait_ge(s_ms, 1)
            act.activation(rms[:, :], ms[:, :], ACT.Sqrt).then_inc(s_rms, 1)
            for t in range(NT):
                act.wait_ge(s_tp, 2 * t + 1)
                act.copy(xnT[:, 0:4, t * P:(t + 1) * P],
                         tp[:, 0, :].rearrange("p (k t) -> p k t", k=4)).then_inc(s_tpa, 1)
            with act.Fori(0, CHUNKS // 2) as c2:
                for n in range(0, 2 * NT, 2):
                    b = n % NB
                    act.wait_ge(s_mm, c2 * (2 * NT) + (n + 1))
                    if n >= NB:
                        act.wait_ge(s_st[b], c2 * (16 * 2 * NT // NB) + 16 * (n // NB))
                    else:
                        act.wait_ge(s_st[b], c2 * (16 * 2 * NT // NB))
                    act.copy(stage[:, b, :], acc[:, b, 0:CW]).then_inc(s_eva, 1)

        @block.vector
        def _(dve):
            dve.memset(h_rows[:, NT - 1, :], 0.0).then_inc(s_zero, 1)
            dve.wait_ge(s_ssq, NT)
            dve.tensor_scalar(ms[:, :], ssq[:, :], 1.0 / D, EPS, ALU.mult, ALU.add).then_inc(s_ms, 1)
            dve.wait_ge(s_rms, 1)
            dve.reciprocal(rstd[:, :], rms[:, :]).then_inc(s_stat, 1)
            dve.wait_ge(s_stat, 1)
            dve.wait_ge(s_g, 16)

            def evacuate(t):
                dve.wait_ge(s_tp, 2 * t + 2)
                dve.tensor_copy(xnT[:, 4:8, t * P:(t + 1) * P],
                                tp[:, 1, :].rearrange("p (k t) -> p k t", k=4)).then_inc(s_tpv, 1)

            for t in range(NT):
                if t >= 2:
                    evacuate(t - 2)
                dve.scalar_tensor_tensor(out=xn[:, t % 2, :], in0=h_rows[:, t, :], scalar=rstd[:, t:t + 1],
                                         in1=g_bc[:, :], op0=ALU.mult, op1=ALU.mult).then_inc(s_xn, 1)
            evacuate(NT - 2)
            evacuate(NT - 1)
            with dve.Fori(0, CHUNKS // 2) as c2:
                for n in range(1, 2 * NT, 2):
                    b = n % NB
                    dve.wait_ge(s_mm, c2 * (2 * NT) + (n + 1))
                    if n >= NB:
                        dve.wait_ge(s_st[b], c2 * (16 * 2 * NT // NB) + 16 * (n // NB))
                    else:
                        dve.wait_ge(s_st[b], c2 * (16 * 2 * NT // NB))
                    dve.tensor_copy(stage[:, b, :], acc[:, b, 0:CW]).then_inc(s_evv, 1)

        @block.tensor
        def _(pe):
            for t in range(NT):
                pe.wait_ge(s_xn, t + 1)
                for half, taken in ((0, s_tpa), (1, s_tpv)):
                    if t >= 1:
                        pe.wait_ge(taken, t)
                    for j in range(4):
                        k = half * 4 + j
                        last = pe.transpose(tp[:, half, j * P:(j + 1) * P], xn[:, t % 2, k * P:(k + 1) * P],
                                            ident[:, :])
                    last.then_inc(s_tp, 1)
            pe.wait_ge(s_tpa, NT)
            pe.wait_ge(s_tpv, NT)
            with pe.Fori(0, CHUNKS // 2) as c2:
                for u in range(2):
                    pe.wait_ge(s_w[u], c2 * 16 + 16)
                    for t in range(NT):
                        n = u * NT + t
                        b = n % NB
                        if n % 2 == 0:
                            pe.wait_ge(s_eva, c2 * NT + max(0, n // 2 + 1 - NB // 2)) if n >= NB else \
                                pe.wait_ge(s_eva, c2 * NT)
                        else:
                            pe.wait_ge(s_evv, c2 * NT + max(0, n // 2 + 1 - NB // 2)) if n >= NB else \
                                pe.wait_ge(s_evv, c2 * NT)
                        for k in range(KT):
                            last = pe.matmul(acc[:, b, 0:CW], xnT[:, k, t * P:(t + 1) * P], w[:, u, k, :],
                                             start=(k == 0), stop=(k == KT - 1))
                        last.then_inc(s_mm, 1)
    return used


def stage_attention(nc, io, scr, ident, xnT):
    W = [min(P * (i + 1), L) for i in range(NT)]
    ZW = P * (NT - 1)
    used = []
    with ExitStack() as ctx:
        def sb(name, shape, dt=F32):
            return ctx.enter_context(nc.sbuf_tensor(name, shape, dt))

        def sem(name):
            used.append(ctx.enter_context(nc.semaphore(name)))
            return used[-1]

        tab = sb("a_tab", [P, NT, TAB])
        rows = sb("a_rows", [P, 2, C_HQ])
        t1 = sb("a_t1", [P, 4, QK_HEADS * ROT // 2])
        t2 = sb("a_t2", [P, 4, (IDX_HEADS + 1) * IROT // 2])
        ik4 = sb("a_ik4", [P, 2, 4 * IDX_DIM])
        qpair = sb("a_qpair", [P, 2, 4, 2, HD])
        iws = sb("a_iws", [P, NT, IDX_HEADS])
        keyT = sb("a_keyT", [P, LP])
        ikT = sb("a_ikT", [P, LP])
        val = sb("a_val", [P, NT, KV_HEADS * HD])
        qT = sb("a_qT", [P, 2, 4, P])
        iqT = sb("a_iqT", [P, 2, 2, P])
        start = sb("a_start", [P, ZW + P])
        rel = sb("a_rel", [P, 2, L])
        score = sb("a_score", [P, 2, L])
        top8 = sb("a_top8", [P, 8])
        drop = sb("a_drop", [P, L])
        lg = sb("a_lg", [P, 2, L])
        mx = sb("a_mx", [P, 2, ATT_HEADS])
        nmx = sb("a_nmx", [P, 2, ATT_HEADS])
        rsum = sb("a_rsum", [P, 2, ATT_HEADS])
        rinv = sb("a_rinv", [P, ATT_HEADS])
        pT = sb("a_pT", [P, 2, NT, P])
        att = sb("a_att", [P, 2, ATT_HEADS * HD])
        fw = sb("a_fw", [P, 2, KT, FW])
        FST = 3
        fst = sb("a_fst", [P, FST, FW])
        ps_x = ctx.enter_context(nc.psum_tensor("a_ps_x", [P, 3, 512], F32))
        ps_l = ctx.enter_context(nc.psum_tensor("a_ps_l", [P, 3, 512], F32))
        ps_t = ctx.enter_context(nc.psum_tensor("a_ps_t", [P, 512], F32))
        ps_o = ctx.enter_context(nc.psum_tensor("a_ps_o", [P, 512], F32))

        s_tab = sem("a_tab_landed")
        s_row = [sem(f"a_rows_landed{b}") for b in range(2)]
        s_mask = sem("a_mask_ready")
        s_rope = sem("a_rope_done")
        s_copy = sem("a_value_and_ik_copied")
        s_t = sem("a_transposes_ready")
        s_te = sem("a_transposes_taken")
        s_x = sem("a_index_product_ready")
        s_relu = sem("a_relu_ready")
        s_acc = sem("a_score_added")
        s_dv = sem("a_dve_chain")
        s_l = sem("a_logit_product_ready")
        s_lm = sem("a_logit_masked")
        s_nm = sem("a_negmax_ready")
        s_exp = sem("a_exp_ready")
        s_pv = sem("a_pv_done")
        s_att = sem("a_att_ready")
        s_out = [sem(f"a_att_stored{b}") for b in range(2)]
        s_zs = sem("a_zeros_stored")

        s_fw = [nc.alloc_semaphore(f"a_fill_w_landed{b}") for b in range(2)]
        s_fm = sem("a_fill_product_ready")
        s_fe = sem("a_fill_product_taken")
        s_fs = [nc.alloc_semaphore(f"a_fill_stored{b}") for b in range(FST)]

        UNITS = FCHUNKS * NT
        room, ends = {}, {}
        for i in range(NT - 1):
            for h in range(ATT_HEADS):
                for place in range(3):
                    room[i, h, place] = 0
            lump = max(2, int(ROUNDS * 2 * (W[i] / 0.96 + 60) / 860)) if P * (i + 1) > K_SEL else 6
            room[i, 0, 0] = lump
        rest = UNITS * KT - sum(room.values())
        heads = [(i, h, place) for i in range(NT - 1) for h in range(ATT_HEADS) for place in range(3)]
        weight = [W[i] + 256 for i, h, place in heads]
        done = 0
        for j, key in enumerate(heads):
            upto = round(rest * sum(weight[:j + 1]) / sum(weight)) if rest > 0 else 0
            room[key] += upto - done
            done = upto
        made = 0
        for key in heads:
            for _ in range(room[key]):
                if made % KT == KT - 1:
                    ends.setdefault(key, []).append(made // KT)
                made += 1
        assert made == UNITS * KT

        def ended(i):
            return [u for (j, h, place), units in ends.items() if j == i for u in units]

        first_a_only = min(ended(NT - 2))

        def fill_bank(u):
            return (ps_x if u % 2 and u < first_a_only else ps_l)[:, 2, :]

        def fill_before(u):
            mine = u % 2 and u < first_a_only
            for v in range(u - 1, -1, -1):
                if bool(v % 2 and v < first_a_only) == bool(mine):
                    return v + 1
            return 0

        number = {}
        for i in range(-1, NT):
            if i + 1 < NT:
                number["q", i + 1] = len(number)
                number["k", i + 1] = len(number)
            if i >= 0:
                for h in range(ATT_HEADS):
                    for g in range(-(-(i + 1) // 4)):
                        number["p", i, h, g] = len(number)

        block = ctx.enter_context(nc.Block())

        def store(sp, i):
            sp.wait_ge(s_att, i + 1)
            sp.dma_start(scr["att"][i * P:(i + 1) * P, :], att[:, i % 2, :]).then_inc(s_out[i % 2], 16)

        @block.sync
        def _(sp):
            sp.dma_start(tab[:, :, :], io["rope"].rearrange("(t p) c -> p t c", p=P)).then_inc(s_tab, 16)
            for i in range(NT):
                if i >= 2:
                    sp.wait_ge(s_t, number["k", i - 2] + 1)
                    sp.wait_ge(s_copy, 4 * (i - 1))
                sp.dma_start(rows[:, i % 2, :], scr["proj"][i * P:(i + 1) * P, 0:C_HQ]).then_inc(s_row[i % 2], 16)
                if i >= 3:
                    store(sp, i - 3)
                if i < ZERO_DMAS:
                    if i == 0:
                        sp.wait_ge(s_mask, 1)
                    r0 = N_EXP * ITEM + i * ZERO_P * ZERO_N
                    sp.dma_start(scr["y"][r0:r0 + ZERO_P * ZERO_N, :].rearrange("(p n) d -> p n d", p=ZERO_P),
                                 start[0:ZERO_P, 0:D].unsqueeze(1).to_broadcast([ZERO_P, ZERO_N, D])).then_inc(s_zs, 16)
            for i in range(NT - 3, NT):
                store(sp, i)
            sp.wait_ge(s_zs, 16 * ZERO_DMAS)
            for b in range(2):
                sp.wait_ge(s_out[b], 16 * len(range(b, NT, 2)))

        @block.gpsimd
        def _(pool):
            w_in = io["w_in"][0].rearrange("(kt p) n -> p kt n", p=P)

            def load_chunk(c):
                pool.dma_start(fw[:, c % 2, :, :], w_in[:, :, C_HQ + c * FW:C_HQ + (c + 1) * FW]).then_inc(s_fw[c % 2], 16)

            def store_unit(u):
                c, t = u // NT, u % NT
                pool.wait_ge(s_fe, u + 1)
                pool.dma_start(scr["proj"][t * P:(t + 1) * P, C_HQ + c * FW:C_HQ + (c + 1) * FW],
                               fst[:, u % FST, :]).then_inc(s_fs[u % FST], 16)
                if t == NT - 1 and c + 2 < FCHUNKS:
                    load_chunk(c + 2)

            load_chunk(0)
            load_chunk(1)
            pool.memset(start[:, :], 0.0).then_inc(s_mask, 1)
            pool.wait_ge(s_mask, 1)
            pool.affine_select(out=start[:, ZW:], in_=start[:, ZW:], compare_op=ALU.is_ge, fill=MASKED,
                               base=0, pattern=[[-1, P]], channel_multiplier=1).then_inc(s_mask, 1)
            for i in range(NT):
                pool.wait_ge(s_rope, i + 1)
                pool.tensor_copy(val[:, i, :], rows[:, i % 2, C_V:C_IQ]).then_inc(s_copy, 1)
                if i >= 2:
                    pool.wait_ge(s_t, number["k", i - 2] + 1)
                ik = rows[:, i % 2, C_IK:C_IW].unsqueeze(1).to_broadcast([P, 4, IDX_DIM])
                pool.tensor_copy(ik4[:, i % 2, :].rearrange("p (r d) -> p r d", r=4), ik).then_inc(s_copy, 1)
                for g in range(KV_HEADS):
                    pool.tensor_copy(qpair[:, i % 2, :, g, :],
                                     rows[:, i % 2, g * 4 * HD:(g + 1) * 4 * HD].rearrange("p (m d) -> p m d", d=HD)
                                     ).then_inc(s_copy, 1)
                for u in ended(i - 1):
                    store_unit(u)
            for b in range(FST):
                pool.wait_ge(s_fs[b], 16 * len(range(b, UNITS, FST)))

        @block.vector
        def _(dve):
            ch = Chain(dve, s_dv)

            def rope(i):
                dve.wait_ge(s_row[i % 2], 16 * (i // 2 + 1))
                parts = []
                c0 = 0
                for heads, d, half, base, t in ((QK_HEADS, HD, ROT // 2, C_Q, t1),
                                                (IDX_HEADS + 1, IDX_DIM, IROT // 2, C_IQ, t2)):
                    n = heads * half
                    v = rows[:, i % 2, base:base + heads * d].rearrange("p (h d) -> p h d", d=d) \
                        if base == C_IQ else rows[:, i % 2, 0:heads * d].rearrange("p (h d) -> p h d", d=d)
                    co = tab[:, i, c0:c0 + n].rearrange("p (h d) -> p h d", d=half)
                    si = tab[:, i, c0 + n:c0 + 2 * n].rearrange("p (h d) -> p h d", d=half)
                    c0 += 2 * n
                    tv = [t[:, j, :].rearrange("p (h d) -> p h d", d=half) for j in range(4)]
                    parts.append((v[:, :, 0:half], v[:, :, half:2 * half], co, si, tv))
                for x1, x2, co, si, tv in parts:
                    dve.tensor_tensor(tv[0], x1, co, ALU.mult)
                    dve.tensor_tensor(tv[1], x2, si, ALU.mult)
                    dve.tensor_tensor(tv[2], x2, co, ALU.mult)
                    last = dve.tensor_tensor(tv[3], x1, si, ALU.mult)
                ch.link(last)
                for x1, x2, co, si, tv in parts:
                    dve.tensor_tensor(x1, tv[0], tv[1], ALU.subtract)
                    dve.tensor_tensor(x2, tv[2], tv[3], ALU.add)
                dve.tensor_scalar(iws[:, i, :], rows[:, i % 2, C_IW:C_HQ], IDX_SCALE, None,
                                  ALU.mult).then_inc(s_rope, 1)

            def add_head(i, h):
                n = IDX_HEADS * i + h
                w = W[i]
                dve.wait_ge(s_relu, n + 1)
                before = start[:, ZW - P * i:ZW - P * i + w] if h == 0 else score[:, i % 2, 0:w]
                if h:
                    dve.wait_ge(s_acc, n)
                dve.scalar_tensor_tensor(out=score[:, i % 2, 0:w], in0=rel[:, n % 2, 0:w], scalar=iws[:, i, h:h + 1],
                                         in1=before, op0=ALU.mult, op1=ALU.add).then_inc(s_acc, 1)

            def select(i):
                s = score[:, i % 2, 0:W[i]]
                dve.wait_ge(s_acc, IDX_HEADS * (i + 1))
                if P * (i + 1) > K_SEL:
                    for r in range(ROUNDS):
                        ch.link(dve.max(top8[:, :], s))
                        ch.link(dve.match_replace(s, top8[:, :], s, TAKEN))
                    ch.link(dve.tensor_scalar(drop[:, 0:W[i]], s, SPLIT, DROP, ALU.is_gt, ALU.mult))
                else:
                    ch.link(dve.tensor_scalar(drop[:, 0:W[i]], s, MASKED / 2, DROP, ALU.is_le, ALU.mult))

            def mask_logits(i, h):
                n = ATT_HEADS * i + h
                w = W[i]
                dve.wait_ge(s_l, n + 1)
                if n >= 2:
                    dve.wait_ge(s_pv, n - 1)
                dve.tensor_tensor_reduce(lg[:, n % 2, 0:w], ps_l[:, :, :].rearrange("p b c -> p (b c)")[:, 0:w],
                                         drop[:, 0:w], 1.0, -3.4e38, ALU.add, ALU.max,
                                         mx[:, i % 2, h:h + 1]).then_inc(s_lm, 1)
                dve.wait_ge(s_lm, n + 1)
                dve.tensor_scalar(nmx[:, i % 2, h:h + 1], mx[:, i % 2, h:h + 1], -ATT_SCALE, None,
                                  ALU.mult).then_inc(s_nm, 1)

            def normalize(i):
                dve.wait_ge(s_pv, ATT_HEADS * (i + 1))
                ch.link(dve.reciprocal(rinv[:, :], rsum[:, i % 2, :]))
                if i >= 2:
                    dve.wait_ge(s_out[i % 2], 16 * (i // 2))
                dve.tensor_tensor(att[:, i % 2, :].rearrange("p (h d) -> p h d", d=HD),
                                  ps_o[:, :].rearrange("p (h d) -> p h d", d=HD),
                                  rinv[:, :].unsqueeze(2).to_broadcast([P, ATT_HEADS, HD]),
                                  ALU.mult).then_inc(s_att, 1)

            dve.wait_ge(s_tab, 16)
            rope(0)
            dve.wait_ge(s_mask, 2)
            for h in range(IDX_HEADS):
                add_head(0, h)
            for i in range(NT):
                if i + 1 < NT:
                    rope(i + 1)
                select(i)
                for h in range(ATT_HEADS):
                    mask_logits(i, h)
                    if i + 1 < NT:
                        add_head(i + 1, h)
                normalize(i)

        @block.scalar
        def _(act):
            def take_rows(i):
                act.wait_ge(s_t, number["q", i] + 1)
                act.copy(qT[:, i % 2, :, :], ps_t[:, :].rearrange("p (m t) -> p m t", m=4)).then_inc(s_te, 1)
                act.wait_ge(s_t, number["k", i] + 1)
                act.copy(keyT[:, i * P:(i + 1) * P], ps_t[:, 0:P])
                act.copy(iqT[:, i % 2, :, :], ps_t[:, P:3 * P].rearrange("p (m t) -> p m t", m=2))
                act.copy(ikT[:, i * P:(i + 1) * P], ps_t[:, 3 * P:4 * P]).then_inc(s_te, 1)

            def relu(i, h):
                n = IDX_HEADS * i + h
                act.wait_ge(s_x, n + 1)
                if n >= 2:
                    act.wait_ge(s_acc, n - 1)
                act.activation(rel[:, n % 2, 0:W[i]], ps_x[:, :, :].rearrange("p b c -> p (b c)")[:, 0:W[i]],
                               ACT.Relu).then_inc(s_relu, 1)

            def exponent(i, h):
                n = ATT_HEADS * i + h
                act.wait_ge(s_nm, n + 1)
                act.activation(lg[:, n % 2, 0:W[i]], lg[:, n % 2, 0:W[i]], ACT.Exp, bias=nmx[:, i % 2, h:h + 1],
                               scale=ATT_SCALE, accum_out=rsum[:, i % 2, h:h + 1]).then_inc(s_exp, 1)

            def take_probs(i, h):
                n = ATT_HEADS * i + h
                if n >= 2:
                    act.wait_ge(s_pv, n - 1)
                for g in range(-(-(i + 1) // 4)):
                    act.wait_ge(s_t, number["p", i, h, g] + 1)
                    k = min(4, i + 1 - 4 * g)
                    rows_ = min(P, W[i] - 4 * g * P)
                    act.copy(pT[0:rows_, n % 2, 4 * g:4 * g + k, :],
                             ps_t[0:rows_, 0:k * P].rearrange("p (m t) -> p m t", m=k)).then_inc(s_te, 1)

            def take_units(i, h, place):
                for u in ends.get((i, h, place), ()):
                    act.wait_ge(s_fm, u + 1)
                    if u >= FST:
                        act.wait_ge(s_fs[u % FST], 16 * (u // FST))
                    act.copy(fst[:, u % FST, :], fill_bank(u)).then_inc(s_fe, 1)

            take_rows(0)
            for h in range(IDX_HEADS):
                relu(0, h)
            for i in range(NT):
                if i + 1 < NT:
                    take_rows(i + 1)
                for h in range(ATT_HEADS):
                    if i + 1 < NT:
                        relu(i + 1, h)
                    if h == 0:
                        take_units(i, h, 0)
                    exponent(i, h)
                    if h:
                        take_units(i, h, 0)
                        take_probs(i, h - 1)
                    take_units(i, h, 1)
                    take_units(i, h, 2)
                take_probs(i, ATT_HEADS - 1)

        @block.tensor
        def _(pe):
            def bank_free(key):
                if number[key]:
                    pe.wait_ge(s_te, number[key])

            def turn_rows(i):
                pe.wait_ge(s_rope, i + 1)
                pe.wait_ge(s_copy, 4 * (i + 1))
                bank_free(("q", i))
                for m in range(4):
                    last = pe.transpose(ps_t[:, m * P:(m + 1) * P],
                                        qpair[:, i % 2, m, :, :].rearrange("p g d -> p (g d)"), ident[:, :])
                last.then_inc(s_t, 1)
                bank_free(("k", i))
                pe.transpose(ps_t[:, 0:P], rows[:, i % 2, C_K:C_V], ident[:, :])
                pe.transpose(ps_t[:, P:2 * P], rows[:, i % 2, C_IQ:C_IQ + P], ident[:, :])
                pe.transpose(ps_t[:, 2 * P:3 * P], rows[:, i % 2, C_IQ + P:C_IK], ident[:, :])
                pe.transpose(ps_t[:, 3 * P:4 * P], ik4[:, i % 2, :], ident[:, :]).then_inc(s_t, 1)

            def index_product(i, h):
                n = IDX_HEADS * i + h
                if h == 0:
                    pe.wait_ge(s_te, number["k", i] + 1)
                if n:
                    pe.wait_ge(s_relu, n)
                r = IDX_DIM * (h % 4)
                for c in range(0, W[i], 512):
                    e = min(c + 512, W[i])
                    last = pe.matmul(ps_x[:, c // 512, 0:e - c], iqT[r:r + IDX_DIM, i % 2, h // 4, :],
                                     ikT[r:r + IDX_DIM, c:e], start=True, stop=True)
                last.then_inc(s_x, 1)

            def logits(i, h):
                n = ATT_HEADS * i + h
                if n:
                    pe.wait_ge(s_lm, n)
                r = HD * (h // 4)
                for c in range(0, W[i], 512):
                    e = min(c + 512, W[i])
                    last = pe.matmul(ps_l[:, c // 512, 0:e - c], qT[r:r + HD, i % 2, h % 4, :],
                                     keyT[r:r + HD, c:e], start=True, stop=True)
                last.then_inc(s_l, 1)

            def turn_probs(i, h):
                n = ATT_HEADS * i + h
                pe.wait_ge(s_exp, n + 1)
                for g in range(-(-(i + 1) // 4)):
                    bank_free(("p", i, h, g))
                    for t in range(4 * g, min(4 * g + 4, i + 1)):
                        k = min(P, W[i] - t * P)
                        last = pe.transpose(ps_t[0:k, (t - 4 * g) * P:(t - 4 * g + 1) * P],
                                            lg[:, n % 2, t * P:t * P + k], ident[:, :])
                    last.then_inc(s_t, 1)

            def attend(i, h):
                n = ATT_HEADS * i + h
                groups = -(-(i + 1) // 4)
                pe.wait_ge(s_te, number["p", i, h, groups - 1] + 1)
                if h == 0 and i:
                    pe.wait_ge(s_att, i)
                v = HD * (h // 4)
                for t in range(i + 1):
                    k = min(P, W[i] - t * P)
                    last = pe.matmul(ps_o[:, h * HD:(h + 1) * HD], pT[0:k, n % 2, t, :], val[0:k, t, v:v + HD],
                                     start=(t == 0), stop=(t == i))
                last.then_inc(s_pv, 1)

            unit = [0, 0]

            def fill(i, h, place):
                for _ in range(room.get((i, h, place), 0)):
                    u, k = unit
                    c, t = u // NT, u % NT
                    if k == 0:
                        pe.wait_ge(s_fw[c % 2], 16 * (c // 2 + 1))
                        if fill_before(u):
                            pe.wait_ge(s_fe, fill_before(u))
                    last = pe.matmul(fill_bank(u), xnT[:, k, t * P:(t + 1) * P], fw[:, c % 2, k, :],
                                     start=(k == 0), stop=(k == KT - 1))
                    if k == KT - 1:
                        last.then_inc(s_fm, 1)
                    unit[0], unit[1] = (u + 1, 0) if k == KT - 1 else (u, k + 1)

            turn_rows(0)
            for h in range(IDX_HEADS):
                index_product(0, h)
            for i in range(NT):
                if i + 1 < NT:
                    turn_rows(i + 1)
                if i == NT - 2:
                    pe.wait_ge(s_fe, first_a_only)
                if i == NT - 1:
                    pe.wait_ge(s_fe, UNITS)
                for h in range(ATT_HEADS):
                    if i + 1 < NT:
                        index_product(i + 1, h)
                    logits(i, h)
                    fill(i, h, 0)
                    if h:
                        turn_probs(i, h - 1)
                        fill(i, h, 1)
                        attend(i, h - 1)
                    else:
                        fill(i, h, 1)
                    fill(i, h, 2)
                turn_probs(i, ATT_HEADS - 1)
                attend(i, ATT_HEADS - 1)
    return used


BL = 32
NB4 = P // BL
BIG = 1.0e37


def stage_hgrn(nc, io, scr, ident):
    used = []
    with ExitStack() as ctx:
        def sb(name, shape, dt=F32):
            return ctx.enter_context(nc.sbuf_tensor(name, shape, dt))

        def bank(name):
            return ctx.enter_context(nc.psum_tensor(name, [P, 512], F32))

        def sem(name):
            used.append(ctx.enter_context(nc.semaphore(name)))
            return used[-1]

        lb_rows = sb("g_lb_rows", [2 * HG_HEADS, P])
        lbt = sb("g_lbt", [P, 8, HG_HEADS])
        g_bc = sb("g_g_bc", [P, HGW])
        ones = sb("g_run", [P, HGW])
        cmask = sb("g_cmask", [P, HG_HEADS, BL])
        qf = sb("g_qf", [P, 2 * HGW])
        v = sb("g_v", [P, HGW])
        hg = sb("g_hg", [P, HGW])
        sg = sb("g_sg", [P, HGW])
        f = sb("g_f", [P, HGW])
        kk = sb("g_kk", [P, HGW])
        lf = sb("g_lf", [P, HGW])
        b = sb("g_b", [P, HGW])
        bm = sb("g_bm", [P, HGW])
        bl = sb("g_bl", [P, HGW])
        e = sb("g_e", [P, 4, HGW])
        dec = sb("g_dec", [P, HG_HEADS, NB4])
        qe = sb("g_qe", [P, HGW])
        ke = sb("g_ke", [P, HGW])
        qs = sb("g_qs", [P, HGW])
        ks = sb("g_ks", [P, HGW])
        kst = sb("g_kst", [P, HGW])
        at = sb("g_at", [P, HG_HEADS, BL])
        state = sb("g_state", [P, NB4, HGW])
        sq = sb("g_sq", [P, HG_HEADS, P])
        st4 = sb("g_st4", [P, 4, HG_HEADS])
        sl = sb("g_sl", [P, 2, HGW])
        on = sb("g_on", [P, HGW])
        res = sb("g_res", [P, HGW])
        ps_q, ps_f, ps_k, ps_o = bank("g_ps_q"), bank("g_ps_f"), bank("g_ps_k"), bank("g_ps_o")
        ps_s = [bank(f"g_ps_s{j}") for j in range(NB4)]

        s_lb = sem("g_lb_landed")
        s_gb = sem("g_g_landed")
        s_qf = sem("g_qf_landed")
        s_v = sem("g_v_landed")
        s_hg = sem("g_hg_landed")
        s_cst = sem("g_constants")
        s_lbt = sem("g_lb_turned")
        s_dv = sem("g_dve_chain")
        s_ac = sem("g_act_chain")
        s_lbe = sem("g_lb_exp_ready")
        s_lbm = sem("g_lb_shifted")
        s_st0 = sem("g_state_zeroed")
        s_turn = sem("g_q_and_f_turned")
        s_eg = sem("g_exp_gate_ready")
        s_f = sem("g_f_ready")
        s_lf = sem("g_log_ready")
        s_b = sem("g_b_ready")
        s_e = sem("g_exps_ready")
        s_qk = sem("g_scaled_ready")
        s_kt = sem("g_ks_turned")
        s_kst = sem("g_kst_ready")
        s_a = sem("g_pairs_ready")
        s_at = sem("g_masked_ready")
        s_ps = sem("g_outer_ready")
        s_s = sem("g_state_ready")
        s_o = sem("g_o_ready")
        s_sq = sem("g_squares_ready")
        s_var = sem("g_variance_ready")
        s_rs = sem("g_rstd_ready")
        s_sl = sem("g_gate_exp_ready")
        s_res = sem("g_result_ready")
        s_out = sem("g_result_stored")

        def blocks(ap):
            return ap.rearrange("p (c t) -> p c t", t=BL)

        block = ctx.enter_context(nc.Block())

        @block.sync
        def _(sp):
            sp.dma_start(lb_rows[:, :], io["hgrn_lb_logits"].rearrange("r (h d) -> (r h) d", d=P)).then_inc(s_lb, 16)
            sp.dma_start(g_bc[:, :], io["hgrn_norm_g"].partition_broadcast(P)).then_inc(s_gb, 16)
            with sp.Fori(0, NT) as i:
                rows = bass.ds(i * P, P)
                sp.wait_ge(s_turn, i)
                sp.dma_start(qf[:, :], scr["proj"][rows, C_HQ:C_HI]).then_inc(s_qf, 16)
                sp.wait_ge(s_o, i * NB4)
                sp.dma_start(v[:, :], scr["proj"][rows, C_HI:C_HG]).then_inc(s_v, 16)
                sp.wait_ge(s_res, i)
                sp.dma_start(hg[:, :], scr["proj"][rows, C_HG:C_GA]).then_inc(s_hg, 16)
                sp.wait_ge(s_res, i + 1)
                sp.dma_start(scr["hgr"][rows, :], res[:, :]).then_inc(s_out, 16)
            sp.wait_ge(s_out, 16 * NT)

        @block.gpsimd
        def _(pool):
            pool.memset(ones[:, :], 1.0).then_inc(s_cst, 1)
            pool.memset(cmask[:, :, :], 0.0).then_inc(s_cst, 1)
            pool.memset(state[:, 0, :], 0.0).then_inc(s_st0, 1)
            pool.wait_ge(s_cst, 2)
            pool.memset(blocks(ones[:, :])[:, :, 0:1], 0.0).then_inc(s_cst, 1)
            for j in range(NB4):
                pool.wait_ge(s_cst, 3 + j)
                pool.affine_select(out=cmask[BL * j:BL * (j + 1), :, :], in_=cmask[BL * j:BL * (j + 1), :, :],
                                   compare_op=ALU.is_gt, fill=1.0, base=0, pattern=[[0, HG_HEADS], [-1, BL]],
                                   channel_multiplier=1).then_inc(s_cst, 1)

        @block.vector
        def _(dve):
            ch = Chain(dve, s_dv)
            a0, a1 = lbt[:, 0, :], lbt[:, 1, :]
            dve.wait_ge(s_lbt, 1)
            ch.link(dve.tensor_copy(lbt[:, 0:2, :], ps_q[:, 0:2 * HG_HEADS].rearrange("p (r h) -> p r h", r=2)))
            ch.link(dve.tensor_tensor(lbt[:, 2, :], a0, a1, ALU.max))
            dve.tensor_tensor(lbt[:, 3, :], a0, lbt[:, 2, :], ALU.subtract)
            dve.tensor_tensor(lbt[:, 4, :], a1, lbt[:, 2, :], ALU.subtract).then_inc(s_lbm, 1)
            dve.wait_ge(s_lbe, 1)
            ch.link(dve.tensor_tensor(lbt[:, 6, :], lbt[:, 3, :], lbt[:, 4, :], ALU.add))
            ch.link(dve.reciprocal(lbt[:, 7, :], lbt[:, 6, :]))
            ch.link(dve.tensor_tensor(lbt[:, 0, :], lbt[:, 3, :], lbt[:, 7, :], ALU.mult))
            ch.link(dve.tensor_scalar(lbt[:, 1, :], lbt[:, 0, :], -1.0, 1.0, ALU.mult, ALU.add))
            before = ch.n
            PER = 15
            dve.wait_ge(s_gb, 16)
            dve.wait_ge(s_cst, 3 + NB4)
            with dve.Fori(0, NT) as i:
                ch = Chain(dve, s_dv, base=i * PER + before)
                dve.wait_ge(s_eg, i + 1)
                ch.link(dve.tensor_scalar(sg[:, :], sg[:, :], 1.0, None, ALU.add))
                ch.link(dve.reciprocal(sg[:, :], sg[:, :]))
                for h in range(HG_HEADS):
                    c = slice(h * P, (h + 1) * P)
                    last = dve.tensor_scalar(f[:, c], sg[:, c], lbt[:, 1, h:h + 1], lbt[:, 0, h:h + 1],
                                             ALU.mult, ALU.add)
                last.then_inc(s_f, 1)
                dve.wait_ge(s_f, i + 1)
                dve.tensor_scalar(kk[:, :], f[:, :], -1.0, 1.0, ALU.mult, ALU.add)
                dve.wait_ge(s_lf, i + 1)
                ch.link(dve.tensor_tensor_scan(b[:, :], ones[:, :], lf[:, :], 0.0, ALU.mult, ALU.add))
                bb = blocks(b[:, :])
                wide = [P, HG_HEADS * NB4, BL]
                dve.tensor_tensor(blocks(bm[:, :]), bb, bb[:, :, BL // 2 - 1:BL // 2].to_broadcast(wide), ALU.subtract)
                dve.tensor_tensor(blocks(bl[:, :]), bb[:, :, BL - 1:BL].to_broadcast(wide), bb,
                                  ALU.subtract).then_inc(s_b, 1)
                dve.wait_ge(s_e, i + 1)
                dve.scalar_tensor_tensor(out=qe[:, :], in0=ps_q[:, :], scalar=float(HG_D) ** -0.5, in1=e[:, 0, :],
                                         op0=ALU.mult, op1=ALU.mult)
                dve.scalar_tensor_tensor(out=qs[:, :], in0=ps_q[:, :], scalar=float(HG_D) ** -0.5, in1=e[:, 2, :],
                                         op0=ALU.mult, op1=ALU.mult)
                dve.tensor_tensor(ke[:, :], kk[:, :], e[:, 1, :], ALU.mult)
                dve.tensor_tensor(ks[:, :], kk[:, :], e[:, 3, :], ALU.mult).then_inc(s_qk, 1)
                dve.wait_ge(s_a, i + 1)
                ch.link(dve.tensor_scalar(at[:, :, :], ps_f[:, 0:HG_HEADS * BL].rearrange("p (h t) -> p h t", t=BL),
                                          -BIG, BIG, ALU.max, ALU.min))
                dve.tensor_tensor(at[:, :, :], at[:, :, :], cmask[:, :, :], ALU.mult).then_inc(s_at, 1)
                for j in range(NB4):
                    dve.wait_ge(s_ps, i * NB4 + (j + 1))
                    if j == 0:
                        dve.wait_ge(s_st0, 1)
                    if j == NB4 - 1:
                        dve.wait_ge(s_o, i * NB4 + 1)
                    for h in range(HG_HEADS):
                        c = slice(h * P, (h + 1) * P)
                        last = dve.scalar_tensor_tensor(out=state[:, (j + 1) % NB4, c], in0=state[:, j, c],
                                                        scalar=dec[:, h, j:j + 1], in1=ps_s[j][:, c],
                                                        op0=ALU.mult, op1=ALU.add)
                    last.then_inc(s_s, 1)
                    dve.wait_ge(s_s, i * NB4 + (j + 1))
                dve.wait_ge(s_sl, i + 1)
                ch.link(dve.tensor_scalar(sl[:, 0, :], sl[:, 0, :], 1.0, None, ALU.add))
                ch.link(dve.reciprocal(sl[:, 0, :], sl[:, 0, :]))
                ch.link(dve.tensor_tensor(sl[:, 1, :], hg[:, :], sl[:, 0, :], ALU.mult))
                ch.link(dve.tensor_tensor(sl[:, 1, :], sl[:, 1, :], g_bc[:, :], ALU.mult))
                dve.wait_ge(s_sq, i + 1)
                dve.tensor_scalar(st4[:, 1, :], st4[:, 0, :], 1.0 / HG_D, EPS, ALU.mult, ALU.add).then_inc(s_var, 1)
                dve.wait_ge(s_rs, i + 1)
                ch.link(dve.tensor_tensor(on[:, :].rearrange("p (h d) -> p h d", h=HG_HEADS),
                                          ps_o[:, :].rearrange("p (h d) -> p h d", h=HG_HEADS),
                                          st4[:, 3, :].unsqueeze(2).to_broadcast([P, HG_HEADS, P]), ALU.mult))
                dve.wait_ge(s_out, i * 16)
                dve.tensor_tensor(res[:, :], on[:, :], sl[:, 1, :], ALU.mult).then_inc(s_res, 1)
                for _ in range(PER - ch.n):
                    ch.link(dve.tensor_copy(lbt[:, 5, 0:1], lbt[:, 1, 0:1]))

        @block.scalar
        def _(act):
            act.wait_ge(s_lbm, 1)
            act.activation(lbt[:, 3:5, :], lbt[:, 3:5, :], ACT.Exp).then_inc(s_lbe, 1)
            with act.Fori(0, NT) as i:
                act.wait_ge(s_turn, i + 1)
                act.activation(sg[:, :], ps_f[:, :], ACT.Exp, scale=-1.0).then_inc(s_eg, 1)
                act.wait_ge(s_f, i + 1)
                act.activation(lf[:, :], f[:, :], ACT.Ln).then_inc(s_lf, 1)
                act.wait_ge(s_b, i + 1)
                act.activation(e[:, 0, :], bm[:, :], ACT.Exp)
                act.activation(e[:, 1, :], bm[:, :], ACT.Exp, scale=-1.0)
                act.activation(e[:, 2, :], b[:, :], ACT.Exp)
                act.activation(e[:, 3, :], bl[:, :], ACT.Exp)
                act.wait_ge(s_s, i * NB4)
                act.activation(dec[:, :, :], b[:, :].rearrange("p (h j t) -> p h j t", h=HG_HEADS, t=BL)[:, :, :, BL - 1],
                               ACT.Exp).then_inc(s_e, 1)
                act.wait_ge(s_kt, i + 1)
                act.copy(kst[:, :], ps_k[:, :]).then_inc(s_kst, 1)
                act.wait_ge(s_hg, 16 * i + 16)
                act.wait_ge(s_res, i)
                act.activation(sl[:, 0, :], hg[:, :], ACT.Exp, scale=-1.0).then_inc(s_sl, 1)
                act.wait_ge(s_o, i * NB4 + NB4)
                for h in range(HG_HEADS):
                    last = act.activation(sq[:, h, :], ps_o[:, h * P:(h + 1) * P], ACT.Square,
                                          accum_out=st4[:, 0, h:h + 1])
                last.then_inc(s_sq, 1)
                act.wait_ge(s_var, i + 1)
                act.activation(st4[:, 2, :], st4[:, 1, :], ACT.Ln).then_inc(s_ac, 1)
                act.wait_ge(s_ac, i + 1)
                act.activation(st4[:, 3, :], st4[:, 2, :], ACT.Exp, scale=-0.5).then_inc(s_rs, 1)

        @block.tensor
        def _(pe):
            pe.wait_ge(s_lb, 16)
            pe.transpose(ps_q[:, 0:2 * HG_HEADS], lb_rows[:, :], ident[0:2 * HG_HEADS, 0:2 * HG_HEADS]).then_inc(s_lbt, 1)
            pe.wait_ge(s_lbe, 1)
            with pe.Fori(0, NT) as i:
                pe.wait_ge(s_qf, 16 * i + 16)
                pe.wait_ge(s_qk, i)
                pe.wait_ge(s_at, i)
                for h in range(HG_HEADS):
                    c = slice(h * P, (h + 1) * P)
                    pe.transpose(ps_q[:, c], qf[:, c], ident[:, :])
                    last = pe.transpose(ps_f[:, c], qf[:, HGW + h * P:HGW + (h + 1) * P], ident[:, :])
                last.then_inc(s_turn, 1)
                pe.wait_ge(s_qk, i + 1)
                for h in range(HG_HEADS):
                    c = slice(h * P, (h + 1) * P)
                    last = pe.transpose(ps_k[:, c], ks[:, c], ident[:, :])
                last.then_inc(s_kt, 1)
                for j in range(NB4):
                    for h in range(HG_HEADS):
                        c = slice(h * P + j * BL, h * P + (j + 1) * BL)
                        last = pe.matmul(ps_f[BL * j:BL * (j + 1), h * BL:(h + 1) * BL], ke[:, c], qe[:, c],
                                         start=True, stop=True)
                last.then_inc(s_a, 1)
                pe.wait_ge(s_v, 16 * i + 16)
                pe.wait_ge(s_kst, i + 1)
                for j in range(NB4):
                    r = slice(BL * j, BL * (j + 1))
                    for h in range(HG_HEADS):
                        c = slice(h * P, (h + 1) * P)
                        last = pe.matmul(ps_s[j][:, c], kst[r, c], v[r, c], start=True, stop=True)
                    last.then_inc(s_ps, 1)
                pe.wait_ge(s_at, i + 1)
                pe.wait_ge(s_res, i)
                for j in range(NB4):
                    r = slice(BL * j, BL * (j + 1))
                    pe.wait_ge(s_s, i * NB4 + j) if j else pe.wait_ge(s_st0, 1)
                    for h in range(HG_HEADS):
                        c = slice(h * P, (h + 1) * P)
                        pe.matmul(ps_o[r, c], qs[:, h * P + j * BL:h * P + (j + 1) * BL], state[:, j, c],
                                  start=True, stop=False)
                        last = pe.matmul(ps_o[r, c], at[r, h, :], v[r, c], start=False, stop=True)
                    last.then_inc(s_o, 1)




def stage_merge(nc, io, scr, ident):
    used = []
    with ExitStack() as ctx:
        def sb(name, shape, dt=F32):
            return ctx.enter_context(nc.sbuf_tensor(name, shape, dt))

        def banks(name, n):
            return ctx.enter_context(nc.psum_tensor(name, [P, n, 512], F32))

        def sem(name):
            used.append(ctx.enter_context(nc.semaphore(name)))
            return used[-1]

        KH = HGW // P
        wa = sb("m_wa", [P, KH, D])
        wh = sb("m_wh", [P, KH, D])
        wo = sb("m_wo", [P, KT, D])
        wr = sb("m_wr", [P, KT, N_EXP])
        rb = sb("m_rb", [P, N_EXP])
        g_bc = sb("m_g_bc", [P, D])
        br = sb("m_br", [P, 2, HGW])
        brT = sb("m_brT", [P, 2, KH, P])
        gate = sb("m_gate", [P, 2, D])
        eg = sb("m_eg", [P, 2, D])
        mixa = sb("m_mixa", [P, D])
        mix = sb("m_mix", [P, D])
        mixT = sb("m_mixT", [P, KT, P])
        hin = sb("m_hin", [P, D])
        h2 = sb("m_h2", [P, D])
        sq = sb("m_sq", [P, D])
        st = sb("m_st", [P, 4])
        xn = sb("m_xn", [P, D])
        xs = sb("m_xs", [P, 2, D], F16)
        xT = sb("m_xT", [P, KT, P])
        lgt = sb("m_lgt", [P, 2, N_EXP])
        ps_b = banks("m_ps_b", 1)
        ps_u = banks("m_ps_u", 4)
        ps_t = banks("m_ps_t", 1)
        ps_o = banks("m_ps_o", 2)

        s_w = sem("m_weights_landed")
        s_br = sem("m_branches_landed")
        s_gate = sem("m_gates_landed")
        s_h = sem("m_h_landed")
        s_bt = sem("m_branches_turned")
        s_bte = sem("m_branches_taken")
        s_u = sem("m_branch_products_ready")
        s_eg = sem("m_exp_gates_ready")
        s_dv = sem("m_dve_chain")
        s_mix = sem("m_mix_ready")
        s_mt = sem("m_mix_turned")
        s_mte = sem("m_mix_taken")
        s_o = sem("m_out_product_ready")
        s_h2 = sem("m_h2_ready")
        s_h2s = sem("m_h2_stored")
        s_ssq = sem("m_squares_ready")
        s_var = sem("m_variance_ready")
        s_ac = sem("m_act_chain")
        s_rs = sem("m_rstd_ready")
        s_xn = sem("m_xn_ready")
        s_xh = sem("m_xn_hi_ready")
        s_xs = sem("m_xn_parts_ready")
        s_xns = sem("m_xn_stored")
        s_xt = sem("m_xn_turned")
        s_xte = sem("m_xn_taken")
        s_lg = sem("m_logits_ready")
        s_lgb = sem("m_logits_biased")
        s_lgs = sem("m_logits_stored")

        def skewed(eng, stages):
            for i in (0, 1):
                for d, f in enumerate(stages):
                    if 0 <= i - d:
                        f(i - d)
            with eng.Fori(2, NT) as i:
                for d, f in enumerate(stages):
                    f(i - d)
            for i in (NT, NT + 1):
                for d, f in enumerate(stages):
                    if i - d < NT:
                        f(i - d)

        def rows(i):
            return bass.ds(i * P, P)

        block = ctx.enter_context(nc.Block())

        @block.sync
        def _(sp):
            sp.dma_start(g_bc[:, :], io["ffn_norm_g"].partition_broadcast(P)).then_inc(s_w, 16)
            sp.dma_start(rb[:, :], io["router_b"].partition_broadcast(P)).then_inc(s_w, 16)
            sp.dma_start(wa[:, :, :], io["w_up_attn"][0].rearrange("(k p) n -> p k n", p=P)).then_inc(s_w, 16)
            sp.dma_start(wh[:, :, :], io["w_up_hgrn"][0].rearrange("(k p) n -> p k n", p=P)).then_inc(s_w, 16)
            sp.dma_start(wo[:, :, :], io["w_out"][0].rearrange("(k p) n -> p k n", p=P)).then_inc(s_w, 16)
            sp.dma_start(wr[:, :, :], io["router_w"][0].rearrange("(k p) n -> p k n", p=P)).then_inc(s_w, 16)

            def load(i):
                sp.wait_ge(s_bt, 2 * i)
                sp.dma_start(br[:, 0, :], scr["att"][rows(i), :]).then_inc(s_br, 16)
                sp.dma_start(br[:, 1, :], scr["hgr"][rows(i), :]).then_inc(s_br, 16)
                sp.wait_ge(s_eg, i)
                sp.dma_start(gate[:, :, :], scr["proj"][rows(i), C_GA:IN_COLS].rearrange("p (g c) -> p g c", g=2)
                             ).then_inc(s_gate, 16)

            def residual(i):
                sp.wait_ge(s_h2, i)
                sp.dma_start(hin[:, :], scr["h"][rows(i), :]).then_inc(s_h, 16)
                sp.wait_ge(s_h2, i + 1)
                sp.dma_start(scr["h2"][rows(i), :], h2[:, :]).then_inc(s_h2s, 16)

            def store(i):
                sp.wait_ge(s_xs, i + 1)
                sp.dma_start(scr["xn"][rows(i), :], xs[:, :, :].rearrange("p c d -> p (c d)")).then_inc(s_xns, 16)
                sp.wait_ge(s_lgb, i + 1)
                sp.dma_start(scr["logits"][rows(i), :], lgt[:, 0, :]).then_inc(s_lgs, 16)

            skewed(sp, (load, residual, store))
            sp.wait_ge(s_h2s, 16 * NT)
            sp.wait_ge(s_xns, 16 * NT)
            sp.wait_ge(s_lgs, 16 * NT)

        @block.tensor
        def _(pe):
            def branches(i):
                for j in range(2):
                    pe.wait_ge(s_br, 32 * i + 32)
                    pe.wait_ge(s_bte, 2 * i + j)
                    for k in range(KH):
                        last = pe.transpose(ps_b[:, 0, k * P:(k + 1) * P], br[:, j, k * P:(k + 1) * P], ident[:, :])
                    last.then_inc(s_bt, 1)
                pe.wait_ge(s_mix, i)
                for j, w in ((0, wa), (1, wh)):
                    pe.wait_ge(s_bte, 2 * i + (j + 1))
                    for n in range(2):
                        for k in range(KH):
                            last = pe.matmul(ps_u[:, 2 * j + n, :], brT[:, j, k, :], w[:, k, n * 512:(n + 1) * 512],
                                             start=(k == 0), stop=(k == KH - 1))
                last.then_inc(s_u, 1)

            def project(i):
                pe.wait_ge(s_mix, i + 1)
                for n in range(2):
                    pe.wait_ge(s_mte, 2 * i + n)
                    for k in range(4):
                        c = (4 * n + k) * P
                        last = pe.transpose(ps_t[:, 0, k * P:(k + 1) * P], mix[:, c:c + P], ident[:, :])
                    last.then_inc(s_mt, 1)
                pe.wait_ge(s_h2, i)
                pe.wait_ge(s_mte, 2 * i + 2)
                for n in range(2):
                    for k in range(KT):
                        last = pe.matmul(ps_o[:, n, :], mixT[:, k, :], wo[:, k, n * 512:(n + 1) * 512],
                                         start=(k == 0), stop=(k == KT - 1))
                last.then_inc(s_o, 1)

            def route(i):
                pe.wait_ge(s_xn, i + 1)
                for n in range(2):
                    pe.wait_ge(s_xte, 2 * i + n)
                    for k in range(4):
                        c = (4 * n + k) * P
                        last = pe.transpose(ps_t[:, 0, k * P:(k + 1) * P], xn[:, c:c + P], ident[:, :])
                    last.then_inc(s_xt, 1)
                pe.wait_ge(s_xte, 2 * i + 2)
                for k in range(KT):
                    last = pe.matmul(ps_t[:, 0, 0:N_EXP], xT[:, k, :], wr[:, k, :], start=(k == 0), stop=(k == KT - 1))
                last.then_inc(s_lg, 1)
                pe.wait_ge(s_lgb, i + 1)

            pe.wait_ge(s_w, 16 * 6)
            skewed(pe, (branches, project, route))

        @block.scalar
        def _(act):
            def branches(i):
                act.wait_ge(s_gate, 16 * i + 16)
                act.wait_ge(s_mix, i)
                act.activation(eg[:, :, :], gate[:, :, :], ACT.Exp, scale=-1.0).then_inc(s_eg, 1)
                for j in range(2):
                    act.wait_ge(s_bt, 2 * i + (j + 1))
                    act.wait_ge(s_u, i)
                    act.copy(brT[:, j, :, :], ps_b[:, 0, :].rearrange("p (k t) -> p k t", t=P)).then_inc(s_bte, 1)

            def project(i):
                for n in range(2):
                    act.wait_ge(s_mt, 2 * i + (n + 1))
                    act.wait_ge(s_o, i)
                    act.copy(mixT[:, 4 * n:4 * n + 4, :],
                             ps_t[:, 0, :].rearrange("p (k t) -> p k t", t=P)).then_inc(s_mte, 1)
                act.wait_ge(s_h2, i + 1)
                act.wait_ge(s_ssq, i)
                act.activation(sq[:, :], h2[:, :], ACT.Square, accum_out=st[:, 0:1]).then_inc(s_ssq, 1)
                act.wait_ge(s_var, i + 1)
                act.activation(st[:, 2:3], st[:, 1:2], ACT.Ln).then_inc(s_ac, 1)
                act.wait_ge(s_ac, i + 1)
                act.activation(st[:, 3:4], st[:, 2:3], ACT.Exp, scale=-0.5).then_inc(s_rs, 1)

            def route(i):
                for n in range(2):
                    act.wait_ge(s_xt, 2 * i + (n + 1))
                    act.wait_ge(s_lg, i)
                    act.copy(xT[:, 4 * n:4 * n + 4, :],
                             ps_t[:, 0, :].rearrange("p (k t) -> p k t", t=P)).then_inc(s_xte, 1)

            skewed(act, (branches, project, route))

        @block.vector
        def _(dve):
            def merge(i):
                ch = Chain(dve, s_dv, base=4 * i)
                dve.wait_ge(s_eg, i + 1)
                ch.link(dve.tensor_scalar(eg[:, :, :], eg[:, :, :], 1.0, None, ALU.add))
                ch.link(dve.reciprocal(eg[:, :, :], eg[:, :, :]))
                dve.wait_ge(s_u, i + 1)
                dve.tensor_tensor(mixa[:, :], ps_u[:, 0:2, :].rearrange("p n c -> p (n c)"), eg[:, 0, :], ALU.mult)
                ch.link(dve.tensor_tensor(eg[:, 1, :], ps_u[:, 2:4, :].rearrange("p n c -> p (n c)"), eg[:, 1, :],
                                          ALU.mult))
                dve.wait_ge(s_mt, 2 * i)
                ch.link(dve.tensor_tensor(mix[:, :], mixa[:, :], eg[:, 1, :], ALU.add))
                dve.sem_inc(s_mix, 1)

            def residual(i):
                dve.wait_ge(s_o, i + 1)
                dve.wait_ge(s_h, 16 * i + 16)
                dve.wait_ge(s_h2s, 16 * i)
                dve.wait_ge(s_ssq, i)
                dve.tensor_tensor(h2[:, :], hin[:, :], ps_o[:, :, :].rearrange("p n c -> p (n c)"),
                                  ALU.add).then_inc(s_h2, 1)
                dve.wait_ge(s_ssq, i + 1)
                dve.tensor_scalar(st[:, 1:2], st[:, 0:1], 1.0 / D, EPS, ALU.mult, ALU.add).then_inc(s_var, 1)
                dve.wait_ge(s_rs, i + 1)
                dve.wait_ge(s_xt, 2 * i)
                dve.scalar_tensor_tensor(out=xn[:, :], in0=h2[:, :], scalar=st[:, 3:4], in1=g_bc[:, :],
                                         op0=ALU.mult, op1=ALU.mult).then_inc(s_xn, 1)
                dve.wait_ge(s_xns, 16 * i)
                dve.wait_ge(s_xn, i + 1)
                dve.tensor_copy(xs[:, 0, :], xn[:, :]).then_inc(s_xh, 1)
                dve.wait_ge(s_xh, i + 1)
                dve.tensor_tensor(xs[:, 1, :], xn[:, :], xs[:, 0, :], ALU.subtract).then_inc(s_xs, 1)

            def bias(i):
                dve.wait_ge(s_lg, i + 1)
                dve.wait_ge(s_lgs, 16 * i)
                dve.tensor_tensor(lgt[:, 0, :], ps_t[:, 0, 0:N_EXP], rb[:, :], ALU.add).then_inc(s_lgb, 1)

            dve.wait_ge(s_w, 16 * 6)
            skewed(dve, (merge, residual, bias))




def stage_route(nc, io, scr, items, n_items):
    used = []
    with ExitStack() as ctx:
        def sb(name, shape, dt=F32):
            return ctx.enter_context(nc.sbuf_tensor(name, shape, dt))

        def sem(name):
            used.append(ctx.enter_context(nc.semaphore(name)))
            return used[-1]

        lg = sb("r_lg", [P, NT, N_EXP])
        top = sb("r_top", [P, NT, 8])
        topi = sb("r_topi", [P, NT, 8], U32)
        topf = sb("r_topf", [P, NT, 8])
        gate = sb("r_gate", [P, NT, TOP])
        gsum = sb("r_gsum", [P, 2, NT])
        expert = sb("r_expert", [P, N_EXP])
        first = sb("r_first", [P, N_EXP])
        work = sb("r_work", [P, MORE])
        item_id = sb("r_item_id", [1, ITEMS + 1])
        valid = sb("r_valid", [P, NT])
        pad = sb("r_pad", [P, TOP])
        before = sb("r_before", [P, P])
        ones = sb("r_ones", [P, P])
        pick = sb("r_pick", [P, TOP, NT, N_EXP])
        chosen = sb("r_chosen", [P, NT, N_EXP])
        prior = sb("r_prior", [P, NT + 1, N_EXP])
        slot = sb("r_slot", [P, NT, N_EXP])
        over = sb("r_over", [P, NT, N_EXP])
        more = sb("r_more", [P, 4, N_EXP])
        prod = sb("r_prod", [P, NT, N_EXP])
        slots = sb("r_slots", [P, NT, TOP])
        slots_i = sb("r_slots_i", [P, NT, TOP], U32)
        token = sb("r_token", [P, NT], I32)
        zero = sb("r_zero", [P, TABLE // P + 1], I32)
        cmp = sb("r_cmp", [1, MORE, N_EXP])
        rank = ctx.enter_context(nc.psum_tensor("r_rank", [P, 512], F32))
        count = ctx.enter_context(nc.psum_tensor("r_count", [P, 512], F32))

        s_lg = sem("r_logits_landed")
        s_pc = sem("r_pool_chain")
        s_dv = sem("r_dve_chain")
        s_sh = sem("r_gates_shifted")
        s_ge = sem("r_gates_exp")
        s_gate = sem("r_gates_ready")
        s_m = sem("r_chosen_ready")
        s_rank = sem("r_rank_ready")
        s_slot = sem("r_slots_ready")
        s_z = sem("r_table_zeroed")
        s_sc = sem("r_scattered")
        s_st = sem("r_stored")
        block = ctx.enter_context(nc.Block())

        @block.sync
        def _(sp):
            sp.dma_start(lg[:, :, :], scr["logits"].rearrange("(t p) e -> p t e", p=P)).then_inc(s_lg, 16)
            sp.wait_ge(s_gate, 1)
            sp.dma_start(scr["gate"].rearrange("(t p) c -> p t c", p=P), gate[:, :, :]).then_inc(s_st, 16)
            sp.wait_ge(s_slot, 1)
            sp.dma_start(scr["slot"].rearrange("(t p) c -> p t c", p=P), slots_i[:, :, :]).then_inc(s_st, 16)
            sp.wait_ge(s_st, 32)

        @block.gpsimd
        def _(pool):
            ch = Chain(pool, s_pc)
            n = TABLE // P
            ch.link(pool.memset(zero[:, :], 0))
            pool.dma_start(scr["token"][0:n * P, :].rearrange("(p n) o -> p (n o)", p=P), zero[:, 0:n]).then_inc(s_z, 16)
            ch.link(pool.iota(token[:, :], [[P, NT]], base=0, channel_multiplier=1))
            pool.iota(expert[:, :], [[1, N_EXP]], base=0, channel_multiplier=0, allow_small_or_imprecise_dtypes=True)
            pool.iota(first[:, :], [[ITEM, N_EXP]], base=0, channel_multiplier=0, allow_small_or_imprecise_dtypes=True)
            pool.iota(work[:, :], [[1, MORE]], base=0, channel_multiplier=0, allow_small_or_imprecise_dtypes=True)
            pool.iota(item_id[:, :], [[1, ITEMS + 1]], base=0, channel_multiplier=0, allow_small_or_imprecise_dtypes=True)
            pool.iota(pad[:, :], [[P, TOP]], base=PAD, channel_multiplier=1, allow_small_or_imprecise_dtypes=True)
            pool.memset(ones[:, :], 1.0)
            pool.memset(valid[:, :], 1.0)
            ch.link(pool.memset(before[:, :], 1.0))
            pool.affine_select(out=before[:, :], in_=before[:, :], compare_op=ALU.is_gt, fill=0.0, base=0,
                               pattern=[[1, P]], channel_multiplier=-1)
            ch.link(pool.affine_select(out=valid[:, :], in_=valid[:, :], compare_op=ALU.is_ge, fill=0.0, base=L - 1,
                                       pattern=[[-P, NT]], channel_multiplier=-1))
            assert ch.n == POOL_SET
            pool.wait_ge(s_z, 16)
            pool.wait_ge(s_slot, 1)
            for t in range(NT):
                for c in range(TOP):
                    pool.indirect_dma_start(out=scr["token"],
                                            out_offset=bass.IndirectOffsetOnAxis(ap=slots_i[:, t, c:c + 1], axis=0),
                                            in_=token[:, t:t + 1], in_offset=None).then_inc(s_sc, 16)
            pool.wait_ge(s_sc, 16 * NT * TOP)

        @block.vector
        def _(dve):
            ch = Chain(dve, s_dv)
            all_t = [P, NT, N_EXP]
            dve.wait_ge(s_lg, 16)
            for t in range(NT):
                last = dve.max(top[:, t, :], lg[:, t, :])
            ch.link(last)
            for t in range(NT):
                last = dve.max_index(topi[:, t, :], top[:, t, :], lg[:, t, :])
            ch.link(last)
            ch.link(dve.tensor_copy(topf[:, :, :], topi[:, :, :]))
            dve.tensor_tensor(gate[:, :, :], top[:, :, 0:TOP], top[:, :, 0:1].to_broadcast([P, NT, TOP]),
                              ALU.subtract).then_inc(s_sh, 1)
            dve.wait_ge(s_ge, 1)
            ch.link(dve.tensor_reduce(gsum[:, 0, :], gate[:, :, :], AX.X, ALU.add))
            ch.link(dve.reciprocal(gsum[:, 1, :], gsum[:, 0, :]))
            dve.tensor_tensor(gate[:, :, :], gate[:, :, :], gsum[:, 1, :].unsqueeze(2).to_broadcast([P, NT, TOP]),
                              ALU.mult).then_inc(s_gate, 1)
            dve.wait_ge(s_pc, POOL_SET)
            for c in range(TOP):
                last = dve.tensor_tensor(pick[:, c, :, :], expert[:, :].unsqueeze(1).to_broadcast(all_t),
                                         topf[:, :, c:c + 1].to_broadcast(all_t), ALU.is_equal)
            ch.link(last)
            dve.tensor_tensor(chosen[:, :, :], pick[:, 0, :, :], pick[:, 1, :, :], ALU.add)
            ch.link(dve.tensor_tensor(prod[:, :, :], pick[:, 2, :, :], pick[:, 3, :, :], ALU.add))
            ch.link(dve.tensor_tensor(chosen[:, :, :], chosen[:, :, :], prod[:, :, :], ALU.add))
            ch.link(dve.tensor_tensor(chosen[:, :, :], chosen[:, :, :], valid[:, :].unsqueeze(2).to_broadcast(all_t),
                                      ALU.mult))
            ch.link(dve.memset(prior[:, 0, :], 0.0))
            for t in range(NT):
                ch.link(dve.tensor_tensor(prior[:, t + 1, :], prior[:, t, :], chosen[:, t, :], ALU.add))
            dve.sem_inc(s_m, 1)
            dve.wait_ge(s_rank, 1)
            cnt = more[:, 0, :]
            ch.link(dve.tensor_copy(cnt, count[:, 0:N_EXP]))
            ch.link(dve.memset(more[:, 1, :], 0.0))
            for c in range(1, -(-L // ITEM)):
                ch.link(dve.scalar_tensor_tensor(out=more[:, 1, :], in0=cnt, scalar=float(c * ITEM),
                                                 in1=more[:, 1, :], op0=ALU.is_gt, op1=ALU.add))
            ch.link(dve.tensor_tensor_scan(more[:, 2, :], ones[:, 0:N_EXP], more[:, 1, :], 0.0, ALU.mult, ALU.add))
            ch.link(dve.tensor_tensor(more[:, 3, :], more[:, 2, :], more[:, 1, :], ALU.subtract))
            ch.link(dve.tensor_scalar(more[:, 3, :], more[:, 3, :], float(ITEM), float(ITEM * (N_EXP - 1)),
                                      ALU.mult, ALU.add))
            ch.link(dve.tensor_tensor(more[:, 3, :], more[:, 3, :], first[:, :], ALU.subtract))
            r3 = rank[:, 0:NT * N_EXP].rearrange("p (t e) -> p t e", e=N_EXP)
            dve.tensor_tensor(slot[:, :, :], r3, first[:, :].unsqueeze(1).to_broadcast(all_t), ALU.add)
            ch.link(dve.tensor_scalar(over[:, :, :], r3, float(ITEM), None, ALU.is_ge))
            ch.link(dve.tensor_tensor(over[:, :, :], over[:, :, :], more[:, 3, :].unsqueeze(1).to_broadcast(all_t),
                                      ALU.mult))
            ch.link(dve.tensor_tensor(slot[:, :, :], slot[:, :, :], over[:, :, :], ALU.add))
            for c in range(TOP):
                ch.link(dve.tensor_tensor(prod[:, :, :], pick[:, c, :, :], slot[:, :, :], ALU.mult))
                ch.link(dve.tensor_reduce(slots[:, :, c], prod[:, :, :], AX.X, ALU.add))
            ch.link(dve.tensor_tensor(slots[:, :, :], slots[:, :, :], valid[:, :].unsqueeze(2).to_broadcast([P, NT, TOP]),
                                      ALU.mult))
            ch.link(dve.tensor_scalar(gsum[:, 0, :], valid[:, :], -1.0, 1.0, ALU.mult, ALU.add))
            ch.link(dve.tensor_tensor(prod[:, :, 0:TOP], pad[:, :].unsqueeze(1).to_broadcast([P, NT, TOP]),
                                      gsum[:, 0, :].unsqueeze(2).to_broadcast([P, NT, TOP]), ALU.mult))
            ch.link(dve.tensor_tensor(slots[:, :, :], slots[:, :, :], prod[:, :, 0:TOP], ALU.add))
            dve.tensor_copy(slots_i[:, :, :], slots[:, :, :]).then_inc(s_slot, 1)
            one = [1, MORE, N_EXP]
            ch.link(dve.tensor_tensor(cmp[:, :, :], more[0:1, 2, :].unsqueeze(1).to_broadcast(one),
                                      work[0:1, :].unsqueeze(2).to_broadcast(one), ALU.is_le))
            ch.link(dve.tensor_reduce(item_id[:, N_EXP:ITEMS], cmp[:, :, :], AX.X, ALU.add))
            ch.link(dve.tensor_scalar(item_id[:, N_EXP:], item_id[:, N_EXP:], float(N_EXP - 1), None, ALU.min))
            ch.link(dve.tensor_copy(items[:, :], item_id[:, :]))
            ch.link(dve.tensor_scalar(n_items[:, :], more[0:1, 2, N_EXP - 1:N_EXP], float(N_EXP), None, ALU.add))

        @block.scalar
        def _(act):
            act.wait_ge(s_sh, 1)
            act.activation(gate[:, :, :], gate[:, :, :], ACT.Exp).then_inc(s_ge, 1)

        @block.tensor
        def _(pe):
            pe.wait_ge(s_m, 1)
            w = NT * N_EXP
            pe.matmul(rank[:, 0:w], before[:, :], chosen[:, :, :].rearrange("p t e -> p (t e)"), start=True, stop=False)
            pe.matmul(rank[:, 0:w], ones[:, :], prior[:, 0:NT, :].rearrange("p t e -> p (t e)"), start=False, stop=True)
            pe.matmul(count[:, 0:N_EXP], ones[:, :], prior[:, NT, :], start=True, stop=True).then_inc(s_rank, 1)


POOL_SET = 4


D_FF = 1024
FT = D_FF // P
LIMIT, ALPHA = 7.0, 1.702
WS = 256.0
QK = 2
QN = KT // QK
RING = QN
MATS = ("gate", "up", "down")
PARTS = ((0, 0), (0, 1), (1, 0))


def stage_experts(nc, io, scr, ident, ident16, items, n_items):
    used = []
    with ExitStack() as ctx:
        def sb(name, shape, dt=F32):
            return ctx.enter_context(nc.sbuf_tensor(name, shape, dt))

        def sem(name):
            used.append(ctx.enter_context(nc.semaphore(name)))
            return used[-1]

        raw = sb("e_raw", [P, RING, QK, D_FF])
        w = {m: sb(f"e_w_{m}", [P, 2, KT, D_FF], F16) for m in MATS}
        bT = sb("e_bT", [P, 3, FT, N_EXP])
        be = sb("e_be", [P, 3, FT])
        idx = sb("e_idx", [HALF, 2], U32)
        xg = sb("e_xg", [HALF, 2, 2 * D], F16)
        xT = sb("e_xT", [P, KT, 2, ITEM], F16)
        g = sb("e_g", [P, FT, ITEM])
        sg = sb("e_sg", [P, FT, ITEM])
        u = sb("e_u", [P, FT, ITEM])
        a = sb("e_a", [P, FT, 2, ITEM], F16)
        yT = sb("e_yT", [P, KT, ITEM])
        yr = sb("e_yr", [HALF, 2, D])
        ACC, TR = 4, 4
        acc = [ctx.enter_context(nc.psum_tensor(f"e_acc{b}", [P, 512], F32)) for b in range(ACC)]
        tr = [ctx.enter_context(nc.psum_tensor(f"e_tr{b}", [P, 512], F32)) for b in range(TR)]

        s_raw = [sem(f"e_raw_landed{b}") for b in range(RING)]
        s_hi = {m: sem(f"e_{m}_hi_ready") for m in MATS}
        s_lo = {m: sem(f"e_{m}_lo_ready") for m in MATS}
        s_b = sem("e_biases_landed")
        s_bt = sem("e_biases_turned")
        s_bte = sem("e_biases_taken")
        s_be = sem("e_bias_ready")
        s_idx = sem("e_indices_landed")
        s_x = sem("e_rows_gathered")
        s_go = sem("e_gathers_started")
        s_xt = sem("e_rows_turned")
        s_xte = sem("e_rows_taken")
        s_m = {m: sem(f"e_{m}_products") for m in MATS}
        s_ge = sem("e_gate_taken")
        s_ue = sem("e_up_taken")
        s_de = sem("e_down_taken")
        s_sg = sem("e_sigmoid_ready")
        s_gs = sem("e_gated_ready")
        s_dv = sem("e_dve_chain")
        s_ag = sem("e_act_whole")
        s_ah = sem("e_act_hi_ready")
        s_a = sem("e_act_ready")
        s_yt = sem("e_y_turned")
        s_yte = sem("e_y_taken")
        s_y = sem("e_y_stored")

        block = ctx.enter_context(nc.Block())
        bias_rows = [g[0:N_EXP, :, :].rearrange("p f t -> p (f t)")[:, 0:D], sg[0:N_EXP, :, :].rearrange("p f t -> p (f t)")[:, 0:D],
                     u[0:N_EXP, :, :].rearrange("p f t -> p (f t)")[:, 0:D]]

        def count_of(eng):
            return eng.value_load(n_items[0:1, 0:1], min_val=N_EXP, max_val=ITEMS)

        def expert_of(eng, i):
            return eng.value_load(items[0:1, bass.ds(i, 1)], min_val=0, max_val=N_EXP - 1)

        def split_hi(act, m, item, turn, q):
            act.wait_ge(s_raw[q], turn * 16 + 16)
            act.wait_ge(s_m[m], item * FT)
            act.activation(w[m][:, 0, QK * q:QK * (q + 1), :], raw[:, q, :, :], ACT.Copy, scale=WS
                           ).then_inc(s_hi[m], 1)

        def split_lo(dve, m, item, q):
            dve.wait_ge(s_hi[m], item * QN + (q + 1))
            dve.scalar_tensor_tensor(out=w[m][:, 1, QK * q:QK * (q + 1), :].rearrange("p k f -> p (k f)"),
                                     in0=raw[:, q, :, :].rearrange("p k f -> p (k f)"), scalar=WS,
                                     in1=w[m][:, 0, QK * q:QK * (q + 1), :].rearrange("p k f -> p (k f)"),
                                     op0=ALU.mult, op1=ALU.subtract).then_inc(s_lo[m], 1)

        @block.sync
        def _(sp):
            for j, m in enumerate(MATS):
                sp.dma_start(bias_rows[j], io[f"b_{m}"][0]).then_inc(s_b, 16)
            n = count_of(sp)

            def load(m, e, q):
                src = io[f"w_{m}"][0][bass.ds(e, 1), QK * P * q:QK * P * (q + 1), :].rearrange("o (k p) f -> p (o k) f", p=P)
                sp.dma_start(raw[:, q, :, :], src).then_inc(s_raw[q], 16)

            e = expert_of(sp, 0)
            for q in range(QN):
                load("gate", e, q)
            for q in range(QN):
                sp.wait_ge(s_lo["gate"], q + 1)
                load("up", e, q)
            with sp.Fori(0, n) as i:
                e = expert_of(sp, i)
                e_next = expert_of(sp, i + 1)
                for m, ee, last, k in (("down", e, "up", 1), ("gate", e_next, "down", 1), ("up", e_next, "gate", 2)):
                    for q in range(QN):
                        sp.wait_ge(s_lo[last], (i + (k - 1)) * QN + (q + 1))
                        load(m, ee, q)

        @block.gpsimd
        def _(pool):
            n = count_of(pool)

            def gather(i):
                pool.dma_start(idx[:, :].bitcast(I32),
                               scr["token"][bass.ds(i * ITEM, ITEM), :].rearrange("(a p) o -> p (a o)", a=2),
                               allow_slow_non_contiguous=True).then_inc(s_idx, 16)
                pool.wait_ge(s_idx, i * 16 + 16)
                pool.sem_inc(s_go, 1)
                for a_ in range(2):
                    pool.indirect_dma_start(out=xg[:, a_, :], out_offset=None, in_=scr["xn"],
                                            in_offset=bass.IndirectOffsetOnAxis(ap=idx[:, a_:a_ + 1], axis=0)
                                            ).then_inc(s_x, 16)

            gather(0)
            with pool.Fori(0, n) as i:
                pool.wait_ge(s_xt, i * 4 + 4)
                gather(i + 1)
                pool.wait_ge(s_yte, i * 4 + 4)
                pool.dma_start(scr["y"][bass.ds(i * ITEM, ITEM), :].rearrange("(a p) d -> p a d", a=2),
                               yr[:, :, :]).then_inc(s_y, 16)
            pool.wait_ge(s_y, n * 16)
            pool.wait_ge(s_x, n * 32 + 32)
            pool.wait_ge(s_lo["gate"], n * QN + QN)
            pool.wait_ge(s_lo["up"], n * QN + QN)

        @block.tensor
        def _(pe):
            n = count_of(pe)
            pe.wait_ge(s_b, 48)
            for j in range(3):
                for f in range(FT):
                    last = pe.transpose(tr[j][:, f * N_EXP:(f + 1) * N_EXP], bias_rows[j][:, f * P:(f + 1) * P],
                                        ident[0:N_EXP, 0:N_EXP])
                last.then_inc(s_bt, 1)
            pe.wait_ge(s_bte, 3)

            def turn_rows(i):
                pe.wait_ge(s_x, i * 32 + 32)
                for q in range(4):
                    t16 = tr[q][:, :].bitcast(F16)
                    for k in range(2):
                        for part in range(2):
                            for a_ in range(2):
                                c = (k * 2 + part) * ITEM + a_ * HALF
                                r = part * D + (2 * q + k) * P
                                last = pe.transpose(t16[:, c:c + HALF], xg[:, a_, r:r + P], ident16[0:HALF, 0:HALF])
                    last.then_inc(s_xt, 1)

            def product(m, f, x):
                for k in range(KT):
                    for j, (wp, xp) in enumerate(PARTS):
                        last = pe.matmul(acc[f % ACC][:, 0:ITEM], w[m][:, wp, k, f * P:(f + 1) * P], x[:, k, xp, :],
                                         start=(k == 0 and j == 0), stop=(k == KT - 1 and j == len(PARTS) - 1))
                last.then_inc(s_m[m], 1)

            turn_rows(0)
            with pe.Fori(0, n) as i:
                pe.wait_ge(s_xte, i * 4 + 4)
                pe.wait_ge(s_lo["gate"], i * QN + QN)
                pe.wait_ge(s_de, i * FT)
                for f in range(FT):
                    if f >= ACC:
                        pe.wait_ge(s_ge, i * FT + (f + 1 - ACC))
                    product("gate", f, xT)
                pe.wait_ge(s_lo["up"], i * QN + QN)
                for f in range(FT):
                    pe.wait_ge(s_ge, i * FT + (f + 1 + FT - ACC)) if f < ACC else pe.wait_ge(s_ue, i * FT + (f + 1 - ACC))
                    product("up", f, xT)
                pe.wait_ge(s_yte, i * 4)
                turn_rows(i + 1)
                pe.wait_ge(s_lo["down"], i * QN + QN)
                pe.wait_ge(s_a, i * (FT // 2) + FT // 2)
                for f in range(KT):
                    pe.wait_ge(s_ue, i * FT + (f + 1 + FT - ACC)) if f < ACC else pe.wait_ge(s_de, i * FT + (f + 1 - ACC))
                    product("down", f, a)
                for q in range(4):
                    a_, half = q // 2, q % 2
                    pe.wait_ge(s_de, i * FT + (4 * half + 4) if a_ == 0 else i * FT + FT)
                    pe.wait_ge(s_xte, i * 4 + (4 + q + 1))
                    for k in range(4):
                        last = pe.transpose(tr[q][0:HALF, k * P:(k + 1) * P],
                                            yT[:, 4 * half + k, a_ * HALF:(a_ + 1) * HALF], ident[:, :])
                    last.then_inc(s_yt, 1)

        @block.vector
        def _(dve):
            n = count_of(dve)
            for j in range(3):
                dve.wait_ge(s_bt, j + 1)
                dve.tensor_scalar(bT[:, j, :, :], tr[j][:, 0:FT * N_EXP].rearrange("p (f e) -> p f e", e=N_EXP),
                                  WS if j == 0 else 1.0, None, ALU.mult).then_inc(s_bte, 1)
            dve.wait_ge(s_bte, 3)
            for m in ("gate", "up"):
                for q in range(QN):
                    split_lo(dve, m, 0, q)

            with dve.Fori(0, n) as i:
                e = expert_of(dve, i)
                dve.wait_ge(s_de, i * FT)
                dve.tensor_copy(be[:, :, :], bT[:, :, :, bass.ds(e, 1)].rearrange("p j f o -> p j (f o)")).then_inc(s_be, 1)
                dve.wait_ge(s_be, i + 1)
                for f in range(FT):
                    dve.wait_ge(s_m["gate"], i * FT + (f + 1))
                    dve.tensor_scalar(g[:, f, :], acc[f % ACC][:, 0:ITEM], be[:, 0, f:f + 1], LIMIT * WS,
                                      ALU.add, ALU.min).then_inc(s_ge, 1)
                    if f % 2 == 1:
                        split_lo(dve, "down", i, f // 2)
                dve.wait_ge(s_sg, i + 1)
                dve.tensor_tensor(g[:, :, :], g[:, :, :], sg[:, :, :], ALU.mult).then_inc(s_gs, 1)
                dve.wait_ge(s_gs, i + 1)
                for h in range(FT // 2):
                    ch = Chain(dve, s_dv, base=i * (FT // 2) + h)
                    pair = slice(2 * h, 2 * h + 2)
                    dve.wait_ge(s_ue, i * FT + (2 * h + 2))
                    ch.link(dve.tensor_scalar(u[:, pair, :], u[:, pair, :], LIMIT, -LIMIT, ALU.min, ALU.max))
                    dve.scalar_tensor_tensor(out=g[:, pair, :], in0=u[:, pair, :], scalar=1.0, in1=g[:, pair, :],
                                             op0=ALU.add, op1=ALU.mult).then_inc(s_ag, 1)
                    split_lo(dve, "gate", i + 1, h)
                    dve.wait_ge(s_ah, i * (FT // 2) + (h + 1))
                    dve.scalar_tensor_tensor(out=a[:, pair, 1, :], in0=g[:, pair, :], scalar=1.0 / WS,
                                             in1=a[:, pair, 0, :], op0=ALU.mult, op1=ALU.subtract).then_inc(s_a, 1)
                for q in range(QN):
                    split_lo(dve, "up", i + 1, q)
                dve.wait_ge(s_y, i * 16)
                for q in range(4):
                    a_, half = q // 2, q % 2
                    dve.wait_ge(s_yt, i * 4 + (q + 1))
                    dve.tensor_copy(yr[:, a_, half * 512:(half + 1) * 512], tr[q][0:HALF, :]).then_inc(s_yte, 1)

        @block.scalar
        def _(act):
            n = count_of(act)

            def take_rows(i, q):
                act.wait_ge(s_xt, i * 4 + (q + 1))
                act.copy(xT[:, 2 * q:2 * q + 2, :, :], tr[q][:, :].bitcast(F16)[:, 0:4 * ITEM]
                         .rearrange("p (k c t) -> p k c t", k=2, c=2)).then_inc(s_xte, 1)

            for q in range(QN):
                split_hi(act, "gate", 0, 0, q)
            for q in range(QN):
                split_hi(act, "up", 0, 1, q)
            for q in range(4):
                take_rows(0, q)
            with act.Fori(0, n) as i:
                for q in range(QN):
                    split_hi(act, "down", i, i * 3 + 2, q)
                act.wait_ge(s_ge, i * FT + FT)
                act.activation(sg[:, :, :], g[:, :, :], ACT.Sigmoid, scale=ALPHA / WS).then_inc(s_sg, 1)
                act.wait_ge(s_be, i + 1)

                def whole(h):
                    act.wait_ge(s_ag, i * (FT // 2) + (h + 1))
                    act.activation(a[:, 2 * h:2 * h + 2, 0, :], g[:, 2 * h:2 * h + 2, :], ACT.Copy,
                                   scale=1.0 / WS).then_inc(s_ah, 1)

                act.wait_ge(s_m["down"], i * FT)
                for f in range(FT):
                    act.wait_ge(s_m["up"], i * FT + (f + 1))
                    act.activation(u[:, f, :], acc[f % ACC][:, 0:ITEM], ACT.Identity, bias=be[:, 1, f:f + 1],
                                   scale=1.0 / WS).then_inc(s_ue, 1)
                    if f % 2 == 1:
                        if f >= 3:
                            whole(f // 2 - 1)
                        split_hi(act, "gate", i + 1, i * 3 + 3, f // 2)
                whole(FT // 2 - 1)
                for q in range(4):
                    take_rows(i + 1, q)
                for f in range(KT):
                    act.wait_ge(s_m["down"], i * FT + (f + 1))
                    act.wait_ge(s_yt, i * 4)
                    act.activation(yT[:, f, :], acc[f % ACC][:, 0:ITEM], ACT.Identity,
                                   bias=be[:, 2, f:f + 1], scale=1.0 / WS).then_inc(s_de, 1)
                    if f % 2 == 1:
                        split_hi(act, "up", i + 1, i * 3 + 4, f // 2)


def stage_combine(nc, io, out, scr):
    OT = SEQ // P
    used = []
    with ExitStack() as ctx:
        def sb(name, shape, dt=F32):
            return ctx.enter_context(nc.sbuf_tensor(name, shape, dt))

        def sem(name):
            used.append(ctx.enter_context(nc.semaphore(name)))
            return used[-1]

        g_bc = sb("c_g_bc", [P, D])
        slot = sb("c_slot", [P, OT, TOP], U32)
        gate = sb("c_gate", [P, OT, TOP])
        yg = sb("c_yg", [P, 2, TOP, D])
        hr = sb("c_hr", [P, 2, D])
        sq = sb("c_sq", [P, D])
        st = sb("c_st", [P, 2, 4])
        res = sb("c_res", [P, 2, D])
        s_in = sem("c_tables_landed")
        s_h = [sem(f"c_h_landed{b}") for b in range(2)]
        s_y = [sem(f"c_rows_gathered{b}") for b in range(2)]
        s_acc = sem("c_sum_chain")
        s_sum = sem("c_sum_ready")
        s_sq = sem("c_squares_ready")
        s_var = sem("c_variance_ready")
        s_ln = sem("c_log_ready")
        s_rs = sem("c_rstd_ready")
        s_res = sem("c_result_ready")
        s_out = [sem(f"c_result_stored{b}") for b in range(2)]
        block = ctx.enter_context(nc.Block())

        @block.sync
        def _(sp):
            sp.dma_start(g_bc[:, :], io["final_norm_g"].partition_broadcast(P)).then_inc(s_in, 16)
            sp.dma_start(slot[:, :, :], scr["slot"][N_META:L, :].rearrange("(t p) c -> p t c", p=P)).then_inc(s_in, 16)
            sp.dma_start(gate[:, :, :], scr["gate"][N_META:L, :].rearrange("(t p) c -> p t c", p=P)).then_inc(s_in, 16)
            sp.dma_start(hr[:, 0, :], scr["h2"][N_META:N_META + P, :]).then_inc(s_h[0], 16)
            for t in range(OT):
                if t + 1 < OT:
                    if t >= 1:
                        sp.wait_ge(s_res, t)
                    sp.dma_start(hr[:, (t + 1) % 2, :],
                                 scr["h2"][N_META + (t + 1) * P:N_META + (t + 2) * P, :]).then_inc(s_h[(t + 1) % 2], 16)
                sp.wait_ge(s_res, t + 1)
                sp.dma_start(out[0, t * P:(t + 1) * P, :], res[:, t % 2, :]).then_inc(s_out[t % 2], 16)
            for b in range(2):
                sp.wait_ge(s_out[b], 16 * OT // 2)

        @block.gpsimd
        def _(pool):
            pool.wait_ge(s_in, 48)
            for t in range(OT):
                if t >= 2:
                    pool.wait_ge(s_sum, t - 1)
                for c in range(TOP):
                    pool.indirect_dma_start(out=yg[:, t % 2, c, :], out_offset=None, in_=scr["y"],
                                            in_offset=bass.IndirectOffsetOnAxis(ap=slot[:, t, c:c + 1], axis=0)
                                            ).then_inc(s_y[t % 2], 16)

        @block.vector
        def _(dve):
            ch = Chain(dve, s_acc)
            dve.wait_ge(s_in, 48)
            for t in range(OT):
                b = t % 2
                dve.wait_ge(s_h[b], 16 * (t // 2 + 1))
                dve.wait_ge(s_y[b], 16 * TOP * (t // 2 + 1))
                for c in range(TOP):
                    ins = dve.scalar_tensor_tensor(out=hr[:, b, :], in0=yg[:, b, c, :], scalar=gate[:, t, c:c + 1],
                                                   in1=hr[:, b, :], op0=ALU.mult, op1=ALU.add)
                    if c < TOP - 1:
                        ch.link(ins)
                    else:
                        ins.then_inc(s_sum, 1)
                dve.wait_ge(s_sq, t + 1)
                dve.tensor_scalar(st[:, b, 1:2], st[:, b, 0:1], 1.0 / D, EPS, ALU.mult, ALU.add).then_inc(s_var, 1)
                dve.wait_ge(s_rs, t + 1)
                if t >= 2:
                    dve.wait_ge(s_out[b], 16 * (t // 2))
                dve.scalar_tensor_tensor(out=res[:, b, :], in0=hr[:, b, :], scalar=st[:, b, 3:4], in1=g_bc[:, :],
                                         op0=ALU.mult, op1=ALU.mult).then_inc(s_res, 1)

        @block.scalar
        def _(act):
            for t in range(OT):
                b = t % 2
                act.wait_ge(s_sum, t + 1)
                if t:
                    act.wait_ge(s_sq, t)
                act.activation(sq[:, :], hr[:, b, :], ACT.Square, accum_out=st[:, b, 0:1]).then_inc(s_sq, 1)
                act.wait_ge(s_var, t + 1)
                act.activation(st[:, b, 2:3], st[:, b, 1:2], ACT.Ln).then_inc(s_ln, 1)
                act.wait_ge(s_ln, t + 1)
                act.activation(st[:, b, 3:4], st[:, b, 2:3], ACT.Exp, scale=-0.5).then_inc(s_rs, 1)


def hybrid_layer(nc, io, out, scr):
    with ExitStack() as ctx:
        ident = ctx.enter_context(nc.sbuf_tensor("ident", [P, P], F32))
        ident16 = ctx.enter_context(nc.sbuf_tensor("ident16", [P, P], F16))
        items = ctx.enter_context(nc.sbuf_tensor("items", [1, ITEMS + 1], I32))
        n_items = ctx.enter_context(nc.sbuf_tensor("n_items", [1, 1], I32))
        s_c = ctx.enter_context(nc.semaphore("constants"))
        with nc.Block() as block:
            @block.gpsimd
            def _(pool):
                pool.memset(ident[:, :], 0.0).then_inc(s_c, 1)
                pool.wait_ge(s_c, 1)
                pool.affine_select(out=ident[:, :], in_=ident[:, :], compare_op=ALU.not_equal, fill=1.0,
                                   base=0, pattern=[[-1, P]], channel_multiplier=1).then_inc(s_c, 1)
                pool.wait_ge(s_c, 2)
                pool.tensor_copy(ident16[:, :], ident[:, :]).then_inc(s_c, 1)
        with nc.sbuf_tensor("xnT", [P, KT, LP], F32) as xnT:
            clear(nc, stage_project(nc, io, scr, ident, xnT))
            clear(nc, stage_attention(nc, io, scr, ident, xnT))
        stage_hgrn(nc, io, scr, ident)
        stage_merge(nc, io, scr, ident)
        stage_route(nc, io, scr, items, n_items)
        stage_experts(nc, io, scr, ident, ident16, items, n_items)
        stage_combine(nc, io, out, scr)


SCRATCH = {
    "h": ((LP, D), F32), "proj": ((LP, IN_COLS), F32), "att": ((LP, ATT_HEADS * HD), F32), "hgr": ((LP, HGW), F32),
    "h2": ((LP, D), F32), "xn": ((LP, 2 * D), F16), "logits": ((LP, N_EXP), F32), "gate": ((LP, TOP), F32),
    "slot": ((LP, TOP), U32), "token": ((TABLE, 1), I32), "y": ((SLOTS, D), F32),
}


def build(nc, shapes):
    io = {n: nc.dram_tensor(f"in_{n}", s, F32, kind="ExternalInput").ap() for n, s in shapes.items()}
    out = nc.dram_tensor("out_0", (1, SEQ, D), F32, kind="ExternalOutput").ap()
    scr = {n: nc.dram_tensor(f"scratch_{n}", s, dt, kind="Internal").ap() for n, (s, dt) in SCRATCH.items()}
    hybrid_layer(nc, io, out, scr)


_INS = ["x", "meta_tokens", "attn_norm_g", "w_in", "hgrn_norm_g", "w_up_attn", "w_up_hgrn", "w_out",
        "hgrn_lb_logits", "ffn_norm_g", "router_w", "router_b", "w_gate", "b_gate", "w_up", "b_up",
        "w_down", "b_down", "final_norm_g"]


def extra_inputs(inputs):
    return {**inputs, "rope": rope_tables()}


def kernel(**inputs):
    import concourse.bacc as _bacc
    from concourse.bass_utils import run_bass_kernel_spmd as _run

    arrays = {n: np.ascontiguousarray(inputs[n]) for n in _INS}
    arrays["rope"] = rope_tables()
    nc = _bacc.Bacc("TRN2", target_bir_lowering=False, num_devices=1)
    build(nc, {n: a.shape for n, a in arrays.items()})
    r = _run(nc, [{f"in_{n}": a for n, a in arrays.items()}], core_ids=[0])
    return r.results[0]["out_0"]
```

```python
from contextlib import ExitStack

import numpy as np

import concourse.bass as bass
from concourse import mybir

F32 = mybir.dt.float32
I32 = mybir.dt.int32
U32 = mybir.dt.uint32
F16 = mybir.dt.float16
ALU = mybir.AluOpType
ACT = mybir.ActivationFunctionType
AX = mybir.AxisListType

P = 128
D = 1024
KT = D // P
SEQ, N_META = 1024, 16
L = SEQ + N_META
NT = -(-L // P)
LP = NT * P
FRONT = LP - L
OT = NT - 1
assert SEQ == OT * P
EPS = 1e-5

ATT_HEADS, KV_HEADS, HD = 8, 2, 64
IDX_HEADS, IDX_DIM = 8, 32
QK_HEADS = ATT_HEADS + KV_HEADS
C_Q = 0
C_K = C_Q + ATT_HEADS * HD
C_V = C_K + KV_HEADS * HD
C_IQ = C_V + KV_HEADS * HD
C_IK = C_IQ + IDX_HEADS * IDX_DIM
C_IW = C_IK + IDX_DIM
C_HQ = C_IW + IDX_HEADS
HG_HEADS, HG_D = 4, 128
HGW = HG_HEADS * HG_D
C_HF, C_HI, C_HG = C_HQ + HGW, C_HQ + 2 * HGW, C_HQ + 3 * HGW
C_GA = C_HG + HGW
C_GH = C_GA + D
IN_COLS = C_GH + D
CHUNKS = 4
CW = C_HQ // CHUNKS
FW = 512
FCHUNKS = (IN_COLS - C_HQ) // FW
assert CW * CHUNKS == C_HQ and FW * FCHUNKS == IN_COLS - C_HQ

IDX_SCALE = float(IDX_DIM ** -0.5) * float(IDX_HEADS ** -0.5)
ATT_SCALE = float(HD) ** -0.5
K_SEL = min(256, L // 4)
ROUNDS = K_SEL // 8
MASKED = -3.0e38
TAKEN = -3.3e38
SPLIT = -3.15e38
DROP = -1.0e30

ROT, IROT = HD // 4, IDX_DIM // 4
N_EXP = 32
TOP = 4
HALF = 80
ITEM = 2 * HALF
MORE = TOP * L // ITEM
ITEMS = N_EXP + MORE
SLOTS = ITEMS * ITEM
TABLE = -(-(SLOTS + ITEM) // P) * P
ZERO_P, ZERO_DMAS = 104, NT - 1
ZERO_N = MORE * ITEM // ZERO_P // ZERO_DMAS
assert ZERO_N * ZERO_P * ZERO_DMAS == MORE * ITEM
TAB = 2 * QK_HEADS * (ROT // 2) + 2 * (IDX_HEADS + 1) * (IROT // 2)


def rope_tables():
    pos = np.maximum(np.arange(LP, dtype=np.float32) - np.float32(FRONT), np.float32(0))
    parts = []
    for rot, heads in ((ROT, QK_HEADS), (IROT, IDX_HEADS + 1)):
        half = rot // 2
        inv = np.float32(500000.0) ** (-np.arange(half, dtype=np.float32) * np.float32(2.0) / np.float32(rot))
        ang = (pos[:, None] * inv[None, :].astype(np.float32)).astype(np.float32)
        for f in (np.cos, np.sin):
            parts.append(np.tile(f(ang).astype(np.float32), (1, heads)))
    return np.concatenate(parts, axis=1)


class Chain:

    def __init__(self, eng, sem, base=0):
        self.eng, self.sem, self.base, self.n = eng, sem, base, 0

    def link(self, ins):
        self.n += 1
        ins.then_inc(self.sem, 1)
        self.eng.wait_ge(self.sem, self.base + self.n)


def clear(nc, sems):
    with nc.Block() as block:
        @block.gpsimd
        def _(pool):
            for s in sems:
                pool.sem_clear(s)


def stage_project(nc, io, scr, ident, xnT):
    used = []
    with ExitStack() as ctx:
        def sb(name, shape, dt=F32):
            return ctx.enter_context(nc.sbuf_tensor(name, shape, dt))

        def sem(name):
            used.append(ctx.enter_context(nc.semaphore(name)))
            return used[-1]

        h_rows = sb("p_h_rows", [P, NT, D])
        g_bc = sb("p_g_bc", [P, D])
        ssq = sb("p_ssq", [P, NT])
        ms = sb("p_ms", [P, NT])
        rms = sb("p_rms", [P, NT])
        rstd = sb("p_rstd", [P, NT])
        xn = sb("p_xn", [P, 2, D])
        w = sb("p_w", [P, 2, KT, CW])
        NB = 6
        stage = sb("p_stage", [P, NB, CW])
        tp = ctx.enter_context(nc.psum_tensor("p_tp", [P, 2, 512], F32))
        acc = ctx.enter_context(nc.psum_tensor("p_acc", [P, NB, 512], F32))

        s_zero = sem("p_zeroed")
        s_h = sem("p_h_landed")
        s_g = sem("p_g_landed")
        s_hout = sem("p_h_stored")
        s_ssq = sem("p_ssq_ready")
        s_stat = sem("p_stat_chain")
        s_ms = sem("p_ms_ready")
        s_rms = sem("p_rms_ready")
        s_xn = sem("p_xn_ready")
        s_tp = sem("p_tp_ready")
        s_tpa = sem("p_tp_taken_act")
        s_tpv = sem("p_tp_taken_dve")
        s_w = [nc.alloc_semaphore(f"p_w_landed{b}") for b in range(2)]
        s_mm = sem("p_product_ready")
        s_eva = sem("p_evacuated_act")
        s_evv = sem("p_evacuated_dve")
        s_st = [sem(f"p_stored{b}") for b in range(NB)]

        w_in = io["w_in"][0].rearrange("(kt p) n -> p kt n", p=P)
        x = io["x"][0]
        block = ctx.enter_context(nc.Block())

        @block.sync
        def _(sp):
            sp.dma_start(g_bc[:, :], io["attn_norm_g"].partition_broadcast(P)).then_inc(s_g, 16)
            sp.wait_ge(s_zero, 1)
            sp.dma_start(h_rows[FRONT:P, 0, :], io["meta_tokens"]).then_inc(s_h, 16)
            sp.dma_start(h_rows[:, 1:NT, :],
                         x.rearrange("(t p) d -> p t d", p=P)).then_inc(s_h, 16)
            sp.wait_ge(s_h, 32)
            sp.dma_start(scr["h"].rearrange("(t p) d -> p t d", p=P), h_rows[:, :, :]).then_inc(s_hout, 16)
            with sp.Fori(0, CHUNKS // 2) as c2:
                for u in range(2):
                    for t in range(NT):
                        n = u * NT + t
                        b = n % NB
                        if n % 2 == 0:
                            sp.wait_ge(s_eva, c2 * NT + (n // 2 + 1))
                        else:
                            sp.wait_ge(s_evv, c2 * NT + (n // 2 + 1))
                        sp.dma_start(scr["proj"][t * P:(t + 1) * P, bass.ds(c2 * (2 * CW) + u * CW, CW)],
                                     stage[:, b, :]).then_inc(s_st[b], 16)
            for b in range(NB):
                sp.wait_ge(s_st[b], 16 * (CHUNKS * NT // NB))
            sp.wait_ge(s_hout, 16)

        @block.gpsimd
        def _(pool):
            pool.dma_start(w[:, 0, :, :], w_in[:, :, 0:CW]).then_inc(s_w[0], 16)
            pool.dma_start(w[:, 1, :, :], w_in[:, :, CW:2 * CW]).then_inc(s_w[1], 16)
            with pool.Fori(1, CHUNKS // 2) as c2:
                for u in range(2):
                    pool.wait_ge(s_mm, (c2 - 1) * (2 * NT) + (u + 1) * NT)
                    pool.dma_start(w[:, u, :, :], w_in[:, :, bass.ds(c2 * (2 * CW) + u * CW, CW)]).then_inc(s_w[u], 16)

        @block.scalar
        def _(act):
            act.wait_ge(s_h, 32)
            for t in range(NT):
                if t >= 2:
                    act.wait_ge(s_ssq, t - 1)
                act.activation(xn[:, t % 2, :], h_rows[:, t, :], ACT.Square,
                               accum_out=ssq[:, t:t + 1]).then_inc(s_ssq, 1)
            act.wait_ge(s_ms, 1)
            act.activation(rms[:, :], ms[:, :], ACT.Sqrt).then_inc(s_rms, 1)
            for t in range(NT):
                act.wait_ge(s_tp, 2 * t + 1)
                act.copy(xnT[:, 0:4, t * P:(t + 1) * P],
                         tp[:, 0, :].rearrange("p (k t) -> p k t", k=4)).then_inc(s_tpa, 1)
            with act.Fori(0, CHUNKS // 2) as c2:
                for n in range(0, 2 * NT, 2):
                    b = n % NB
                    act.wait_ge(s_mm, c2 * (2 * NT) + (n + 1))
                    if n >= NB:
                        act.wait_ge(s_st[b], c2 * (16 * 2 * NT // NB) + 16 * (n // NB))
                    else:
                        act.wait_ge(s_st[b], c2 * (16 * 2 * NT // NB))
                    act.copy(stage[:, b, :], acc[:, b, 0:CW]).then_inc(s_eva, 1)

        @block.vector
        def _(dve):
            dve.memset(h_rows[:, 0, :], 0.0).then_inc(s_zero, 1)
            dve.wait_ge(s_ssq, NT)
            dve.tensor_scalar(ms[:, :], ssq[:, :], 1.0 / D, EPS, ALU.mult, ALU.add).then_inc(s_ms, 1)
            dve.wait_ge(s_rms, 1)
            dve.reciprocal(rstd[:, :], rms[:, :]).then_inc(s_stat, 1)
            dve.wait_ge(s_stat, 1)
            dve.wait_ge(s_g, 16)

            def evacuate(t):
                dve.wait_ge(s_tp, 2 * t + 2)
                dve.tensor_copy(xnT[:, 4:8, t * P:(t + 1) * P],
                                tp[:, 1, :].rearrange("p (k t) -> p k t", k=4)).then_inc(s_tpv, 1)

            for t in range(NT):
                if t >= 2:
                    evacuate(t - 2)
                dve.scalar_tensor_tensor(out=xn[:, t % 2, :], in0=h_rows[:, t, :], scalar=rstd[:, t:t + 1],
                                         in1=g_bc[:, :], op0=ALU.mult, op1=ALU.mult).then_inc(s_xn, 1)
            evacuate(NT - 2)
            evacuate(NT - 1)
            with dve.Fori(0, CHUNKS // 2) as c2:
                for n in range(1, 2 * NT, 2):
                    b = n % NB
                    dve.wait_ge(s_mm, c2 * (2 * NT) + (n + 1))
                    if n >= NB:
                        dve.wait_ge(s_st[b], c2 * (16 * 2 * NT // NB) + 16 * (n // NB))
                    else:
                        dve.wait_ge(s_st[b], c2 * (16 * 2 * NT // NB))
                    dve.tensor_copy(stage[:, b, :], acc[:, b, 0:CW]).then_inc(s_evv, 1)

        @block.tensor
        def _(pe):
            for t in range(NT):
                pe.wait_ge(s_xn, t + 1)
                for half, taken in ((0, s_tpa), (1, s_tpv)):
                    if t >= 1:
                        pe.wait_ge(taken, t)
                    for j in range(4):
                        k = half * 4 + j
                        last = pe.transpose(tp[:, half, j * P:(j + 1) * P], xn[:, t % 2, k * P:(k + 1) * P],
                                            ident[:, :])
                    last.then_inc(s_tp, 1)
            pe.wait_ge(s_tpa, NT)
            pe.wait_ge(s_tpv, NT)
            with pe.Fori(0, CHUNKS // 2) as c2:
                for u in range(2):
                    pe.wait_ge(s_w[u], c2 * 16 + 16)
                    for t in range(NT):
                        n = u * NT + t
                        b = n % NB
                        if n % 2 == 0:
                            pe.wait_ge(s_eva, c2 * NT + max(0, n // 2 + 1 - NB // 2)) if n >= NB else \
                                pe.wait_ge(s_eva, c2 * NT)
                        else:
                            pe.wait_ge(s_evv, c2 * NT + max(0, n // 2 + 1 - NB // 2)) if n >= NB else \
                                pe.wait_ge(s_evv, c2 * NT)
                        for k in range(KT):
                            last = pe.matmul(acc[:, b, 0:CW], xnT[:, k, t * P:(t + 1) * P], w[:, u, k, :],
                                             start=(k == 0), stop=(k == KT - 1))
                        last.then_inc(s_mm, 1)
    return used


def stage_attention(nc, io, scr, ident, xnT):
    W = [P * (i + 1) - FRONT for i in range(NT)]
    ZW = P * (NT - 1)
    used = []
    with ExitStack() as ctx:
        def sb(name, shape, dt=F32):
            return ctx.enter_context(nc.sbuf_tensor(name, shape, dt))

        def sem(name):
            used.append(ctx.enter_context(nc.semaphore(name)))
            return used[-1]

        tab = sb("a_tab", [P, NT, TAB])
        rows = sb("a_rows", [P, 2, C_HQ])
        t1 = sb("a_t1", [P, 4, QK_HEADS * ROT // 2])
        t2 = sb("a_t2", [P, 4, (IDX_HEADS + 1) * IROT // 2])
        ik4 = sb("a_ik4", [P, 2, 4 * IDX_DIM])
        qpair = sb("a_qpair", [P, 2, 4, 2, HD])
        iws = sb("a_iws", [P, NT, IDX_HEADS])
        keyT = sb("a_keyT", [P, LP])
        ikT = sb("a_ikT", [P, LP])
        val = sb("a_val", [P, NT, KV_HEADS * HD])
        qT = sb("a_qT", [P, 2, ATT_HEADS, P])
        iqT = sb("a_iqT", [P, 2, IDX_HEADS, P])
        start = sb("a_start", [P, ZW + P])
        rel = sb("a_rel", [P, 2, L])
        score = sb("a_score", [P, 2, L])
        top8 = sb("a_top8", [P, 8])
        drop = sb("a_drop", [P, L])
        lg = sb("a_lg", [P, 2, LP])
        mx = sb("a_mx", [P, 2, ATT_HEADS])
        nmx = sb("a_nmx", [P, 2, ATT_HEADS])
        rsum = sb("a_rsum", [P, 2, ATT_HEADS])
        rinv = sb("a_rinv", [P, ATT_HEADS])
        pT = sb("a_pT", [P, 2, NT, P])
        att = sb("a_att", [P, 2, ATT_HEADS * HD])
        fw = sb("a_fw", [P, 2, KT, FW])
        FST = 3
        fst = sb("a_fst", [P, FST, FW])
        ps_x = ctx.enter_context(nc.psum_tensor("a_ps_x", [P, 3, 512], F32))
        ps_l = ctx.enter_context(nc.psum_tensor("a_ps_l", [P, 3, 512], F32))
        ps_t = ctx.enter_context(nc.psum_tensor("a_ps_t", [P, 512], F32))
        ps_o = ctx.enter_context(nc.psum_tensor("a_ps_o", [P, 512], F32))

        s_tab = sem("a_tab_landed")
        s_pad = sem("a_padding_zeroed")
        s_row = [sem(f"a_rows_landed{b}") for b in range(2)]
        s_mask = sem("a_mask_ready")
        s_rope = sem("a_rope_done")
        s_copy = sem("a_value_and_ik_copied")
        s_t = sem("a_transposes_ready")
        s_te = sem("a_transposes_taken")
        s_x = sem("a_index_product_ready")
        s_relu = sem("a_relu_ready")
        s_acc = sem("a_score_added")
        s_dv = sem("a_dve_chain")
        s_l = sem("a_logit_product_ready")
        s_lm = sem("a_logit_masked")
        s_nm = sem("a_negmax_ready")
        s_exp = sem("a_exp_ready")
        s_pv = sem("a_pv_done")
        s_att = sem("a_att_ready")
        s_out = [sem(f"a_att_stored{b}") for b in range(2)]
        s_zs = sem("a_zeros_stored")

        s_fw = [nc.alloc_semaphore(f"a_fill_w_landed{b}") for b in range(2)]
        s_fm = sem("a_fill_product_ready")
        s_fe = sem("a_fill_product_taken")
        s_fs = [nc.alloc_semaphore(f"a_fill_stored{b}") for b in range(FST)]

        unit_at = [(c, t) for c in range(FCHUNKS) for t in range(NT) if t or C_HQ + c * FW < C_GA]
        UNITS = len(unit_at)
        room, ends = {}, {}
        for i in range(1, NT):
            for h in range(ATT_HEADS):
                for place in range(3):
                    room[i, h, place] = 0
            if W[i] > K_SEL:
                lasts = ROUNDS * 2 * (W[i] / 0.96 + 200) - (11000 + 5 * W[i] if i < NT - 1 else 2000)
                room[i, 0, 0] = int(lasts / (1000 if i == NT - 2 else 900))
            else:
                room[i, 0, 0] = 3 * KT
        rest = UNITS * KT - sum(room.values())
        assert rest >= 0
        heads = list(room)
        weight = [W[i] + 400 for i, h, place in heads]
        done = 0
        for j, key in enumerate(heads):
            upto = round(rest * sum(weight[:j + 1]) / sum(weight))
            room[key] += upto - done
            done = upto
        odd = sum(n for (i, h, place), n in room.items() if i < NT - 1) % KT
        room[NT - 2, ATT_HEADS - 1, 2] += KT - odd
        room[NT - 1, 0, 0] -= KT - odd
        made = 0
        for key in heads:
            for _ in range(room[key]):
                if made % KT == KT - 1:
                    ends.setdefault(key, []).append(made // KT)
                made += 1
        assert made == UNITS * KT

        def ended(i):
            return [u for (j, h, place), units in ends.items() if j == i for u in units]

        first_a_only = min(ended(NT - 2))
        first_last = min(ended(NT - 1))

        def fill_place(u):
            return ("x", u % 2) if u >= first_last else ("x", 2) if u % 2 and u < first_a_only else ("l", 2)

        def fill_bank(u):
            name, b = fill_place(u)
            return (ps_x if name == "x" else ps_l)[:, b, :]

        def fill_before(u):
            for v in range(u - 1, -1, -1):
                if fill_place(v) == fill_place(u):
                    return v + 1
            return 0

        number = {}
        for i in range(-1, NT):
            if i + 1 < NT:
                number["q", i + 1] = len(number)
                number["k", i + 1] = len(number)
            if i >= 1:
                for h in range(ATT_HEADS):
                    for g in range(-(-(i + 1) // 4)):
                        number["p", i, h, g] = len(number)

        block = ctx.enter_context(nc.Block())

        def store(sp, i):
            sp.wait_ge(s_att, i)
            sp.dma_start(scr["att"][i * P:(i + 1) * P, :], att[:, i % 2, :]).then_inc(s_out[i % 2], 16)

        @block.sync
        def _(sp):
            sp.dma_start(tab[:, :, :], io["rope"].rearrange("(t p) c -> p t c", p=P)).then_inc(s_tab, 16)
            for i in range(NT):
                if i >= 2:
                    sp.wait_ge(s_t, number["k", i - 2] + 1)
                    sp.wait_ge(s_copy, 4 * (i - 1))
                sp.dma_start(rows[:, i % 2, :], scr["proj"][i * P:(i + 1) * P, 0:C_HQ]).then_inc(s_row[i % 2], 16)
                if i >= 4:
                    store(sp, i - 3)
                if i < ZERO_DMAS:
                    if i == 0:
                        sp.wait_ge(s_mask, 1)
                    r0 = N_EXP * ITEM + i * ZERO_P * ZERO_N
                    sp.dma_start(scr["y"][r0:r0 + ZERO_P * ZERO_N, :].rearrange("(p n) d -> p n d", p=ZERO_P),
                                 start[0:ZERO_P, 0:D].unsqueeze(1).to_broadcast([ZERO_P, ZERO_N, D])).then_inc(s_zs, 16)
            for i in range(NT - 3, NT):
                store(sp, i)
            sp.wait_ge(s_zs, 16 * ZERO_DMAS)
            for b in range(2):
                sp.wait_ge(s_out[b], 16 * len(range(2 - b, NT, 2)))

        @block.gpsimd
        def _(pool):
            w_in = io["w_in"][0].rearrange("(kt p) n -> p kt n", p=P)

            def load_chunk(c):
                pool.dma_start(fw[:, c % 2, :, :], w_in[:, :, C_HQ + c * FW:C_HQ + (c + 1) * FW]).then_inc(s_fw[c % 2], 16)

            def store_unit(u):
                c, t = unit_at[u]
                pool.wait_ge(s_fe, u + 1)
                pool.dma_start(scr["proj"][t * P:(t + 1) * P, C_HQ + c * FW:C_HQ + (c + 1) * FW],
                               fst[:, u % FST, :]).then_inc(s_fs[u % FST], 16)
                if t == NT - 1 and c + 2 < FCHUNKS:
                    load_chunk(c + 2)

            load_chunk(0)
            load_chunk(1)
            pool.memset(qT[:, :, :, :], 0.0).then_inc(s_pad, 1)
            pool.memset(iqT[:, :, :, :], 0.0).then_inc(s_pad, 1)
            pool.memset(lg[:, :, 0:FRONT], 0.0).then_inc(s_pad, 1)
            pool.memset(start[:, :], 0.0).then_inc(s_mask, 1)
            pool.wait_ge(s_mask, 1)
            pool.affine_select(out=start[:, ZW:], in_=start[:, ZW:], compare_op=ALU.is_ge, fill=MASKED,
                               base=0, pattern=[[-1, P]], channel_multiplier=1).then_inc(s_mask, 1)
            for i in range(NT):
                pool.wait_ge(s_rope, i + 1)
                pool.tensor_copy(val[:, i, :], rows[:, i % 2, C_V:C_IQ]).then_inc(s_copy, 1)
                if i >= 2:
                    pool.wait_ge(s_t, number["k", i - 2] + 1)
                ik = rows[:, i % 2, C_IK:C_IW].unsqueeze(1).to_broadcast([P, 4, IDX_DIM])
                pool.tensor_copy(ik4[:, i % 2, :].rearrange("p (r d) -> p r d", r=4), ik).then_inc(s_copy, 1)
                for g in range(KV_HEADS):
                    pool.tensor_copy(qpair[:, i % 2, :, g, :],
                                     rows[:, i % 2, g * 4 * HD:(g + 1) * 4 * HD].rearrange("p (m d) -> p m d", d=HD)
                                     ).then_inc(s_copy, 1)
                for u in ended(i - 1):
                    store_unit(u)
            for u in ended(NT - 1):
                store_unit(u)
            for b in range(FST):
                pool.wait_ge(s_fs[b], 16 * len(range(b, UNITS, FST)))

        @block.vector
        def _(dve):
            ch = Chain(dve, s_dv)

            def rope(i):
                dve.wait_ge(s_row[i % 2], 16 * (i // 2 + 1))
                if i:
                    dve.wait_ge(s_rope, i)
                parts = []
                c0 = 0
                for heads, d, half, base, t in ((QK_HEADS, HD, ROT // 2, C_Q, t1),
                                                (IDX_HEADS + 1, IDX_DIM, IROT // 2, C_IQ, t2)):
                    n = heads * half
                    v = rows[:, i % 2, base:base + heads * d].rearrange("p (h d) -> p h d", d=d) \
                        if base == C_IQ else rows[:, i % 2, 0:heads * d].rearrange("p (h d) -> p h d", d=d)
                    co = tab[:, i, c0:c0 + n].rearrange("p (h d) -> p h d", d=half)
                    si = tab[:, i, c0 + n:c0 + 2 * n].rearrange("p (h d) -> p h d", d=half)
                    c0 += 2 * n
                    tv = [t[:, j, :].rearrange("p (h d) -> p h d", d=half) for j in range(4)]
                    parts.append((v[:, :, 0:half], v[:, :, half:2 * half], co, si, tv))
                for x1, x2, co, si, tv in parts:
                    dve.tensor_tensor(tv[0], x1, co, ALU.mult)
                    dve.tensor_tensor(tv[1], x2, si, ALU.mult)
                    dve.tensor_tensor(tv[2], x2, co, ALU.mult)
                    last = dve.tensor_tensor(tv[3], x1, si, ALU.mult)
                ch.link(last)
                for x1, x2, co, si, tv in parts:
                    dve.tensor_tensor(x1, tv[0], tv[1], ALU.subtract)
                    dve.tensor_tensor(x2, tv[2], tv[3], ALU.add)
                dve.tensor_scalar(iws[:, i, :], rows[:, i % 2, C_IW:C_HQ], IDX_SCALE, None,
                                  ALU.mult).then_inc(s_rope, 1)

            def add_head(i, h):
                n = IDX_HEADS * (i - 1) + h
                w = W[i]
                dve.wait_ge(s_relu, n + 1)
                before = start[:, ZW + P - w:] if h == 0 else score[:, i % 2, 0:w]
                if h:
                    dve.wait_ge(s_acc, n)
                dve.scalar_tensor_tensor(out=score[:, i % 2, 0:w], in0=rel[:, n % 2, 0:w], scalar=iws[:, i, h:h + 1],
                                         in1=before, op0=ALU.mult, op1=ALU.add).then_inc(s_acc, 1)

            def select(i):
                s = score[:, i % 2, 0:W[i]]
                dve.wait_ge(s_acc, IDX_HEADS * i)
                if W[i] > K_SEL:
                    for r in range(ROUNDS):
                        ch.link(dve.max(top8[:, :], s))
                        ch.link(dve.match_replace(s, top8[:, :], s, TAKEN))
                    ch.link(dve.tensor_scalar(drop[:, 0:W[i]], s, SPLIT, DROP, ALU.is_gt, ALU.mult))
                    if P * i - FRONT + 1 < K_SEL:
                        ch.link(dve.tensor_tensor(drop[:, 0:W[i]], drop[:, 0:W[i]], start[:, ZW + P - W[i]:], ALU.min))
                else:
                    ch.link(dve.tensor_scalar(drop[:, 0:W[i]], s, MASKED / 2, DROP, ALU.is_le, ALU.mult))

            def mask_logits(i, h):
                n = ATT_HEADS * (i - 1) + h
                w = W[i]
                dve.wait_ge(s_l, n + 1)
                if n >= 2:
                    dve.wait_ge(s_pv, n - 1)
                dve.tensor_tensor_reduce(lg[:, n % 2, FRONT:FRONT + w], ps_l[:, :, :].rearrange("p b c -> p (b c)")[:, 0:w],
                                         drop[:, 0:w], 1.0, -3.4e38, ALU.add, ALU.max,
                                         mx[:, i % 2, h:h + 1]).then_inc(s_lm, 1)
                dve.wait_ge(s_lm, n + 1)
                dve.tensor_scalar(nmx[:, i % 2, h:h + 1], mx[:, i % 2, h:h + 1], -ATT_SCALE, None,
                                  ALU.mult).then_inc(s_nm, 1)

            def normalize(i):
                dve.wait_ge(s_pv, ATT_HEADS * i)
                ch.link(dve.reciprocal(rinv[:, :], rsum[:, i % 2, :]))
                if i >= 3:
                    dve.wait_ge(s_out[i % 2], 16 * ((i - 1) // 2))
                dve.tensor_tensor(att[:, i % 2, :].rearrange("p (h d) -> p h d", d=HD),
                                  ps_o[:, :].rearrange("p (h d) -> p h d", d=HD),
                                  rinv[:, :].unsqueeze(2).to_broadcast([P, ATT_HEADS, HD]),
                                  ALU.mult).then_inc(s_att, 1)

            dve.wait_ge(s_tab, 16)
            rope(0)
            rope(1)
            dve.wait_ge(s_mask, 2)
            for h in range(IDX_HEADS):
                add_head(1, h)
            for i in range(1, NT):
                if i + 1 < NT:
                    rope(i + 1)
                select(i)
                for h in range(ATT_HEADS):
                    mask_logits(i, h)
                    if i + 1 < NT:
                        add_head(i + 1, h)
                normalize(i)

        @block.scalar
        def _(act):
            def take_rows(i):
                act.wait_ge(s_t, number["q", i] + 1)
                for g in range(KV_HEADS):
                    r = slice(HD * g, HD * (g + 1))
                    last = act.copy(qT[r, i % 2, 4 * g:4 * g + 4, :], ps_t[r, :].rearrange("p (m t) -> p m t", m=4))
                last.then_inc(s_te, 1)
                act.wait_ge(s_t, number["k", i] + 1)
                act.copy(keyT[:, i * P:(i + 1) * P], ps_t[:, 0:P])
                for b in range(4):
                    r = slice(IDX_DIM * b, IDX_DIM * (b + 1))
                    act.copy(iqT[r, i % 2, b::4, :], ps_t[r, P:3 * P].rearrange("p (m t) -> p m t", m=2))
                act.copy(ikT[:, i * P:(i + 1) * P], ps_t[:, 3 * P:4 * P]).then_inc(s_te, 1)

            def relu(i, h):
                n = IDX_HEADS * (i - 1) + h
                act.wait_ge(s_x, n + 1)
                if n >= 2:
                    act.wait_ge(s_acc, n - 1)
                act.activation(rel[:, n % 2, 0:W[i]], ps_x[:, :, :].rearrange("p b c -> p (b c)")[:, 0:W[i]],
                               ACT.Relu).then_inc(s_relu, 1)

            def exponent(i, h):
                n = ATT_HEADS * (i - 1) + h
                act.wait_ge(s_nm, n + 1)
                act.activation(lg[:, n % 2, FRONT:FRONT + W[i]], lg[:, n % 2, FRONT:FRONT + W[i]], ACT.Exp, bias=nmx[:, i % 2, h:h + 1],
                               scale=ATT_SCALE, accum_out=rsum[:, i % 2, h:h + 1]).then_inc(s_exp, 1)

            def take_probs(i, h):
                n = ATT_HEADS * (i - 1) + h
                if n >= 2:
                    act.wait_ge(s_pv, n - 1)
                for g in range(-(-(i + 1) // 4)):
                    act.wait_ge(s_t, number["p", i, h, g] + 1)
                    k = min(4, i + 1 - 4 * g)
                    act.copy(pT[:, n % 2, 4 * g:4 * g + k, :],
                             ps_t[:, 0:k * P].rearrange("p (m t) -> p m t", m=k)).then_inc(s_te, 1)

            def take_units(i, h, place):
                for u in ends.get((i, h, place), ()):
                    act.wait_ge(s_fm, u + 1)
                    if u >= FST:
                        act.wait_ge(s_fs[u % FST], 16 * (u // FST))
                    act.copy(fst[:, u % FST, :], fill_bank(u)).then_inc(s_fe, 1)

            act.wait_ge(s_pad, 3)
            take_rows(0)
            take_rows(1)
            for h in range(IDX_HEADS):
                relu(1, h)
            for i in range(1, NT):
                if i + 1 < NT:
                    take_rows(i + 1)
                for h in range(ATT_HEADS):
                    if i + 1 < NT:
                        relu(i + 1, h)
                    if h == 0:
                        take_units(i, h, 0)
                    else:
                        take_units(i, h, 0)
                        take_probs(i, h - 1)
                    exponent(i, h)
                    take_units(i, h, 1)
                    take_units(i, h, 2)
                take_probs(i, ATT_HEADS - 1)

        @block.tensor
        def _(pe):
            def bank_free(key):
                if number[key]:
                    pe.wait_ge(s_te, number[key])

            def turn_rows(i):
                pe.wait_ge(s_rope, i + 1)
                pe.wait_ge(s_copy, 4 * (i + 1))
                bank_free(("q", i))
                for m in range(4):
                    last = pe.transpose(ps_t[:, m * P:(m + 1) * P],
                                        qpair[:, i % 2, m, :, :].rearrange("p g d -> p (g d)"), ident[:, :])
                last.then_inc(s_t, 1)
                bank_free(("k", i))
                pe.transpose(ps_t[:, 0:P], rows[:, i % 2, C_K:C_V], ident[:, :])
                pe.transpose(ps_t[:, P:2 * P], rows[:, i % 2, C_IQ:C_IQ + P], ident[:, :])
                pe.transpose(ps_t[:, 2 * P:3 * P], rows[:, i % 2, C_IQ + P:C_IK], ident[:, :])
                pe.transpose(ps_t[:, 3 * P:4 * P], ik4[:, i % 2, :], ident[:, :]).then_inc(s_t, 1)

            def index_product(i, h):
                n = IDX_HEADS * (i - 1) + h
                if h == 0:
                    pe.wait_ge(s_te, number["k", i] + 1)
                if n:
                    pe.wait_ge(s_relu, n)
                for c in range(0, W[i], 512):
                    e = min(c + 512, W[i])
                    last = pe.matmul(ps_x[:, c // 512, 0:e - c], iqT[:, i % 2, h, :],
                                     ikT[:, FRONT + c:FRONT + e], start=True, stop=True)
                last.then_inc(s_x, 1)

            def logits(i, h):
                n = ATT_HEADS * (i - 1) + h
                if n:
                    pe.wait_ge(s_lm, n)
                for c in range(0, W[i], 512):
                    e = min(c + 512, W[i])
                    last = pe.matmul(ps_l[:, c // 512, 0:e - c], qT[:, i % 2, h, :],
                                     keyT[:, FRONT + c:FRONT + e], start=True, stop=True)
                last.then_inc(s_l, 1)

            def turn_probs(i, h):
                n = ATT_HEADS * (i - 1) + h
                pe.wait_ge(s_exp, n + 1)
                for g in range(-(-(i + 1) // 4)):
                    bank_free(("p", i, h, g))
                    for t in range(4 * g, min(4 * g + 4, i + 1)):
                        last = pe.transpose(ps_t[:, (t - 4 * g) * P:(t - 4 * g + 1) * P],
                                            lg[:, n % 2, t * P:(t + 1) * P], ident[:, :])
                    last.then_inc(s_t, 1)

            def attend(i, h):
                n = ATT_HEADS * (i - 1) + h
                groups = -(-(i + 1) // 4)
                pe.wait_ge(s_te, number["p", i, h, groups - 1] + 1)
                if h == 0 and i > 1:
                    pe.wait_ge(s_att, i - 1)
                v = HD * (h // 4)
                for t in range(i + 1):
                    last = pe.matmul(ps_o[:, h * HD:(h + 1) * HD], pT[:, n % 2, t, :], val[:, t, v:v + HD],
                                     start=(t == 0), stop=(t == i))
                last.then_inc(s_pv, 1)

            unit = [0, 0]

            def fill(i, h, place):
                for _ in range(room.get((i, h, place), 0)):
                    u, k = unit
                    c, t = unit_at[u]
                    if k == 0:
                        pe.wait_ge(s_fw[c % 2], 16 * (c // 2 + 1))
                        if fill_before(u):
                            pe.wait_ge(s_fe, fill_before(u))
                    last = pe.matmul(fill_bank(u), xnT[:, k, t * P:(t + 1) * P], fw[:, c % 2, k, :],
                                     start=(k == 0), stop=(k == KT - 1))
                    if k == KT - 1:
                        last.then_inc(s_fm, 1)
                    unit[0], unit[1] = (u + 1, 0) if k == KT - 1 else (u, k + 1)

            pe.wait_ge(s_pad, 3)
            turn_rows(0)
            turn_rows(1)
            for h in range(IDX_HEADS):
                index_product(1, h)
            for i in range(1, NT):
                if i + 1 < NT:
                    turn_rows(i + 1)
                if i == NT - 2:
                    pe.wait_ge(s_fe, first_a_only)
                if i == NT - 1:
                    pe.wait_ge(s_fe, first_last)
                    pe.wait_ge(s_relu, IDX_HEADS * (NT - 1))
                for h in range(ATT_HEADS):
                    if i + 1 < NT:
                        index_product(i + 1, h)
                    logits(i, h)
                    fill(i, h, 0)
                    if h:
                        turn_probs(i, h - 1)
                        fill(i, h, 1)
                        attend(i, h - 1)
                    else:
                        fill(i, h, 1)
                    fill(i, h, 2)
                turn_probs(i, ATT_HEADS - 1)
                attend(i, ATT_HEADS - 1)
    return used


BL = 32
NB4 = P // BL
BIG = 1.0e37


def stage_hgrn(nc, io, scr, ident, wa, wh, wo, s_w):
    used = []
    with ExitStack() as ctx:
        def sb(name, shape, dt=F32):
            return ctx.enter_context(nc.sbuf_tensor(name, shape, dt))

        def bank(name):
            return ctx.enter_context(nc.psum_tensor(name, [P, 512], F32))

        def sem(name):
            used.append(ctx.enter_context(nc.semaphore(name)))
            return used[-1]

        lb_rows = sb("g_lb_rows", [2 * HG_HEADS, P])
        lbt = sb("g_lbt", [P, 8, HG_HEADS])
        g_bc = sb("g_g_bc", [P, HGW])
        ones = sb("g_run", [P, HGW])
        cmask = sb("g_cmask", [P, HG_HEADS, BL])
        qf = sb("g_qf", [P, 2 * HGW])
        v = sb("g_v", [P, HGW])
        hg = sb("g_hg", [P, HGW])
        sg = sb("g_sg", [P, HGW])
        f = sb("g_f", [P, HGW])
        kk = sb("g_kk", [P, HGW])
        lf = sb("g_lf", [P, HGW])
        b = sb("g_b", [P, HGW])
        bm = sb("g_bm", [P, HGW])
        bl = sb("g_bl", [P, HGW])
        hgg = sb("g_hgg", [P, HGW])
        e = sb("g_e", [P, 4, HGW])
        dec = sb("g_dec", [P, HG_HEADS, NB4])
        qe = sb("g_qe", [P, HGW])
        ke = sb("g_ke", [P, HGW])
        qs = sb("g_qs", [P, HGW])
        ks = sb("g_ks", [P, HGW])
        kst = sb("g_kst", [P, HGW])
        at = sb("g_at", [P, HG_HEADS, BL])
        state = sb("g_state", [P, NB4, HGW])
        sq = sb("g_sq", [P, HG_HEADS, P])
        st4 = sb("g_st4", [P, 4, HG_HEADS])
        sl = sb("g_sl", [P, 2, HGW])
        on = sb("g_on", [P, HGW])
        res = sb("g_res", [P, HGW])
        ps_q, ps_f, ps_k, ps_o = bank("g_ps_q"), bank("g_ps_f"), bank("g_ps_k"), bank("g_ps_o")
        ps_s = [bank(f"g_ps_s{j}") for j in range(NB4)]

        s_lb = sem("g_lb_landed")
        s_gb = sem("g_g_landed")
        s_qf = sem("g_qf_landed")
        s_v = sem("g_v_landed")
        s_hg = sem("g_hg_landed")
        s_cst = sem("g_constants")
        s_lbt = sem("g_lb_turned")
        s_dv = sem("g_dve_chain")
        s_ac = sem("g_act_chain")
        s_lbe = sem("g_lb_exp_ready")
        s_lbm = sem("g_lb_shifted")
        s_st0 = sem("g_state_zeroed")
        s_turn = sem("g_q_and_f_turned")
        s_eg = sem("g_sigmoid_ready")
        s_f = sem("g_f_ready")
        s_lf = sem("g_log_ready")
        s_b = sem("g_b_ready")
        s_e = sem("g_exps_ready")
        s_kk = sem("g_b_summed")
        s_hgg = sem("g_hg_scaled")
        s_g1 = sem("g_silu_ready")
        s_dec = sem("g_decay_ready")
        s_qk = sem("g_scaled_ready")
        s_kt = sem("g_ks_turned")
        s_kst = sem("g_kst_ready")
        s_a = sem("g_pairs_ready")
        s_at = sem("g_masked_ready")
        s_ps = sem("g_outer_ready")
        s_s = sem("g_state_ready")
        s_o = sem("g_o_ready")
        s_sq = sem("g_squares_ready")
        s_var = sem("g_variance_ready")
        s_rs = sem("g_rstd_ready")
        s_sl = sem("g_output_gate_ready")
        s_res = sem("g_result_ready")
        s_out = sem("g_result_stored")

        def blocks(ap):
            return ap.rearrange("p (c t) -> p c t", t=BL)

        block = ctx.enter_context(nc.Block())

        @block.sync
        def _(sp):
            sp.dma_start(lb_rows[:, :], io["hgrn_lb_logits"].rearrange("r (h d) -> (r h) d", d=P)).then_inc(s_lb, 16)
            sp.dma_start(g_bc[:, :], io["hgrn_norm_g"].partition_broadcast(P)).then_inc(s_gb, 16)

            def load_qf(i):
                sp.wait_ge(s_turn, i)
                sp.dma_start(qf[:, :], scr["proj"][bass.ds(i * P, P), C_HQ:C_HI]).then_inc(s_qf, 16)

            def load_v(i):
                sp.wait_ge(s_o, i * NB4)
                sp.dma_start(v[:, :], scr["proj"][bass.ds(i * P, P), C_HI:C_HG]).then_inc(s_v, 16)

            def load_hg(i):
                sp.wait_ge(s_hgg, i)
                sp.dma_start(hg[:, :], scr["proj"][bass.ds(i * P, P), C_HG:C_GA]).then_inc(s_hg, 16)

            def store(i):
                sp.wait_ge(s_res, i + 1)
                sp.dma_start(scr["hgr"][bass.ds(i * P, P), :], res[:, :]).then_inc(s_out, 16)

            load_qf(0)
            load_hg(0)
            load_qf(1)
            load_hg(1)
            load_v(0)
            sp.dma_start(wa[:, :, :], io["w_up_attn"][0].rearrange("(k p) n -> p k n", p=P)).then_inc(s_w, 16)
            sp.dma_start(wh[:, :, :], io["w_up_hgrn"][0].rearrange("(k p) n -> p k n", p=P)).then_inc(s_w, 16)
            with sp.Fori(1, NT - 1) as i:
                load_qf(i + 1)
                load_hg(i + 1)
                load_v(i)
                store(i - 1)
            load_v(NT - 1)
            sp.dma_start(wo[:, :, :], io["w_out"][0].rearrange("(k p) n -> p k n", p=P)).then_inc(s_w, 16)
            store(NT - 2)
            store(NT - 1)
            sp.wait_ge(s_out, 16 * NT)

        @block.gpsimd
        def _(pool):
            pool.memset(ones[:, :], 1.0).then_inc(s_cst, 1)
            pool.memset(cmask[:, :, :], 0.0).then_inc(s_cst, 1)
            pool.memset(state[:, 0, :], 0.0).then_inc(s_st0, 1)
            pool.wait_ge(s_cst, 2)
            pool.memset(blocks(ones[:, :])[:, :, 0:1], 0.0).then_inc(s_cst, 1)
            for j in range(NB4):
                pool.wait_ge(s_cst, 3 + j)
                pool.affine_select(out=cmask[BL * j:BL * (j + 1), :, :], in_=cmask[BL * j:BL * (j + 1), :, :],
                                   compare_op=ALU.is_gt, fill=1.0, base=0, pattern=[[0, HG_HEADS], [-1, BL]],
                                   channel_multiplier=1).then_inc(s_cst, 1)

        @block.vector
        def _(dve):
            ch = Chain(dve, s_dv)
            a0, a1 = lbt[:, 0, :], lbt[:, 1, :]
            dve.wait_ge(s_lbt, 1)
            ch.link(dve.tensor_copy(lbt[:, 0:2, :], ps_q[:, 0:2 * HG_HEADS].rearrange("p (r h) -> p r h", r=2)))
            ch.link(dve.tensor_tensor(lbt[:, 2, :], a0, a1, ALU.max))
            dve.tensor_tensor(lbt[:, 3, :], a0, lbt[:, 2, :], ALU.subtract)
            dve.tensor_tensor(lbt[:, 4, :], a1, lbt[:, 2, :], ALU.subtract).then_inc(s_lbm, 1)
            dve.wait_ge(s_lbe, 1)
            ch.link(dve.tensor_tensor(lbt[:, 6, :], lbt[:, 3, :], lbt[:, 4, :], ALU.add))
            ch.link(dve.reciprocal(lbt[:, 7, :], lbt[:, 6, :]))
            ch.link(dve.tensor_tensor(lbt[:, 0, :], lbt[:, 3, :], lbt[:, 7, :], ALU.mult))
            ch.link(dve.tensor_scalar(lbt[:, 1, :], lbt[:, 0, :], -1.0, 1.0, ALU.mult, ALU.add))
            before = ch.n
            dve.wait_ge(s_gb, 16)
            dve.wait_ge(s_cst, 3 + NB4)

            def forget(i):
                dve.wait_ge(s_eg, i + 1)
                for h in range(HG_HEADS):
                    c = slice(h * P, (h + 1) * P)
                    last = dve.tensor_scalar(f[:, c], sg[:, c], lbt[:, 1, h:h + 1], lbt[:, 0, h:h + 1],
                                             ALU.mult, ALU.add)
                last.then_inc(s_f, 1)
                dve.wait_ge(s_f, i + 1)
                dve.tensor_scalar(kk[:, :], f[:, :], -1.0, 1.0, ALU.mult, ALU.add)
                dve.wait_ge(s_sl, i + 1)
                dve.tensor_tensor(hgg[:, :], hg[:, :], g_bc[:, :], ALU.mult).then_inc(s_hgg, 1)

            def mask(i):
                dve.wait_ge(s_a, i + 1)
                ch = Chain(dve, s_dv, base=i * 2 + before)
                ch.link(dve.tensor_scalar(at[:, :, :], ps_o[:, 0:HG_HEADS * BL].rearrange("p (h t) -> p h t", t=BL),
                                          -BIG, BIG, ALU.max, ALU.min))
                dve.tensor_tensor(at[:, :, :], at[:, :, :], cmask[:, :, :], ALU.mult).then_inc(s_at, 1)

            def running_sum(i):
                dve.wait_ge(s_lf, i + 1)
                dve.wait_ge(s_dec, i)
                dve.tensor_tensor_scan(b[:, :], ones[:, :], lf[:, :], 0.0, ALU.mult, ALU.add).then_inc(s_kk, 1)
                dve.wait_ge(s_kk, i + 1)
                bb = blocks(b[:, :])
                wide = [P, HG_HEADS * NB4, BL]
                dve.tensor_tensor(blocks(bm[:, :]), bb, bb[:, :, BL // 2 - 1:BL // 2].to_broadcast(wide), ALU.subtract)
                dve.tensor_tensor(blocks(bl[:, :]), bb[:, :, BL - 1:BL].to_broadcast(wide), bb,
                                  ALU.subtract).then_inc(s_b, 1)

            def states(i):
                dve.wait_ge(s_dec, i + 1)
                for j in range(NB4):
                    dve.wait_ge(s_ps, i * NB4 + (j + 1))
                    if j == 0:
                        dve.wait_ge(s_st0, 1)
                    if j == NB4 - 1:
                        dve.wait_ge(s_o, i * NB4 + 1)
                    for h in range(HG_HEADS):
                        c = slice(h * P, (h + 1) * P)
                        last = dve.scalar_tensor_tensor(out=state[:, (j + 1) % NB4, c], in0=state[:, j, c],
                                                        scalar=dec[:, h, j:j + 1], in1=ps_s[j][:, c],
                                                        op0=ALU.mult, op1=ALU.add)
                    last.then_inc(s_s, 1)
                    dve.wait_ge(s_s, i * NB4 + (j + 1))

            def normalize(i):
                dve.wait_ge(s_sq, i + 1)
                dve.tensor_scalar(st4[:, 1, :], st4[:, 0, :], 1.0 / HG_D, EPS, ALU.mult, ALU.add).then_inc(s_var, 1)
                dve.wait_ge(s_rs, i + 1)
                ch = Chain(dve, s_dv, base=i * 2 + (before + 1))
                ch.link(dve.tensor_tensor(on[:, :].rearrange("p (h d) -> p h d", h=HG_HEADS),
                                          ps_o[:, :].rearrange("p (h d) -> p h d", h=HG_HEADS),
                                          st4[:, 3, :].unsqueeze(2).to_broadcast([P, HG_HEADS, P]), ALU.mult))
                dve.wait_ge(s_out, i * 16)
                dve.wait_ge(s_g1, i + 1)
                dve.tensor_tensor(res[:, :], on[:, :], sl[:, 1, :], ALU.mult).then_inc(s_res, 1)

            def scale(i):
                dve.wait_ge(s_e, i + 1)
                dve.wait_ge(s_o, i * NB4)
                dve.tensor_tensor(ks[:, :], kk[:, :], e[:, 3, :], ALU.mult)
                dve.tensor_tensor(ke[:, :], kk[:, :], e[:, 1, :], ALU.mult)
                dve.scalar_tensor_tensor(out=qe[:, :], in0=ps_q[:, :], scalar=float(HG_D) ** -0.5, in1=e[:, 0, :],
                                         op0=ALU.mult, op1=ALU.mult)
                dve.scalar_tensor_tensor(out=qs[:, :], in0=ps_q[:, :], scalar=float(HG_D) ** -0.5, in1=e[:, 2, :],
                                         op0=ALU.mult, op1=ALU.mult).then_inc(s_qk, 1)
                dve.wait_ge(s_res, i)
                dve.tensor_tensor(sl[:, 1, :], hgg[:, :], sl[:, 0, :], ALU.mult).then_inc(s_g1, 1)

            def back(i):
                states(i)
                normalize(i)

            forget(0)
            running_sum(0)
            scale(0)
            with dve.Fori(1, NT) as t:
                forget(t)
                mask(t - 1)
                running_sum(t)
                back(t - 1)
                scale(t)
            mask(NT - 1)
            back(NT - 1)

        @block.scalar
        def _(act):
            act.wait_ge(s_lbm, 1)
            act.activation(lbt[:, 3:5, :], lbt[:, 3:5, :], ACT.Exp).then_inc(s_lbe, 1)

            def sigmoids(i):
                act.wait_ge(s_turn, i + 1)
                act.activation(sg[:, :], ps_f[:, :], ACT.Sigmoid).then_inc(s_eg, 1)
                act.wait_ge(s_hg, 16 * i + 16)
                act.wait_ge(s_g1, i)
                act.activation(sl[:, 0, :], hg[:, :], ACT.Sigmoid).then_inc(s_sl, 1)

            def take_keys(i):
                act.wait_ge(s_kt, i + 1)
                act.wait_ge(s_ps, i * NB4)
                act.copy(kst[:, :], ps_k[:, :]).then_inc(s_kst, 1)

            def decays(i):
                act.preload_act_table_set("natural_log_exp_and_others")
                act.wait_ge(s_f, i + 1)
                act.activation(lf[:, :], f[:, :], ACT.Ln).then_inc(s_lf, 1)
                act.wait_ge(s_b, i + 1)
                act.wait_ge(s_qk, i)
                act.activation(e[:, 0, :], bm[:, :], ACT.Exp)
                act.activation(e[:, 1, :], bm[:, :], ACT.Exp, scale=-1.0)
                act.activation(e[:, 2, :], b[:, :], ACT.Exp)
                act.activation(e[:, 3, :], bl[:, :], ACT.Exp).then_inc(s_e, 1)

            def statistics(i):
                act.wait_ge(s_o, i * NB4 + NB4)
                for h in range(HG_HEADS):
                    last = act.activation(sq[:, h, :], ps_o[:, h * P:(h + 1) * P], ACT.Square,
                                          accum_out=st4[:, 0, h:h + 1])
                last.then_inc(s_sq, 1)
                act.wait_ge(s_var, i + 1)
                act.activation(st4[:, 2, :], st4[:, 1, :], ACT.Ln).then_inc(s_ac, 1)
                act.wait_ge(s_ac, i + 1)
                act.activation(st4[:, 3, :], st4[:, 2, :], ACT.Exp, scale=-0.5).then_inc(s_rs, 1)

            def decay(i):
                act.wait_ge(s_s, i * NB4)
                act.activation(dec[:, :, :], b[:, :].rearrange("p (h j t) -> p h j t", h=HG_HEADS, t=BL)[:, :, :, BL - 1],
                               ACT.Exp).then_inc(s_dec, 1)

            sigmoids(0)
            decays(0)
            decay(0)
            with act.Fori(1, NT) as t:
                sigmoids(t)
                take_keys(t - 1)
                decays(t)
                statistics(t - 1)
                decay(t)
            take_keys(NT - 1)
            statistics(NT - 1)

        @block.tensor
        def _(pe):
            pe.wait_ge(s_lb, 16)
            pe.transpose(ps_q[:, 0:2 * HG_HEADS], lb_rows[:, :], ident[0:2 * HG_HEADS, 0:2 * HG_HEADS]).then_inc(s_lbt, 1)
            pe.wait_ge(s_lbe, 1)

            def turn(i):
                pe.wait_ge(s_qf, 16 * i + 16)
                pe.wait_ge(s_qk, i)
                pe.wait_ge(s_eg, i)
                for h in range(HG_HEADS):
                    c = slice(h * P, (h + 1) * P)
                    pe.transpose(ps_f[:, c], qf[:, HGW + h * P:HGW + (h + 1) * P], ident[:, :])
                    last = pe.transpose(ps_q[:, c], qf[:, c], ident[:, :])
                last.then_inc(s_turn, 1)

            def recur(i):
                pe.wait_ge(s_qk, i + 1)
                pe.wait_ge(s_kst, i)
                for h in range(HG_HEADS):
                    c = slice(h * P, (h + 1) * P)
                    last = pe.transpose(ps_k[:, c], ks[:, c], ident[:, :])
                last.then_inc(s_kt, 1)
                pe.wait_ge(s_res, i)
                for j in range(NB4):
                    for h in range(HG_HEADS):
                        c = slice(h * P + j * BL, h * P + (j + 1) * BL)
                        last = pe.matmul(ps_o[BL * j:BL * (j + 1), h * BL:(h + 1) * BL], ke[:, c], qe[:, c],
                                         start=True, stop=True)
                last.then_inc(s_a, 1)
                pe.wait_ge(s_v, 16 * i + 16)
                pe.wait_ge(s_kst, i + 1)
                for j in range(NB4):
                    r = slice(BL * j, BL * (j + 1))
                    for h in range(HG_HEADS):
                        c = slice(h * P, (h + 1) * P)
                        last = pe.matmul(ps_s[j][:, c], kst[r, c], v[r, c], start=True, stop=True)
                    last.then_inc(s_ps, 1)
                pe.wait_ge(s_at, i + 1)
                for j in range(NB4):
                    r = slice(BL * j, BL * (j + 1))
                    pe.wait_ge(s_s, i * NB4 + j) if j else pe.wait_ge(s_st0, 1)
                    for h in range(HG_HEADS):
                        c = slice(h * P, (h + 1) * P)
                        pe.matmul(ps_o[r, c], qs[:, h * P + j * BL:h * P + (j + 1) * BL], state[:, j, c],
                                  start=True, stop=False)
                        last = pe.matmul(ps_o[r, c], at[r, h, :], v[r, c], start=False, stop=True)
                    last.then_inc(s_o, 1)

            turn(0)
            with pe.Fori(1, NT) as t:
                turn(t)
                recur(t - 1)
            recur(NT - 1)





def stage_merge(nc, io, scr, ident, wa, wh, wo, s_w):
    used = []
    with ExitStack() as ctx:
        def sb(name, shape, dt=F32):
            return ctx.enter_context(nc.sbuf_tensor(name, shape, dt))

        def banks(name, n):
            return ctx.enter_context(nc.psum_tensor(name, [P, n, 512], F32))

        def sem(name):
            used.append(ctx.enter_context(nc.semaphore(name)))
            return used[-1]

        KH = HGW // P
        wr = sb("m_wr", [P, KT, N_EXP])
        rb = sb("m_rb", [P, N_EXP])
        g_bc = sb("m_g_bc", [P, D])
        br = sb("m_br", [P, 2, HGW])
        brT = sb("m_brT", [P, 2, KH, P])
        gate = sb("m_gate", [P, 2, D])
        eg = sb("m_eg", [P, 2, D])
        mixa = sb("m_mixa", [P, D])
        mix = sb("m_mix", [P, D])
        mixT = sb("m_mixT", [P, KT, P])
        hin = sb("m_hin", [P, D])
        h2 = sb("m_h2", [P, D])
        sq = sb("m_sq", [P, D])
        st = sb("m_st", [P, 4])
        xn = sb("m_xn", [P, D])
        xs = sb("m_xs", [P, 2, D], F16)
        xT = sb("m_xT", [P, KT, P])
        lgt = sb("m_lgt", [P, 2, N_EXP])
        ps_u = banks("m_ps_u", 4)
        ps_t = banks("m_ps_t", 2)
        ps_o = banks("m_ps_o", 2)

        s_br = sem("m_branches_landed")
        s_gate = sem("m_gates_landed")
        s_h = nc.alloc_semaphore("m_h_landed")
        s_bt = sem("m_branches_turned")
        s_bte = sem("m_branches_taken")
        s_u = sem("m_branch_products_ready")
        s_eg = sem("m_gates_ready")
        s_dv = sem("m_dve_chain")
        s_mix = sem("m_mix_ready")
        s_pool = sem("m_pool_waited")
        s_mt = sem("m_mix_turned")
        s_mte = sem("m_mix_taken")
        s_o = sem("m_out_product_ready")
        s_h2 = sem("m_h2_ready")
        s_h2s = nc.alloc_semaphore("m_h2_stored")
        s_ssq = sem("m_squares_ready")
        s_var = sem("m_variance_ready")
        s_ac = sem("m_act_chain")
        s_rs = sem("m_rstd_ready")
        s_xn = sem("m_xn_ready")
        s_xh = sem("m_xn_hi_ready")
        s_xs = sem("m_xn_parts_ready")
        s_xns = nc.alloc_semaphore("m_xn_stored")
        s_xt = sem("m_xn_turned")
        s_xte = sem("m_xn_taken")
        s_lg = sem("m_logits_ready")
        s_lgb = sem("m_logits_biased")
        s_lgs = nc.alloc_semaphore("m_logits_stored")

        def skewed(eng, stages):
            for i in (0, 1):
                for f, d in stages:
                    if 0 <= i - d:
                        f(i - d)
            with eng.Fori(2, OT) as i:
                for f, d in stages:
                    f(i - d)
            for i in (OT, OT + 1):
                for f, d in stages:
                    if i - d < OT:
                        f(i - d)

        def rows(i):
            return bass.ds(i * P, P)

        def rows_in(i):
            return bass.ds(i * P + P, P)

        block = ctx.enter_context(nc.Block())

        @block.sync
        def _(sp):
            sp.dma_start(g_bc[:, :], io["ffn_norm_g"].partition_broadcast(P)).then_inc(s_w, 16)
            sp.dma_start(rb[:, :], io["router_b"].partition_broadcast(P)).then_inc(s_w, 16)
            sp.dma_start(wr[:, :, :], io["router_w"][0].rearrange("(k p) n -> p k n", p=P)).then_inc(s_w, 16)

            def load(i):
                sp.wait_ge(s_bt, 2 * i)
                sp.dma_start(br[:, 0, :], scr["att"][rows_in(i), :]).then_inc(s_br, 16)
                sp.dma_start(br[:, 1, :], scr["hgr"][rows_in(i), :]).then_inc(s_br, 16)
                sp.wait_ge(s_eg, i)
                sp.dma_start(gate[:, :, :], scr["proj"][rows_in(i), C_GA:IN_COLS].rearrange("p (g c) -> p g c", g=2)
                             ).then_inc(s_gate, 16)

            with sp.Fori(0, OT) as i:
                load(i)

        @block.gpsimd
        def _(pool):
            def residual(i):
                pool.wait_ge(s_h2, i)
                pool.sem_inc(s_pool, 1)
                pool.dma_start(hin[:, :], scr["h"][rows_in(i), :]).then_inc(s_h, 16)
                pool.wait_ge(s_h2, i + 1)
                pool.sem_inc(s_pool, 1)
                pool.dma_start(scr["h2"][rows(i), :], h2[:, :]).then_inc(s_h2s, 16)

            def store(i):
                pool.wait_ge(s_xs, i + 1)
                pool.sem_inc(s_pool, 1)
                pool.dma_start(scr["xn"][rows(i), :], xs[:, :, :].rearrange("p c d -> p (c d)")).then_inc(s_xns, 16)
                pool.wait_ge(s_lgb, i + 1)
                pool.sem_inc(s_pool, 1)
                pool.dma_start(scr["logits"][rows(i), :], lgt[:, 0, :]).then_inc(s_lgs, 16)

            skewed(pool, ((residual, 1), (store, 2)))
            pool.wait_ge(s_h2s, 16 * OT)
            pool.wait_ge(s_xns, 16 * OT)
            pool.wait_ge(s_lgs, 16 * OT)

        @block.tensor
        def _(pe):
            def turn(src, c, bank):
                for k in range(4):
                    last = pe.transpose(ps_t[:, bank, k * P:(k + 1) * P], src[:, c + k * P:c + (k + 1) * P], ident[:, :])
                return last

            def branches(i):
                pe.wait_ge(s_br, 32 * i + 32)
                for j in range(2):
                    if j:
                        pe.wait_ge(s_lgb, max(0, i - 2) if isinstance(i, int) else i - 2)
                    turn(br[:, j, :], 0, j).then_inc(s_bt, 1)
                pe.wait_ge(s_mix, i)
                for j, w in ((0, wa), (1, wh)):
                    pe.wait_ge(s_bte, 2 * i + (j + 1))
                    for k in range(KH):
                        for n in range(2):
                            last = pe.matmul(ps_u[:, 2 * j + n, :], brT[:, j, k, :], w[:, k, n * 512:(n + 1) * 512],
                                             start=(k == 0), stop=(k == KH - 1))
                last.then_inc(s_u, 1)

            def project(i):
                pe.wait_ge(s_mix, i + 1)
                for n in range(2):
                    if n:
                        pe.wait_ge(s_lgb, max(0, i - 1) if isinstance(i, int) else i - 1)
                    turn(mix, 512 * n, n).then_inc(s_mt, 1)
                pe.wait_ge(s_h2, i)
                for k in range(KT):
                    if k % 4 == 0:
                        pe.wait_ge(s_mte, 2 * i + (k // 4 + 1))
                    for n in range(2):
                        last = pe.matmul(ps_o[:, n, :], mixT[:, k, :], wo[:, k, n * 512:(n + 1) * 512],
                                         start=(k == 0), stop=(k == KT - 1))
                last.then_inc(s_o, 1)

            def route(i):
                pe.wait_ge(s_xn, i + 1)
                for n in range(2):
                    if n:
                        pe.wait_ge(s_lgb, i)
                    turn(xn, 512 * n, n).then_inc(s_xt, 1)
                pe.wait_ge(s_xte, 2 * i + 2)
                for k in range(KT):
                    last = pe.matmul(ps_t[:, 1, 0:N_EXP], xT[:, k, :], wr[:, k, :], start=(k == 0), stop=(k == KT - 1))
                last.then_inc(s_lg, 1)

            pe.wait_ge(s_w, 16 * 6)
            skewed(pe, ((branches, 0), (project, 1), (route, 2)))

        @block.scalar
        def _(act):
            def branches(i):
                for j in range(2):
                    act.wait_ge(s_bt, 2 * i + (j + 1))
                    act.wait_ge(s_u, i)
                    act.copy(brT[:, j, :, :], ps_t[:, j, :].rearrange("p (k t) -> p k t", t=P)).then_inc(s_bte, 1)
                act.wait_ge(s_gate, 16 * i + 16)
                act.wait_ge(s_mix, i)
                act.activation(eg[:, :, :], gate[:, :, :], ACT.Sigmoid).then_inc(s_eg, 1)

            def project(i):
                for n in range(2):
                    act.wait_ge(s_mt, 2 * i + (n + 1))
                    act.wait_ge(s_o, i)
                    act.copy(mixT[:, 4 * n:4 * n + 4, :],
                             ps_t[:, n, :].rearrange("p (k t) -> p k t", t=P)).then_inc(s_mte, 1)

            def statistics(i):
                act.preload_act_table_set("natural_log_exp_and_others")
                act.wait_ge(s_h2, i + 1)
                act.wait_ge(s_ssq, i)
                act.activation(sq[:, :], h2[:, :], ACT.Square, accum_out=st[:, 0:1]).then_inc(s_ssq, 1)
                act.wait_ge(s_var, i + 1)
                act.activation(st[:, 2:3], st[:, 1:2], ACT.Ln).then_inc(s_ac, 1)
                act.wait_ge(s_ac, i + 1)
                act.activation(st[:, 3:4], st[:, 2:3], ACT.Exp, scale=-0.5).then_inc(s_rs, 1)

            def route(i):
                for n in range(2):
                    act.wait_ge(s_xt, 2 * i + (n + 1))
                    act.wait_ge(s_lg, i)
                    act.copy(xT[:, 4 * n:4 * n + 4, :],
                             ps_t[:, n, :].rearrange("p (k t) -> p k t", t=P)).then_inc(s_xte, 1)

            skewed(act, ((branches, 0), (project, 1), (route, 2), (statistics, 1)))

        @block.vector
        def _(dve):
            def merge(i):
                ch = Chain(dve, s_dv, base=2 * i)
                dve.wait_ge(s_eg, i + 1)
                dve.wait_ge(s_u, i + 1)
                dve.tensor_tensor(mixa[:, :], ps_u[:, 0:2, :].rearrange("p n c -> p (n c)"), eg[:, 0, :], ALU.mult)
                ch.link(dve.tensor_tensor(eg[:, 1, :], ps_u[:, 2:4, :].rearrange("p n c -> p (n c)"), eg[:, 1, :],
                                          ALU.mult))
                dve.wait_ge(s_mt, 2 * i)
                ch.link(dve.tensor_tensor(mix[:, :], mixa[:, :], eg[:, 1, :], ALU.add))
                dve.sem_inc(s_mix, 1)

            def add(i):
                dve.wait_ge(s_o, i + 1)
                dve.wait_ge(s_h, 16 * i + 16)
                dve.wait_ge(s_h2s, 16 * i)
                dve.wait_ge(s_ssq, i)
                dve.tensor_tensor(h2[:, :], hin[:, :], ps_o[:, :, :].rearrange("p n c -> p (n c)"),
                                  ALU.add).then_inc(s_h2, 1)

            def residual(i):
                dve.wait_ge(s_ssq, i + 1)
                dve.tensor_scalar(st[:, 1:2], st[:, 0:1], 1.0 / D, EPS, ALU.mult, ALU.add).then_inc(s_var, 1)
                dve.wait_ge(s_rs, i + 1)
                dve.wait_ge(s_xt, 2 * i)
                dve.scalar_tensor_tensor(out=xn[:, :], in0=h2[:, :], scalar=st[:, 3:4], in1=g_bc[:, :],
                                         op0=ALU.mult, op1=ALU.mult).then_inc(s_xn, 1)
                dve.wait_ge(s_xns, 16 * i)
                dve.wait_ge(s_xn, i + 1)
                dve.tensor_copy(xs[:, 0, :], xn[:, :]).then_inc(s_xh, 1)
                dve.wait_ge(s_xh, i + 1)
                dve.tensor_tensor(xs[:, 1, :], xn[:, :], xs[:, 0, :], ALU.subtract).then_inc(s_xs, 1)

            def bias(i):
                dve.wait_ge(s_lg, i + 1)
                dve.wait_ge(s_lgs, 16 * i)
                dve.tensor_tensor(lgt[:, 0, :], ps_t[:, 1, 0:N_EXP], rb[:, :], ALU.add).then_inc(s_lgb, 1)

            dve.wait_ge(s_w, 16 * 6)
            skewed(dve, ((merge, 0), (add, 1), (bias, 2), (residual, 1)))




def stage_route(nc, io, scr, items, n_items, slots_i, token):
    used = []
    with ExitStack() as ctx:
        def sb(name, shape, dt=F32):
            return ctx.enter_context(nc.sbuf_tensor(name, shape, dt))

        def sem(name):
            used.append(ctx.enter_context(nc.semaphore(name)))
            return used[-1]

        lg = sb("r_lg", [P, OT, N_EXP])
        top = sb("r_top", [P, OT, 8])
        topi = sb("r_topi", [P, OT, 8], U32)
        topf = sb("r_topf", [P, OT, 8])
        gate = sb("r_gate", [P, OT, TOP])
        gsum = sb("r_gsum", [P, 2, OT])
        expert = sb("r_expert", [P, N_EXP])
        first = sb("r_first", [P, N_EXP])
        work = sb("r_work", [P, MORE])
        item_id = sb("r_item_id", [1, ITEMS + 1])
        before = sb("r_before", [P, P])
        ones = sb("r_ones", [P, P])
        pick = sb("r_pick", [P, TOP, OT, N_EXP])
        chosen = sb("r_chosen", [P, OT, N_EXP])
        prior = sb("r_prior", [P, OT + 1, N_EXP])
        slot = sb("r_slot", [P, OT, N_EXP])
        over = sb("r_over", [P, OT, N_EXP])
        more = sb("r_more", [P, 4, N_EXP])
        prod = sb("r_prod", [P, OT, N_EXP])
        slots = sb("r_slots", [P, OT, TOP])
        zero = sb("r_zero", [P, TABLE // P + 1], I32)
        cmp = sb("r_cmp", [1, MORE, N_EXP])
        rank = ctx.enter_context(nc.psum_tensor("r_rank", [P, 512], F32))
        count = ctx.enter_context(nc.psum_tensor("r_count", [P, 512], F32))

        s_lg = sem("r_logits_landed")
        s_pc = sem("r_pool_chain")
        s_dv = sem("r_dve_chain")
        s_sh = sem("r_gates_shifted")
        s_ge = sem("r_gates_exp")
        s_gate = sem("r_gates_ready")
        s_m = sem("r_chosen_ready")
        s_rank = sem("r_rank_ready")
        s_slot = sem("r_slots_ready")
        s_z = sem("r_table_zeroed")
        s_st = sem("r_stored")
        block = ctx.enter_context(nc.Block())

        @block.sync
        def _(sp):
            sp.dma_start(lg[:, :, :], scr["logits"].rearrange("(t p) e -> p t e", p=P)).then_inc(s_lg, 16)
            sp.wait_ge(s_gate, 1)
            sp.dma_start(scr["gate"].rearrange("(t p) c -> p t c", p=P), gate[:, :, :]).then_inc(s_st, 16)
            sp.wait_ge(s_slot, 1)
            sp.dma_start(scr["slot"].rearrange("(t p) c -> p t c", p=P), slots_i[:, :, :]).then_inc(s_st, 16)
            sp.wait_ge(s_st, 32)

        @block.gpsimd
        def _(pool):
            ch = Chain(pool, s_pc)
            n = TABLE // P
            ch.link(pool.memset(zero[:, :], 0))
            pool.dma_start(scr["token"][0:n * P, :].rearrange("(p n) o -> p (n o)", p=P), zero[:, 0:n]).then_inc(s_z, 16)
            ch.link(pool.iota(token[:, :], [[P, OT]], base=0, channel_multiplier=1))
            pool.iota(expert[:, :], [[1, N_EXP]], base=0, channel_multiplier=0, allow_small_or_imprecise_dtypes=True)
            pool.iota(first[:, :], [[ITEM, N_EXP]], base=0, channel_multiplier=0, allow_small_or_imprecise_dtypes=True)
            pool.iota(work[:, :], [[1, MORE]], base=0, channel_multiplier=0, allow_small_or_imprecise_dtypes=True)
            pool.iota(item_id[:, :], [[1, ITEMS + 1]], base=0, channel_multiplier=0, allow_small_or_imprecise_dtypes=True)
            pool.memset(ones[:, :], 1.0)
            ch.link(pool.memset(before[:, :], 1.0))
            ch.link(pool.affine_select(out=before[:, :], in_=before[:, :], compare_op=ALU.is_gt, fill=0.0, base=0,
                                       pattern=[[1, P]], channel_multiplier=-1))
            assert ch.n == POOL_SET
            pool.wait_ge(s_z, 16)

        @block.vector
        def _(dve):
            ch = Chain(dve, s_dv)
            all_t = [P, OT, N_EXP]
            dve.wait_ge(s_lg, 16)
            for t in range(OT):
                last = dve.max(top[:, t, :], lg[:, t, :])
            ch.link(last)
            for t in range(OT):
                last = dve.max_index(topi[:, t, :], top[:, t, :], lg[:, t, :])
            ch.link(last)
            ch.link(dve.tensor_copy(topf[:, :, :], topi[:, :, :]))
            dve.tensor_tensor(gate[:, :, :], top[:, :, 0:TOP], top[:, :, 0:1].to_broadcast([P, OT, TOP]),
                              ALU.subtract).then_inc(s_sh, 1)
            dve.wait_ge(s_ge, 1)
            ch.link(dve.tensor_reduce(gsum[:, 0, :], gate[:, :, :], AX.X, ALU.add))
            ch.link(dve.reciprocal(gsum[:, 1, :], gsum[:, 0, :]))
            dve.tensor_tensor(gate[:, :, :], gate[:, :, :], gsum[:, 1, :].unsqueeze(2).to_broadcast([P, OT, TOP]),
                              ALU.mult).then_inc(s_gate, 1)
            dve.wait_ge(s_pc, POOL_SET)
            for c in range(TOP):
                last = dve.tensor_tensor(pick[:, c, :, :], expert[:, :].unsqueeze(1).to_broadcast(all_t),
                                         topf[:, :, c:c + 1].to_broadcast(all_t), ALU.is_equal)
            ch.link(last)
            dve.tensor_tensor(chosen[:, :, :], pick[:, 0, :, :], pick[:, 1, :, :], ALU.add)
            ch.link(dve.tensor_tensor(prod[:, :, :], pick[:, 2, :, :], pick[:, 3, :, :], ALU.add))
            ch.link(dve.tensor_tensor(chosen[:, :, :], chosen[:, :, :], prod[:, :, :], ALU.add))
            ch.link(dve.memset(prior[:, 0, :], 0.0))
            for t in range(OT):
                ch.link(dve.tensor_tensor(prior[:, t + 1, :], prior[:, t, :], chosen[:, t, :], ALU.add))
            dve.sem_inc(s_m, 1)
            dve.wait_ge(s_rank, 1)
            cnt = more[:, 0, :]
            ch.link(dve.tensor_copy(cnt, count[:, 0:N_EXP]))
            ch.link(dve.memset(more[:, 1, :], 0.0))
            for c in range(1, -(-L // ITEM)):
                ch.link(dve.scalar_tensor_tensor(out=more[:, 1, :], in0=cnt, scalar=float(c * ITEM),
                                                 in1=more[:, 1, :], op0=ALU.is_gt, op1=ALU.add))
            ch.link(dve.tensor_tensor_scan(more[:, 2, :], ones[:, 0:N_EXP], more[:, 1, :], 0.0, ALU.mult, ALU.add))
            ch.link(dve.tensor_tensor(more[:, 3, :], more[:, 2, :], more[:, 1, :], ALU.subtract))
            ch.link(dve.tensor_scalar(more[:, 3, :], more[:, 3, :], float(ITEM), float(ITEM * (N_EXP - 1)),
                                      ALU.mult, ALU.add))
            ch.link(dve.tensor_tensor(more[:, 3, :], more[:, 3, :], first[:, :], ALU.subtract))
            r3 = rank[:, 0:OT * N_EXP].rearrange("p (t e) -> p t e", e=N_EXP)
            dve.tensor_tensor(slot[:, :, :], r3, first[:, :].unsqueeze(1).to_broadcast(all_t), ALU.add)
            ch.link(dve.tensor_scalar(over[:, :, :], r3, float(ITEM), None, ALU.is_ge))
            ch.link(dve.tensor_tensor(over[:, :, :], over[:, :, :], more[:, 3, :].unsqueeze(1).to_broadcast(all_t),
                                      ALU.mult))
            ch.link(dve.tensor_tensor(slot[:, :, :], slot[:, :, :], over[:, :, :], ALU.add))
            for c in range(TOP):
                ch.link(dve.tensor_tensor(prod[:, :, :], pick[:, c, :, :], slot[:, :, :], ALU.mult))
                ch.link(dve.tensor_reduce(slots[:, :, c], prod[:, :, :], AX.X, ALU.add))
            dve.tensor_copy(slots_i[:, :, :], slots[:, :, :]).then_inc(s_slot, 1)
            one = [1, MORE, N_EXP]
            ch.link(dve.tensor_tensor(cmp[:, :, :], more[0:1, 2, :].unsqueeze(1).to_broadcast(one),
                                      work[0:1, :].unsqueeze(2).to_broadcast(one), ALU.is_le))
            ch.link(dve.tensor_reduce(item_id[:, N_EXP:ITEMS], cmp[:, :, :], AX.X, ALU.add))
            ch.link(dve.tensor_scalar(item_id[:, N_EXP:], item_id[:, N_EXP:], float(N_EXP - 1), None, ALU.min))
            ch.link(dve.tensor_copy(items[:, :], item_id[:, :]))
            dve.tensor_scalar(n_items[:, 0:1], more[0:1, 2, N_EXP - 1:N_EXP], float(N_EXP), None, ALU.add)
            ch.link(dve.tensor_scalar(n_items[:, 1:2], more[0:1, 2, N_EXP - 1:N_EXP], float(N_EXP - 1), None, ALU.add))

        @block.scalar
        def _(act):
            act.wait_ge(s_sh, 1)
            act.activation(gate[:, :, :], gate[:, :, :], ACT.Exp).then_inc(s_ge, 1)

        @block.tensor
        def _(pe):
            pe.wait_ge(s_m, 1)
            w = OT * N_EXP
            pe.matmul(rank[:, 0:w], before[:, :], chosen[:, :, :].rearrange("p t e -> p (t e)"), start=True, stop=False)
            pe.matmul(rank[:, 0:w], ones[:, :], prior[:, 0:OT, :].rearrange("p t e -> p (t e)"), start=False, stop=True)
            pe.matmul(count[:, 0:N_EXP], ones[:, :], prior[:, OT, :], start=True, stop=True).then_inc(s_rank, 1)


POOL_SET = 4


D_FF = 1024
FT = D_FF // P
LIMIT, ALPHA = 7.0, 1.702
WS = 256.0
MATS = ("gate", "up", "down")
FPB = 2
BPM = FT // FPB
BPI = len(MATS) * BPM
RING = 6
AHEAD = 4
SOON = 2
PARTS = ((0, 0), (0, 1), (1, 0))


def stage_experts(nc, io, scr, ident, ident16, items, n_items, slots_i, token):
    used = []
    with ExitStack() as ctx:
        def sb(name, shape, dt=F32):
            return ctx.enter_context(nc.sbuf_tensor(name, shape, dt))

        def sem(name):
            used.append(ctx.enter_context(nc.semaphore(name)))
            return used[-1]

        BW = FPB * P
        raw = sb("e_raw", [P, RING, KT, BW])
        w = sb("e_w", [P, RING, 2, KT, BW], F16)
        bT = sb("e_bT", [P, 3, FT, N_EXP])
        bg = sb("e_bg", [P, FT])
        bud = sb("e_bud", [P, 2, FT])
        idx = sb("e_idx", [HALF, 2], U32)
        xg = sb("e_xg", [HALF, 2, 2 * D], F16)
        xT = sb("e_xT", [P, KT, 2, ITEM], F16)
        g = sb("e_g", [P, FT, ITEM])
        sg = sb("e_sg", [P, FT, ITEM])
        u = sb("e_u", [P, FT, ITEM])
        a = sb("e_a", [P, FT, 2, ITEM], F16)
        yT = sb("e_yT", [P, KT, ITEM])
        yr = sb("e_yr", [HALF, 2, D])
        ACC, TR = 4, 4
        acc = [ctx.enter_context(nc.psum_tensor(f"e_acc{b}", [P, 512], F32)) for b in range(ACC)]
        tr = [ctx.enter_context(nc.psum_tensor(f"e_tr{b}", [P, 512], F32)) for b in range(TR)]

        s_raw = [sem(f"e_raw_landed{b}") for b in range(RING)]
        s_hi = sem("e_w_hi_ready")
        s_lo = sem("e_w_ready")
        s_b = sem("e_biases_landed")
        s_bt = sem("e_biases_turned")
        s_bte = sem("e_biases_taken")
        s_bg = sem("e_gate_bias_ready")
        s_bud = sem("e_up_down_bias_ready")
        s_idx = sem("e_indices_landed")
        s_sc = sem("e_tokens_scattered")
        s_x = sem("e_rows_gathered")
        s_go = sem("e_gathers_started")
        s_xt = sem("e_rows_turned")
        s_xte = sem("e_rows_taken")
        s_f = sem("e_products")
        s_ge = sem("e_gate_taken")
        s_ue = sem("e_up_taken")
        s_de = sem("e_down_taken")
        s_sg = sem("e_sigmoid_ready")
        s_gs = sem("e_gated_ready")
        s_dv = sem("e_dve_chain")
        s_ag = sem("e_act_whole")
        s_ah = sem("e_act_hi_ready")
        s_a = sem("e_act_ready")
        s_yt = sem("e_y_turned")
        s_yte = sem("e_y_taken")
        s_y = sem("e_y_stored")

        block = ctx.enter_context(nc.Block())
        bias_rows = [t[0:N_EXP, :, :].rearrange("p f t -> p (f t)")[:, 0:D] for t in (g, sg, u)]

        def count_of(eng):
            return eng.value_load(n_items[0:1, 0:1], min_val=N_EXP, max_val=ITEMS)

        def last_of(eng):
            return eng.value_load(n_items[0:1, 1:2], min_val=N_EXP - 1, max_val=ITEMS - 1)

        def expert_of(eng, i):
            return eng.value_load(items[0:1, bass.ds(i, 1)], min_val=0, max_val=N_EXP - 1)


        def split_hi(act, i, j):
            q = j % RING
            act.wait_ge(s_raw[q], (i * (BPI // RING) + j // RING + 1) * 16)
            if not (isinstance(i, int) and i == 0 and j < RING):
                act.wait_ge(s_f, (i * BPI + (j - RING + 1)) * FPB)
            act.activation(w[:, q, 0, :, :], raw[:, q, :, :], ACT.Copy, scale=WS).then_inc(s_hi, 1)

        def split_lo(dve, i, j):
            q = j % RING
            dve.wait_ge(s_hi, i * BPI + (j + 1))
            dve.scalar_tensor_tensor(out=w[:, q, 1, :, :].rearrange("p k f -> p (k f)"),
                                     in0=raw[:, q, :, :].rearrange("p k f -> p (k f)"), scalar=WS,
                                     in1=w[:, q, 0, :, :].rearrange("p k f -> p (k f)"),
                                     op0=ALU.mult, op1=ALU.subtract).then_inc(s_lo, 1)

        @block.sync
        def _(sp):
            for j, m in enumerate(MATS):
                sp.dma_start(bias_rows[j], io[f"b_{m}"][0]).then_inc(s_b, 16)
            n = count_of(sp)

            def load(e, j):
                c = (j % BPM) * BW
                src = io[f"w_{MATS[j // BPM]}"][0][bass.ds(e, 1), :, c:c + BW].rearrange("o (k p) f -> p (o k) f", p=P)
                sp.dma_start(raw[:, j % RING, :, :], src).then_inc(s_raw[j % RING], 16)

            e = expert_of(sp, 0)
            for j in range(BPI):
                if j >= RING:
                    sp.wait_ge(s_lo, j - RING + 1)
                load(e, j)
            with sp.Fori(1, n) as i:
                e = expert_of(sp, i)
                for j in range(BPI):
                    sp.wait_ge(s_lo, i * BPI + (j - RING + 1))
                    load(e, j)

        @block.gpsimd
        def _(pool):
            n = count_of(pool)

            def gather(i):
                pool.dma_start(idx[:, :].bitcast(I32),
                               scr["token"][bass.ds(i * ITEM, ITEM), :].rearrange("(a p) o -> p (a o)", a=2),
                               allow_slow_non_contiguous=True).then_inc(s_idx, 16)
                pool.wait_ge(s_idx, i * 16 + 16)
                pool.sem_inc(s_go, 1)
                for a_ in range(2):
                    pool.indirect_dma_start(out=xg[:, a_, :], out_offset=None, in_=scr["xn"],
                                            in_offset=bass.IndirectOffsetOnAxis(ap=idx[:, a_:a_ + 1], axis=0)
                                            ).then_inc(s_x, 16)

            for t in range(OT):
                for c in range(TOP):
                    pool.indirect_dma_start(out=scr["token"],
                                            out_offset=bass.IndirectOffsetOnAxis(ap=slots_i[:, t, c:c + 1], axis=0),
                                            in_=token[:, t:t + 1], in_offset=None).then_inc(s_sc, 16)
            pool.wait_ge(s_sc, 16 * OT * TOP)
            gather(0)
            with pool.Fori(0, n) as i:
                pool.wait_ge(s_xt, i * 4 + 4)
                gather(i + 1)
                pool.wait_ge(s_yte, i * 4 + 4)
                pool.dma_start(scr["y"][bass.ds(i * ITEM, ITEM), :].rearrange("(a p) d -> p a d", a=2),
                               yr[:, :, :]).then_inc(s_y, 16)
            pool.wait_ge(s_y, n * 16)
            pool.wait_ge(s_x, n * 32 + 32)

        @block.tensor
        def _(pe):
            last_i = last_of(pe)
            pe.wait_ge(s_b, 48)
            for j in range(3):
                for f in range(FT):
                    last = pe.transpose(tr[j][:, f * N_EXP:(f + 1) * N_EXP], bias_rows[j][:, f * P:(f + 1) * P],
                                        ident[0:N_EXP, 0:N_EXP])
                last.then_inc(s_bt, 1)
            pe.wait_ge(s_bte, 3)

            def turn_rows(i):
                pe.wait_ge(s_x, i * 32 + 32)
                for q in range(4):
                    t16 = tr[q][:, :].bitcast(F16)
                    for k in range(2):
                        for part in range(2):
                            for a_ in range(2):
                                c = (k * 2 + part) * ITEM + a_ * HALF
                                r = part * D + (2 * q + k) * P
                                last = pe.transpose(t16[:, c:c + HALF], xg[:, a_, r:r + P], ident16[0:HALF, 0:HALF])
                    last.then_inc(s_xt, 1)

            def product(j, f, x, k0=0, k1=KT):
                q = j % RING
                c = (f % FPB) * P
                for k in range(k0, k1):
                    for p, (wp, xp) in enumerate(PARTS):
                        last = pe.matmul(acc[f % ACC][:, 0:ITEM], w[:, q, wp, k, c:c + P], x[:, k, xp, :],
                                         start=(k == 0 and p == 0), stop=(k == KT - 1 and p == len(PARTS) - 1))
                if k1 == KT:
                    last.then_inc(s_f, 1)

            def gate(i, s):
                pe.wait_ge(s_lo, i * BPI + (s + 1))
                for f in range(FPB * s, FPB * s + FPB):
                    if f >= ACC:
                        pe.wait_ge(s_ge, i * FT + (f + 1 - ACC))
                    elif not isinstance(i, int):
                        pe.wait_ge(s_de, i * FT + (f + 1 - ACC))
                    product(s, f, xT)

            def turn_y(i):
                pe.wait_ge(s_de, i * FT + FT)
                for q in range(4):
                    a_, half = q // 2, q % 2
                    for k in range(4):
                        last = pe.transpose(tr[q][0:HALF, k * P:(k + 1) * P],
                                            yT[:, 4 * half + k, a_ * HALF:(a_ + 1) * HALF], ident[:, :])
                    last.then_inc(s_yt, 1)

            def up_and_down(i, last_item):
                for s in range(BPM):
                    j = BPM + s
                    pe.wait_ge(s_lo, i * BPI + (j + 1))
                    for f in range(FPB * s, FPB * s + FPB):
                        pe.wait_ge(s_ge, i * FT + (f + 1 + FT - ACC)) if f < ACC else pe.wait_ge(s_ue, i * FT + (f + 1 - ACC))
                        product(j, f, xT)
                pe.wait_ge(s_yte, i * 4)
                if not last_item:
                    turn_rows(i + 1)
                for s in range(BPM):
                    j = 2 * BPM + s
                    pe.wait_ge(s_lo, i * BPI + (j + 1))
                    fs = range(FPB * s, FPB * s + FPB)
                    for f in fs:
                        pe.wait_ge(s_ue, i * FT + (f + 1 + FT - ACC)) if f < ACC else pe.wait_ge(s_de, i * FT + (f + 1 - ACC))
                        if s:
                            product(j, f, a)
                        else:
                            pe.wait_ge(s_a, i * BPM + (BPM - 1))
                            product(j, f, a, 0, KT - FPB)
                    if s == 0:
                        pe.wait_ge(s_a, i * BPM + BPM)
                        for f in fs:
                            product(j, f, a, KT - FPB, KT)

            turn_rows(0)
            pe.wait_ge(s_xte, 4)
            for s in range(BPM):
                gate(0, s)
            with pe.Fori(0, last_i) as i:
                up_and_down(i, False)
                pe.wait_ge(s_xte, i * 4 + 8)
                gate(i + 1, 0)
                turn_y(i)
                for s in range(1, BPM):
                    gate(i + 1, s)
            up_and_down(last_i, True)
            turn_y(last_i)

        @block.vector
        def _(dve):
            last_i = last_of(dve)
            for j in range(3):
                dve.wait_ge(s_bt, j + 1)
                dve.tensor_scalar(bT[:, j, :, :], tr[j][:, 0:FT * N_EXP].rearrange("p (f e) -> p f e", e=N_EXP),
                                  WS if j == 0 else 1.0, None, ALU.mult).then_inc(s_bte, 1)
            dve.wait_ge(s_bte, 3)

            def gate(i, s):
                if s == 0:
                    e = expert_of(dve, i)
                    if not isinstance(i, int):
                        dve.wait_ge(s_ge, i * FT)
                        dve.wait_ge(s_a, i * BPM)
                    dve.tensor_copy(bg[:, :], bT[:, 0, :, bass.ds(e, 1)].rearrange("p f o -> p (f o)")).then_inc(s_bg, 1)
                    dve.wait_ge(s_bg, i + 1)
                for f in range(FPB * s, FPB * s + FPB):
                    dve.wait_ge(s_f, i * (3 * FT) + (f + 1))
                    dve.tensor_scalar(g[:, f, :], acc[f % ACC][:, 0:ITEM], bg[:, f:f + 1], LIMIT * WS,
                                      ALU.add, ALU.min).then_inc(s_ge, 1)
                split_lo(dve, i, s + AHEAD)
                if s:
                    gated(i, s - 1)
                if s == BPM - 1:
                    e = expert_of(dve, i)
                    if not isinstance(i, int):
                        dve.wait_ge(s_de, i * FT)
                    dve.tensor_copy(bud[:, :, :], bT[:, 1:3, :, bass.ds(e, 1)].rearrange("p j f o -> p j (f o)")
                                    ).then_inc(s_bud, 1)

            def gated(i, h):
                pair = slice(2 * h, 2 * h + 2)
                dve.wait_ge(s_sg, i * BPM + (h + 1))
                dve.tensor_tensor(g[:, pair, :], g[:, pair, :], sg[:, pair, :], ALU.mult).then_inc(s_gs, 1)

            def up_and_down(i, last_item):
                gated(i, BPM - 1)
                for h in range(BPM):
                    ch = Chain(dve, s_dv, base=i * BPM + h)
                    pair = slice(2 * h, 2 * h + 2)
                    dve.wait_ge(s_ue, i * FT + (2 * h + 2))
                    ch.link(dve.tensor_scalar(u[:, pair, :], u[:, pair, :], LIMIT, -LIMIT, ALU.min, ALU.max))
                    dve.wait_ge(s_gs, i * BPM + (h + 1))
                    dve.scalar_tensor_tensor(out=g[:, pair, :], in0=u[:, pair, :], scalar=1.0, in1=g[:, pair, :],
                                             op0=ALU.add, op1=ALU.mult).then_inc(s_ag, 1)
                    if h < SOON:
                        split_lo(dve, i, BPM + h + AHEAD)
                    dve.wait_ge(s_ah, i * BPM + (h + 1))
                    dve.scalar_tensor_tensor(out=a[:, pair, 1, :], in0=g[:, pair, :], scalar=1.0 / WS,
                                             in1=a[:, pair, 0, :], op0=ALU.mult, op1=ALU.subtract).then_inc(s_a, 1)
                for h in range(SOON, BPM):
                    split_lo(dve, i, BPM + h + AHEAD)
                if not last_item:
                    for s in range(BPM):
                        split_lo(dve, i, 2 * BPM + s + AHEAD)

            def take_y(i):
                dve.wait_ge(s_y, i * 16)
                for q in range(4):
                    a_, half = q // 2, q % 2
                    dve.wait_ge(s_yt, i * 4 + (q + 1))
                    dve.tensor_copy(yr[:, a_, half * 512:(half + 1) * 512], tr[q][0:HALF, :]).then_inc(s_yte, 1)

            for j in range(AHEAD):
                split_lo(dve, 0, j)
            for s in range(BPM):
                gate(0, s)
            with dve.Fori(0, last_i) as i:
                up_and_down(i, False)
                gate(i + 1, 0)
                gate(i + 1, 1)
                take_y(i)
                gate(i + 1, 2)
                gate(i + 1, 3)
            up_and_down(last_i, True)
            take_y(last_i)

        @block.scalar
        def _(act):
            last_i = last_of(act)

            def take_rows(i, q):
                act.wait_ge(s_xt, i * 4 + (q + 1))
                act.copy(xT[:, 2 * q:2 * q + 2, :, :], tr[q][:, :].bitcast(F16)[:, 0:4 * ITEM]
                         .rearrange("p (k c t) -> p k c t", k=2, c=2)).then_inc(s_xte, 1)

            def gate(i, s):
                split_hi(act, i, s + AHEAD)
                pair = slice(2 * s, 2 * s + 2)
                act.wait_ge(s_ge, i * FT + (2 * s + 2))
                act.activation(sg[:, pair, :], g[:, pair, :], ACT.Sigmoid, scale=ALPHA / WS).then_inc(s_sg, 1)

            def whole(i, h):
                act.wait_ge(s_ag, i * BPM + (h + 1))
                act.activation(a[:, 2 * h:2 * h + 2, 0, :], g[:, 2 * h:2 * h + 2, :], ACT.Copy,
                               scale=1.0 / WS).then_inc(s_ah, 1)

            def up_and_down(i, last_item):
                act.wait_ge(s_bud, i + 1)
                for s in range(BPM):
                    for f in range(FPB * s, FPB * s + FPB):
                        act.wait_ge(s_f, i * (3 * FT) + (FT + f + 1))
                        act.activation(u[:, f, :], acc[f % ACC][:, 0:ITEM], ACT.Identity, bias=bud[:, 0, f:f + 1],
                                       scale=1.0 / WS).then_inc(s_ue, 1)
                    if s < SOON:
                        split_hi(act, i, BPM + s + AHEAD)
                    whole(i, s)
                for s in range(SOON, BPM):
                    split_hi(act, i, BPM + s + AHEAD)
                for s in range(BPM):
                    if not last_item:
                        split_hi(act, i, 2 * BPM + s + AHEAD)
                    for f in range(FPB * s, FPB * s + FPB):
                        act.wait_ge(s_f, i * (3 * FT) + (2 * FT + f + 1))
                        act.wait_ge(s_yt, i * 4)
                        act.activation(yT[:, f, :], acc[f % ACC][:, 0:ITEM], ACT.Identity,
                                       bias=bud[:, 1, f:f + 1], scale=1.0 / WS).then_inc(s_de, 1)
                    if not last_item and s < 2:
                        take_rows(i + 1, 2 * s)
                        take_rows(i + 1, 2 * s + 1)

            for j in range(AHEAD):
                split_hi(act, 0, j)
            for q in range(4):
                take_rows(0, q)
            for s in range(BPM):
                gate(0, s)
            with act.Fori(0, last_i) as i:
                up_and_down(i, False)
                for s in range(BPM):
                    gate(i + 1, s)
            up_and_down(last_i, True)


def stage_combine(nc, io, out, scr):
    used = []
    with ExitStack() as ctx:
        def sb(name, shape, dt=F32):
            return ctx.enter_context(nc.sbuf_tensor(name, shape, dt))

        def sem(name):
            used.append(ctx.enter_context(nc.semaphore(name)))
            return used[-1]

        g_bc = sb("c_g_bc", [P, D])
        slot = sb("c_slot", [P, OT, TOP], U32)
        gate = sb("c_gate", [P, OT, TOP])
        yg = sb("c_yg", [P, 2, TOP, D])
        hr = sb("c_hr", [P, 2, D])
        sq = sb("c_sq", [P, D])
        st = sb("c_st", [P, 2, 4])
        res = sb("c_res", [P, 2, D])
        s_in = sem("c_tables_landed")
        s_h = [sem(f"c_h_landed{b}") for b in range(2)]
        s_y = [sem(f"c_rows_gathered{b}") for b in range(2)]
        s_acc = sem("c_sum_chain")
        s_sum = sem("c_sum_ready")
        s_sq = sem("c_squares_ready")
        s_var = sem("c_variance_ready")
        s_ln = sem("c_log_ready")
        s_rs = sem("c_rstd_ready")
        s_res = sem("c_result_ready")
        s_out = [sem(f"c_result_stored{b}") for b in range(2)]
        block = ctx.enter_context(nc.Block())

        @block.sync
        def _(sp):
            sp.dma_start(g_bc[:, :], io["final_norm_g"].partition_broadcast(P)).then_inc(s_in, 16)
            sp.dma_start(slot[:, :, :], scr["slot"].rearrange("(t p) c -> p t c", p=P)).then_inc(s_in, 16)
            sp.dma_start(gate[:, :, :], scr["gate"].rearrange("(t p) c -> p t c", p=P)).then_inc(s_in, 16)
            sp.dma_start(hr[:, 0, :], scr["h2"][0:P, :]).then_inc(s_h[0], 16)
            for t in range(OT):
                if t + 1 < OT:
                    if t >= 1:
                        sp.wait_ge(s_res, t)
                    sp.dma_start(hr[:, (t + 1) % 2, :],
                                 scr["h2"][(t + 1) * P:(t + 2) * P, :]).then_inc(s_h[(t + 1) % 2], 16)
                sp.wait_ge(s_res, t + 1)
                sp.dma_start(out[0, t * P:(t + 1) * P, :], res[:, t % 2, :]).then_inc(s_out[t % 2], 16)
            for b in range(2):
                sp.wait_ge(s_out[b], 16 * OT // 2)

        @block.gpsimd
        def _(pool):
            pool.wait_ge(s_in, 48)
            for t in range(OT):
                if t >= 2:
                    pool.wait_ge(s_sum, t - 1)
                for c in range(TOP):
                    pool.indirect_dma_start(out=yg[:, t % 2, c, :], out_offset=None, in_=scr["y"],
                                            in_offset=bass.IndirectOffsetOnAxis(ap=slot[:, t, c:c + 1], axis=0)
                                            ).then_inc(s_y[t % 2], 16)

        @block.vector
        def _(dve):
            ch = Chain(dve, s_acc)
            dve.wait_ge(s_in, 48)
            for t in range(OT):
                b = t % 2
                dve.wait_ge(s_h[b], 16 * (t // 2 + 1))
                dve.wait_ge(s_y[b], 16 * TOP * (t // 2 + 1))
                for c in range(TOP):
                    ins = dve.scalar_tensor_tensor(out=hr[:, b, :], in0=yg[:, b, c, :], scalar=gate[:, t, c:c + 1],
                                                   in1=hr[:, b, :], op0=ALU.mult, op1=ALU.add)
                    if c < TOP - 1:
                        ch.link(ins)
                    else:
                        ins.then_inc(s_sum, 1)
                dve.wait_ge(s_sq, t + 1)
                dve.tensor_scalar(st[:, b, 1:2], st[:, b, 0:1], 1.0 / D, EPS, ALU.mult, ALU.add).then_inc(s_var, 1)
                dve.wait_ge(s_rs, t + 1)
                if t >= 2:
                    dve.wait_ge(s_out[b], 16 * (t // 2))
                dve.scalar_tensor_tensor(out=res[:, b, :], in0=hr[:, b, :], scalar=st[:, b, 3:4], in1=g_bc[:, :],
                                         op0=ALU.mult, op1=ALU.mult).then_inc(s_res, 1)

        @block.scalar
        def _(act):
            act.preload_act_table_set("natural_log_exp_and_others")
            for t in range(OT):
                b = t % 2
                act.wait_ge(s_sum, t + 1)
                if t:
                    act.wait_ge(s_sq, t)
                act.activation(sq[:, :], hr[:, b, :], ACT.Square, accum_out=st[:, b, 0:1]).then_inc(s_sq, 1)
                act.wait_ge(s_var, t + 1)
                act.activation(st[:, b, 2:3], st[:, b, 1:2], ACT.Ln).then_inc(s_ln, 1)
                act.wait_ge(s_ln, t + 1)
                act.activation(st[:, b, 3:4], st[:, b, 2:3], ACT.Exp, scale=-0.5).then_inc(s_rs, 1)


def hybrid_layer(nc, io, out, scr):
    with ExitStack() as ctx:
        ident = ctx.enter_context(nc.sbuf_tensor("ident", [P, P], F32))
        ident16 = ctx.enter_context(nc.sbuf_tensor("ident16", [P, P], F16))
        items = ctx.enter_context(nc.sbuf_tensor("items", [1, ITEMS + 1], I32))
        n_items = ctx.enter_context(nc.sbuf_tensor("n_items", [1, 2], I32))
        slots_i = ctx.enter_context(nc.sbuf_tensor("slots_i", [P, OT, TOP], U32))
        token = ctx.enter_context(nc.sbuf_tensor("token_ids", [P, OT], I32))
        s_c = ctx.enter_context(nc.semaphore("constants"))
        with nc.Block() as block:
            @block.gpsimd
            def _(pool):
                pool.memset(ident[:, :], 0.0).then_inc(s_c, 1)
                pool.wait_ge(s_c, 1)
                pool.affine_select(out=ident[:, :], in_=ident[:, :], compare_op=ALU.not_equal, fill=1.0,
                                   base=0, pattern=[[-1, P]], channel_multiplier=1).then_inc(s_c, 1)
                pool.wait_ge(s_c, 2)
                pool.tensor_copy(ident16[:, :], ident[:, :]).then_inc(s_c, 1)
        with nc.sbuf_tensor("xnT", [P, KT, LP], F32) as xnT:
            clear(nc, stage_project(nc, io, scr, ident, xnT))
            clear(nc, stage_attention(nc, io, scr, ident, xnT))
        with (nc.sbuf_tensor("w_up_attn", [P, HGW // P, D], F32) as wa, nc.sbuf_tensor("w_up_hgrn", [P, HGW // P, D], F32) as wh,
              nc.sbuf_tensor("w_out", [P, KT, D], F32) as wo, nc.semaphore("merge_weights_landed") as s_w):
            stage_hgrn(nc, io, scr, ident, wa, wh, wo, s_w)
            stage_merge(nc, io, scr, ident, wa, wh, wo, s_w)
        stage_route(nc, io, scr, items, n_items, slots_i, token)
        stage_experts(nc, io, scr, ident, ident16, items, n_items, slots_i, token)
        stage_combine(nc, io, out, scr)


SCRATCH = {
    "h": ((LP, D), F32), "proj": ((LP, IN_COLS), F32), "att": ((LP, ATT_HEADS * HD), F32), "hgr": ((LP, HGW), F32),
    "h2": ((SEQ, D), F32), "xn": ((SEQ, 2 * D), F16), "logits": ((SEQ, N_EXP), F32), "gate": ((SEQ, TOP), F32),
    "slot": ((SEQ, TOP), U32), "token": ((TABLE, 1), I32), "y": ((SLOTS, D), F32),
}


def build(nc, shapes):
    io = {n: nc.dram_tensor(f"in_{n}", s, F32, kind="ExternalInput").ap() for n, s in shapes.items()}
    out = nc.dram_tensor("out_0", (1, SEQ, D), F32, kind="ExternalOutput").ap()
    scr = {n: nc.dram_tensor(f"scratch_{n}", s, dt, kind="Internal").ap() for n, (s, dt) in SCRATCH.items()}
    hybrid_layer(nc, io, out, scr)


_INS = ["x", "meta_tokens", "attn_norm_g", "w_in", "hgrn_norm_g", "w_up_attn", "w_up_hgrn", "w_out",
        "hgrn_lb_logits", "ffn_norm_g", "router_w", "router_b", "w_gate", "b_gate", "w_up", "b_up",
        "w_down", "b_down", "final_norm_g"]


def extra_inputs(inputs):
    return {**inputs, "rope": rope_tables()}


def kernel(**inputs):
    import concourse.bacc as _bacc
    from concourse.bass_utils import run_bass_kernel_spmd as _run

    arrays = {n: np.ascontiguousarray(inputs[n]) for n in _INS}
    arrays["rope"] = rope_tables()
    nc = _bacc.Bacc("TRN2", target_bir_lowering=False, num_devices=1)
    build(nc, {n: a.shape for n, a in arrays.items()})
    r = _run(nc, [{f"in_{n}": a for n, a in arrays.items()}], core_ids=[0])
    return r.results[0]["out_0"]
```
